# Optimizing a Trainium2 kernel written in Bass

```python
import math
import jax, jax.numpy as jnp
from jax import lax
import numpy as np
import jax
import jax.numpy as jnp

D_MODEL = 1024
BATCH = 1
SEQ = 512
DEPTH = 2

HEAD_DIM = 64
SB_HEADS = 8
SWA_HEADS = 8
SWA_KV_HEADS = 2
WINDOW = 128
BLOCK = 128
D_FF = 4 * D_MODEL
ROPE_THETA = 10000.0
NORM_EPS = 1e-6
N_BRANCHES = 2

SB_WIDTH = SB_HEADS * HEAD_DIM
SWA_Q_WIDTH = SWA_HEADS * HEAD_DIM
SWA_KV_WIDTH = SWA_KV_HEADS * HEAD_DIM
IN_WIDTH = 3 * SB_WIDTH + SWA_Q_WIDTH + 2 * SWA_KV_WIDTH + N_BRANCHES * D_MODEL


def rms_norm(x, g):
    xf = x.astype(jnp.float32)
    y = xf * lax.rsqrt(jnp.mean(xf * xf, axis=-1, keepdims=True) + NORM_EPS)
    return (y * g.astype(jnp.float32)).astype(x.dtype)

def rope_tables(seq):
    inv_freq = 1.0 / (ROPE_THETA ** (jnp.arange(0, HEAD_DIM, 2, dtype=jnp.float32) / HEAD_DIM))
    ang = jnp.arange(seq, dtype=jnp.float32)[:, None] * inv_freq[None, :]
    return jnp.cos(ang), jnp.sin(ang)

def apply_rope(x, cos, sin):
    c = cos[None, :, None, :].astype(x.dtype)
    s = sin[None, :, None, :].astype(x.dtype)
    x1, x2 = jnp.split(x, 2, axis=-1)
    return jnp.concatenate([x1 * c - x2 * s, x2 * c + x1 * s], axis=-1)

def stick_breaking_attention(q, k, v):
    B, S, H, d = q.shape
    scale = d ** -0.5
    outs = []
    for blk in range(S // BLOCK):
        t0, t1 = blk * BLOCK, (blk + 1) * BLOCK
        qb = q[:, t0:t1]
        kb = k[:, :t1]
        vb = v[:, :t1]
        z = jnp.einsum('bqhd,bshd->bhqs', qb, kb).astype(jnp.float32) * scale
        t_idx = jnp.arange(t0, t1)[:, None]
        s_idx = jnp.arange(t1)[None, :]
        strict = s_idx < t_idx
        log_keep = jnp.where(strict, -jax.nn.softplus(z), 0.0)
        tail = lax.cumsum(log_keep, axis=3, reverse=True) - log_keep
        w = jnp.where(strict, jnp.exp(jax.nn.log_sigmoid(z) + tail), 0.0)
        outs.append(jnp.einsum('bhqs,bshd->bqhd', w.astype(v.dtype), vb))
    return jnp.concatenate(outs, axis=1)

def sliding_window_sink_attention(q, k, v, sinks):
    B, S, Hq, d = q.shape
    G = Hq // SWA_KV_HEADS
    nb = S // BLOCK
    scale = d ** -0.5
    qb = q.reshape(B, nb, BLOCK, SWA_KV_HEADS, G, d)
    pad = ((0, 0), (BLOCK, 0), (0, 0), (0, 0))
    kb = jnp.pad(k, pad).reshape(B, nb + 1, BLOCK, SWA_KV_HEADS, d)
    vb = jnp.pad(v, pad).reshape(B, nb + 1, BLOCK, SWA_KV_HEADS, d)
    k_band = jnp.concatenate([kb[:, :-1], kb[:, 1:]], axis=2)
    v_band = jnp.concatenate([vb[:, :-1], vb[:, 1:]], axis=2)
    scores = jnp.einsum('bnqkgd,bnskd->bnkgqs', qb, k_band).astype(jnp.float32) * scale
    i = jnp.arange(BLOCK)[:, None]
    j = jnp.arange(2 * BLOCK)[None, :]
    rel = j - BLOCK - i
    in_window = (rel <= 0) & (rel > -WINDOW)
    key_pos = jnp.arange(nb)[:, None, None] * BLOCK + j[None] - BLOCK
    valid = in_window[None] & (key_pos >= 0)
    scores = jnp.where(valid[None, :, None, None], scores, -jnp.inf)
    sink = jnp.broadcast_to(sinks.astype(jnp.float32).reshape(1, 1, SWA_KV_HEADS, G, 1, 1),
                            scores.shape[:-1] + (1,))
    probs = jax.nn.softmax(jnp.concatenate([scores, sink], axis=-1), axis=-1)[..., :-1]
    out = jnp.einsum('bnkgqs,bnskd->bnqkgd', probs.astype(v.dtype), v_band)
    return out.reshape(B, S, Hq * d)

def first_inputs(seed: int = 0) -> dict:
    key = jax.random.key(seed)
    ks = jax.random.split(key, 12)
    nrm = lambda k, shape, scale: jax.random.normal(k, shape, jnp.float32) * scale
    return {
        "x": nrm(ks[0], (BATCH, SEQ, D_MODEL), 1.0),
        "mix_norm_g": 1.0 + nrm(ks[1], (DEPTH, D_MODEL), 0.02),
        "w_in": nrm(ks[2], (DEPTH, D_MODEL, IN_WIDTH), D_MODEL ** -0.5),
        "q_norm_g": 1.0 + nrm(ks[3], (DEPTH, HEAD_DIM), 0.02),
        "k_norm_g": 1.0 + nrm(ks[4], (DEPTH, HEAD_DIM), 0.02),
        "sinks": nrm(ks[5], (DEPTH, SWA_HEADS), 0.5),
        "w_branch_sb": nrm(ks[6], (DEPTH, SB_WIDTH, D_MODEL), SB_WIDTH ** -0.5),
        "w_branch_swa": nrm(ks[7], (DEPTH, SWA_Q_WIDTH, D_MODEL), SWA_Q_WIDTH ** -0.5),
        "w_out": nrm(ks[8], (DEPTH, D_MODEL, D_MODEL), D_MODEL ** -0.5),
        "mlp_norm_g": 1.0 + nrm(ks[9], (DEPTH, D_MODEL), 0.02),
        "w_up": nrm(ks[10], (DEPTH, D_MODEL, D_FF), D_MODEL ** -0.5),
        "w_down": nrm(ks[11], (DEPTH, D_FF, D_MODEL), D_FF ** -0.5),
    }

def first_block(x, mix_norm_g, w_in, q_norm_g, k_norm_g, sinks, w_branch_sb, w_branch_swa,
              w_out, mlp_norm_g, w_up, w_down):
    B, S, D = x.shape
    cos, sin = rope_tables(S)
    split_at = np.cumsum([SB_WIDTH, SB_WIDTH, SB_WIDTH, SWA_Q_WIDTH, SWA_KV_WIDTH, SWA_KV_WIDTH]).tolist()
    for l in range(DEPTH):
        h = rms_norm(x, mix_norm_g[l])
        proj = h @ w_in[l]
        sb_q, sb_k, sb_v, sw_q, sw_k, sw_v, gate_logits = jnp.split(proj, split_at, axis=-1)

        to_heads = lambda t, n: t.reshape(B, S, n, HEAD_DIM)
        o_sb = stick_breaking_attention(to_heads(sb_q, SB_HEADS), to_heads(sb_k, SB_HEADS),
                                        to_heads(sb_v, SB_HEADS)).reshape(B, S, SB_WIDTH)
        y_sb = o_sb @ w_branch_sb[l]

        q = apply_rope(rms_norm(to_heads(sw_q, SWA_HEADS), q_norm_g[l]), cos, sin)
        k = apply_rope(rms_norm(to_heads(sw_k, SWA_KV_HEADS), k_norm_g[l]), cos, sin)
        v = to_heads(sw_v, SWA_KV_HEADS)
        y_swa = sliding_window_sink_attention(q, k, v, sinks[l]) @ w_branch_swa[l]

        gates = jax.nn.sigmoid(gate_logits.astype(jnp.float32)).astype(x.dtype).reshape(B, S, N_BRANCHES, D)
        merged = gates[:, :, 0] * y_sb + gates[:, :, 1] * y_swa
        x = x + merged @ w_out[l]

        h2 = rms_norm(x, mlp_norm_g[l])
        x = x + jnp.square(jax.nn.relu(h2 @ w_up[l])) @ w_down[l]
    return x


DEPTH_2 = 1

SSM_EXPAND = 2
SSM_D_INNER = SSM_EXPAND * D_MODEL
SSM_HEAD_DIM = 64
SSM_HEADS = SSM_D_INNER // SSM_HEAD_DIM
SSM_GROUPS = 4
SSM_HPG = SSM_HEADS // SSM_GROUPS
SSM_STATE = 128
SSM_CONV = 4
SSM_CHUNK = 128
SSM_CONV_DIM = SSM_D_INNER + 2 * SSM_GROUPS * SSM_STATE

NSA_HEADS = 16
NSA_HEAD_DIM = 64
NSA_WIDTH = NSA_HEADS * NSA_HEAD_DIM
NSA_KV_GROUPS = 2
NSA_HPG = NSA_HEADS // NSA_KV_GROUPS
NSA_KV_WIDTH = NSA_KV_GROUPS * NSA_HEAD_DIM
CMP_BLOCK = 32
CMP_STRIDE = 16
CMP_HIDDEN = 256
SEL_BLOCK = 64
SEL_TOPK = 4
WINDOW_2 = 512
NSA_QBLOCK = 64

MOE_GROUPS = 4
EXPERTS_PER_GROUP = 8
N_EXPERTS = MOE_GROUPS * EXPERTS_PER_GROUP
EXPERT_TOPK = 2
EXPERT_HIDDEN = 256


IN_SIZES = (SSM_D_INNER, SSM_CONV_DIM, SSM_HEADS, NSA_WIDTH, NSA_KV_WIDTH, NSA_KV_WIDTH, NSA_KV_WIDTH, NSA_KV_WIDTH, NSA_KV_WIDTH, NSA_KV_WIDTH, 3 * NSA_HEADS, D_MODEL, D_MODEL)
IN_WIDTH_2 = SSM_D_INNER + SSM_CONV_DIM + SSM_HEADS + NSA_WIDTH + 6 * NSA_KV_WIDTH + 3 * NSA_HEADS + 2 * D_MODEL


def _rmsnorm(x, g):
    xf = x.astype(jnp.float32)
    y = xf * lax.rsqrt(jnp.mean(xf * xf, axis=-1, keepdims=True) + NORM_EPS)
    return (y * g.astype(jnp.float32)).astype(x.dtype)

def _masked_softmax(s, mask):
    s = jnp.where(mask, s.astype(jnp.float32), -1e30)
    m = jnp.max(s, axis=-1, keepdims=True)
    p = jnp.where(mask, jnp.exp(s - m), 0.0)
    return p / jnp.maximum(jnp.sum(p, axis=-1, keepdims=True), 1e-30)

def _rope(t, cos, sin):
    shape = cos.shape[:2] + (1,) * (t.ndim - 3) + cos.shape[2:]
    cos = cos.reshape(shape)
    sin = sin.reshape(shape)
    t1, t2 = jnp.split(t.astype(jnp.float32), 2, axis=-1)
    return jnp.concatenate([t1 * cos - t2 * sin, t2 * cos + t1 * sin], axis=-1).astype(t.dtype)

def _ssd_chunked_scan(xh, dt, a, bm, cm):
    b, s = xh.shape[:2]
    nc = s // SSM_CHUNK

    def chunks(t):
        t = t.astype(jnp.float32)
        return jnp.moveaxis(t.reshape((b, nc, SSM_CHUNK) + t.shape[2:]), 1, 0)

    tril = jnp.tril(jnp.ones((SSM_CHUNK, SSM_CHUNK), dtype=bool))[None, :, :, None, None]
    a = a.astype(jnp.float32)

    def step(state, inp):
        xc, dtc, bc, cc = inp
        acum = jnp.cumsum(dtc * a, axis=1)
        seg = acum[:, :, None] - acum[:, None, :]
        decay = jnp.exp(jnp.where(tril, seg, -jnp.inf))
        cb = jnp.einsum('btgn,bsgn->bgts', cc, bc)
        y_diag = jnp.einsum('bgts,btsgr,bsgr,bsgrp->btgrp', cb, decay, dtc, xc)
        y_off = jnp.einsum('btgn,bgrpn->btgrp', cc, state) * jnp.exp(acum)[..., None]
        w_end = jnp.exp(acum[:, -1:] - acum) * dtc
        new_state = state * jnp.exp(acum[:, -1])[..., None, None] + jnp.einsum('bsgn,bsgr,bsgrp->bgrpn', bc, w_end, xc)
        return new_state, y_diag + y_off

    state0 = jnp.zeros((b, SSM_GROUPS, SSM_HPG, SSM_HEAD_DIM, SSM_STATE), jnp.float32)
    _, ys = lax.scan(step, state0, (chunks(xh), chunks(dt), chunks(bm), chunks(cm)))
    return jnp.moveaxis(ys, 0, 1).reshape(xh.shape).astype(xh.dtype)

def _mamba2_mixer(h_z, h_xbc, h_dt, conv_w, conv_b, dt_bias, a_log, d_skip, ssm_norm_g):
    b, s, _ = h_xbc.shape
    xbc = lax.conv_general_dilated(h_xbc, conv_w[:, None, :], window_strides=(1,), padding=[(SSM_CONV - 1, 0)], dimension_numbers=('NWC', 'WIO', 'NWC'), feature_group_count=SSM_CONV_DIM)
    xbc = jax.nn.silu(xbc + conv_b)
    xs, bm, cm = jnp.split(xbc, [SSM_D_INNER, SSM_D_INNER + SSM_GROUPS * SSM_STATE], axis=-1)
    xh = xs.reshape(b, s, SSM_GROUPS, SSM_HPG, SSM_HEAD_DIM)
    bm = bm.reshape(b, s, SSM_GROUPS, SSM_STATE)
    cm = cm.reshape(b, s, SSM_GROUPS, SSM_STATE)
    dt = jax.nn.softplus((h_dt + dt_bias).astype(jnp.float32)).reshape(b, s, SSM_GROUPS, SSM_HPG)
    a = -jnp.exp(a_log.astype(jnp.float32)).reshape(SSM_GROUPS, SSM_HPG)
    y = _ssd_chunked_scan(xh, dt, a, bm, cm) + d_skip.reshape(SSM_GROUPS, SSM_HPG, 1) * xh
    y = y.reshape(b, s, SSM_D_INNER) * jax.nn.silu(h_z)
    yg = y.astype(jnp.float32).reshape(b, s, SSM_GROUPS, SSM_D_INNER // SSM_GROUPS)
    yg = yg * lax.rsqrt(jnp.mean(yg * yg, axis=-1, keepdims=True) + NORM_EPS)
    return (yg.reshape(b, s, SSM_D_INNER) * ssm_norm_g).astype(h_z.dtype)

def _compress(t, pe, w1, w2, idx):
    b = t.shape[0]
    blk = t[:, idx] + pe[None, None, :, None, :]
    blk = jnp.moveaxis(blk, 3, 2).reshape(b, idx.shape[0], NSA_KV_GROUPS, CMP_BLOCK * NSA_HEAD_DIM)
    return jax.nn.silu(blk @ w1) @ w2

def _nsa_mixer(q, kc, vc, ksl, vsl, kw, vw, gates, cos, sin, cmp_pe_k, cmp_w1_k, cmp_w2_k, cmp_pe_v, cmp_w1_v, cmp_w2_v):
    b, s = q.shape[:2]
    G, R, dk = NSA_KV_GROUPS, NSA_HPG, NSA_HEAD_DIM
    q = _rope(q.reshape(b, s, G, R, dk), cos, sin)
    kc = _rope(kc.reshape(b, s, G, dk), cos, sin)
    ksl = _rope(ksl.reshape(b, s, G, dk), cos, sin)
    kw = _rope(kw.reshape(b, s, G, dk), cos, sin)
    vc = vc.reshape(b, s, G, dk)
    vsl = vsl.reshape(b, s, G, dk)
    vw = vw.reshape(b, s, G, dk)
    gates = jax.nn.sigmoid(gates.astype(jnp.float32)).reshape(b, s, G, R, 3)
    n_cmp = (s - CMP_BLOCK) // CMP_STRIDE + 1
    cidx = jnp.arange(n_cmp)[:, None] * CMP_STRIDE + jnp.arange(CMP_BLOCK)[None, :]
    kcmp = _compress(kc, cmp_pe_k, cmp_w1_k, cmp_w2_k, cidx)
    vcmp = _compress(vc, cmp_pe_v, cmp_w1_v, cmp_w2_v, cidx)
    cstart = jnp.arange(n_cmp) * CMP_STRIDE
    cmp_end = cstart + CMP_BLOCK - 1
    n_sel = s // SEL_BLOCK
    sstart = jnp.arange(n_sel) * SEL_BLOCK
    overlap = ((cstart[:, None] < sstart[None, :] + SEL_BLOCK) & (cstart[:, None] + CMP_BLOCK > sstart[None, :])).astype(jnp.float32)
    ksb = jnp.moveaxis(ksl.reshape(b, n_sel, SEL_BLOCK, G, dk), 3, 1)
    vsb = jnp.moveaxis(vsl.reshape(b, n_sel, SEL_BLOCK, G, dk), 3, 1)
    kwp = jnp.pad(kw, ((0, 0), (WINDOW_2, 0), (0, 0), (0, 0)))
    vwp = jnp.pad(vw, ((0, 0), (WINDOW_2, 0), (0, 0), (0, 0)))
    scale = NSA_HEAD_DIM ** -0.5
    bi = jnp.arange(b)[:, None, None, None]
    gi = jnp.arange(G)[None, :, None, None]
    sel_j = jnp.arange(n_sel)
    win_off = jnp.arange(WINDOW_2 + NSA_QBLOCK) - WINDOW_2

    def block(qi):
        s0 = qi * NSA_QBLOCK
        t = s0 + jnp.arange(NSA_QBLOCK)
        qb = lax.dynamic_slice_in_dim(q, s0, NSA_QBLOCK, axis=1)
        gb = lax.dynamic_slice_in_dim(gates, s0, NSA_QBLOCK, axis=1)
        mask_c = (cmp_end[None, :] <= t[:, None])[None, :, None, None, :]
        pc = _masked_softmax(jnp.einsum('bqgrd,bcgd->bqgrc', qb, kcmp) * scale, mask_c)
        o_cmp = jnp.einsum('bqgrc,bcgd->bqgrd', pc, vcmp)
        local = t // SEL_BLOCK
        prio = jnp.where(sel_j[None, :] == local[:, None], 1e6, jnp.where(sel_j[None, :] > local[:, None], -jnp.inf, jnp.where(sel_j[None, :] == 0, 5e5, 0.0)))
        imp = jnp.einsum('bqgrc,cj->bqgj', pc, overlap) + prio[None, :, None, :]
        _, sel = lax.top_k(imp, SEL_TOPK)
        sel = jnp.swapaxes(sel, 1, 2)
        k_g = ksb[bi, gi, sel]
        v_g = vsb[bi, gi, sel]
        kpos = sel[..., None] * SEL_BLOCK + jnp.arange(SEL_BLOCK)
        mask_s = jnp.swapaxes(kpos <= t[None, None, :, None, None], 1, 2).reshape(b, NSA_QBLOCK, G, 1, SEL_TOPK * SEL_BLOCK)
        ss = jnp.einsum('bqgrd,bgqkld->bqgrkl', qb, k_g).reshape(b, NSA_QBLOCK, G, R, SEL_TOPK * SEL_BLOCK) * scale
        ps = _masked_softmax(ss, mask_s).reshape(b, NSA_QBLOCK, G, R, SEL_TOPK, SEL_BLOCK)
        o_slc = jnp.einsum('bqgrkl,bgqkld->bqgrd', ps, v_g)
        kwb = lax.dynamic_slice_in_dim(kwp, s0, WINDOW_2 + NSA_QBLOCK, axis=1)
        vwb = lax.dynamic_slice_in_dim(vwp, s0, WINDOW_2 + NSA_QBLOCK, axis=1)
        kpos_w = s0 + win_off
        mask_w = ((kpos_w[None, :] <= t[:, None]) & (kpos_w[None, :] > t[:, None] - WINDOW_2) & (kpos_w[None, :] >= 0))[None, :, None, None, :]
        pw = _masked_softmax(jnp.einsum('bqgrd,bkgd->bqgrk', qb, kwb) * scale, mask_w)
        o_win = jnp.einsum('bqgrk,bkgd->bqgrd', pw, vwb)
        return gb[..., 0:1] * o_cmp + gb[..., 1:2] * o_slc + gb[..., 2:3] * o_win

    out = lax.map(block, jnp.arange(s // NSA_QBLOCK))
    return jnp.moveaxis(out, 0, 1).reshape(b, s, NSA_WIDTH).astype(q.dtype)

def _hier_moe(h, w_rg, b_rg, w_re, b_re, w_g, w_u, w_d):
    b, s, d = h.shape
    t = h.reshape(b * s, d)
    tf = t.astype(jnp.float32)
    p_group = jax.nn.softmax(tf @ w_rg.astype(jnp.float32) + b_rg.astype(jnp.float32), axis=-1)
    pg, gsel = lax.top_k(p_group, 1)
    le = (tf @ w_re.astype(jnp.float32) + b_re.astype(jnp.float32)).reshape(-1, MOE_GROUPS, EXPERTS_PER_GROUP)
    le_g = jnp.einsum('tge,tg->te', le, jax.nn.one_hot(gsel[:, 0], MOE_GROUPS, dtype=jnp.float32))
    pe = jax.nn.softmax(le_g, axis=-1)
    pv, pi = lax.top_k(pe, EXPERT_TOPK)
    wts = pg * pv / jnp.sum(pv, axis=-1, keepdims=True)
    ids = gsel * EXPERTS_PER_GROUP + pi
    combine = jnp.sum(jax.nn.one_hot(ids, N_EXPERTS, dtype=jnp.float32) * wts[..., None], axis=1)
    out = jnp.zeros((b * s, d), jnp.float32)
    for e in range(N_EXPERTS):
        he = jax.nn.silu(t @ w_g[e]) * (t @ w_u[e])
        out = out + combine[:, e:e + 1] * (he @ w_d[e])
    return out.reshape(b, s, d).astype(h.dtype)

def _hybrid_layer(h, c, cos, sin, w_ada, b_ada, norm1_g, w_in, conv_w, conv_b, dt_bias, a_log, d_skip, ssm_norm_g, w_ssm_out, cmp_pe_k, cmp_w1_k, cmp_w2_k, cmp_pe_v, cmp_w1_v, cmp_w2_v, w_nsa_out, w_o, norm2_g, w_router_group, b_router_group, w_router_expert, b_router_expert, w_exp_gate, w_exp_up, w_exp_down):
    ada = jax.nn.silu(c) @ w_ada + b_ada
    shift1, scale1, gate1, shift2, scale2, gate2 = [a[:, None, :] for a in jnp.split(ada, 6, axis=-1)]
    hn = _rmsnorm(h, norm1_g) * (1.0 + scale1) + shift1
    offsets = [int(o) for o in np.cumsum(IN_SIZES)[:-1]]
    w_z, w_xbc, w_dt, w_q, w_kc, w_vc, w_ks, w_vs, w_kw, w_vw, w_gn, w_gs, w_ga = jnp.split(w_in, offsets, axis=1)
    y_ssm = _mamba2_mixer(hn @ w_z, hn @ w_xbc, hn @ w_dt, conv_w, conv_b, dt_bias, a_log, d_skip, ssm_norm_g) @ w_ssm_out
    y_nsa = _nsa_mixer(hn @ w_q, hn @ w_kc, hn @ w_vc, hn @ w_ks, hn @ w_vs, hn @ w_kw, hn @ w_vw, hn @ w_gn, cos, sin, cmp_pe_k, cmp_w1_k, cmp_w2_k, cmp_pe_v, cmp_w1_v, cmp_w2_v) @ w_nsa_out
    merged = jax.nn.sigmoid(hn @ w_gs) * y_ssm + jax.nn.sigmoid(hn @ w_ga) * y_nsa
    h = h + gate1 * (merged @ w_o)
    hn2 = _rmsnorm(h, norm2_g) * (1.0 + scale2) + shift2
    h = h + gate2 * _hier_moe(hn2, w_router_group, b_router_group, w_router_expert, b_router_expert, w_exp_gate, w_exp_up, w_exp_down)
    return h

def second_inputs(seed: int = 0) -> dict:
    key = jax.random.key(seed)
    ks = jax.random.split(key, 40)
    f32 = jnp.float32

    def nrm(k, shape, fan_in):
        return jax.random.normal(k, shape, f32) * fan_in ** -0.5

    def gain(k, shape):
        return 1.0 + 0.05 * jax.random.normal(k, shape, f32)

    def small(k, shape, s=0.02):
        return s * jax.random.normal(k, shape, f32)

    L = DEPTH_2
    dt0 = jnp.exp(jax.random.uniform(ks[9], (L, SSM_HEADS), f32) * (math.log(0.1) - math.log(0.001)) + math.log(0.001))
    return {
        'x': jax.random.normal(ks[0], (BATCH, SEQ, D_MODEL), f32),
        'c': jax.random.normal(ks[1], (BATCH, D_MODEL), f32),
        'positions': jnp.arange(SEQ, dtype=jnp.int32)[None, :] + jax.random.randint(ks[2], (BATCH, 1), 0, 4096, dtype=jnp.int32),
        'w_ada': nrm(ks[3], (L, D_MODEL, 6 * D_MODEL), D_MODEL),
        'b_ada': small(ks[4], (L, 6 * D_MODEL)),
        'norm1_g': gain(ks[5], (L, D_MODEL)),
        'w_in': nrm(ks[6], (L, D_MODEL, IN_WIDTH_2), D_MODEL),
        'conv_w': nrm(ks[7], (L, SSM_CONV, SSM_CONV_DIM), SSM_CONV),
        'conv_b': small(ks[8], (L, SSM_CONV_DIM)),
        'dt_bias': dt0 + jnp.log(-jnp.expm1(-dt0)),
        'a_log': jnp.log(jax.random.uniform(ks[10], (L, SSM_HEADS), f32, minval=1.0, maxval=16.0)),
        'd_skip': 1.0 + 0.1 * jax.random.normal(ks[11], (L, SSM_HEADS), f32),
        'ssm_norm_g': gain(ks[12], (L, SSM_D_INNER)),
        'w_ssm_out': nrm(ks[13], (L, SSM_D_INNER, D_MODEL), SSM_D_INNER),
        'cmp_pe_k': small(ks[14], (L, CMP_BLOCK, NSA_HEAD_DIM)),
        'cmp_w1_k': nrm(ks[15], (L, CMP_BLOCK * NSA_HEAD_DIM, CMP_HIDDEN), CMP_BLOCK * NSA_HEAD_DIM),
        'cmp_w2_k': nrm(ks[16], (L, CMP_HIDDEN, NSA_HEAD_DIM), CMP_HIDDEN),
        'cmp_pe_v': small(ks[17], (L, CMP_BLOCK, NSA_HEAD_DIM)),
        'cmp_w1_v': nrm(ks[18], (L, CMP_BLOCK * NSA_HEAD_DIM, CMP_HIDDEN), CMP_BLOCK * NSA_HEAD_DIM),
        'cmp_w2_v': nrm(ks[19], (L, CMP_HIDDEN, NSA_HEAD_DIM), CMP_HIDDEN),
        'w_nsa_out': nrm(ks[20], (L, NSA_WIDTH, D_MODEL), NSA_WIDTH),
        'w_o': nrm(ks[21], (L, D_MODEL, D_MODEL), D_MODEL),
        'norm2_g': gain(ks[22], (L, D_MODEL)),
        'w_router_group': nrm(ks[23], (L, D_MODEL, MOE_GROUPS), D_MODEL),
        'b_router_group': small(ks[24], (L, MOE_GROUPS), 0.01),
        'w_router_expert': nrm(ks[25], (L, D_MODEL, N_EXPERTS), D_MODEL),
        'b_router_expert': small(ks[26], (L, N_EXPERTS), 0.01),
        'w_exp_gate': nrm(ks[27], (L, N_EXPERTS, D_MODEL, EXPERT_HIDDEN), D_MODEL),
        'w_exp_up': nrm(ks[28], (L, N_EXPERTS, D_MODEL, EXPERT_HIDDEN), D_MODEL),
        'w_exp_down': nrm(ks[29], (L, N_EXPERTS, EXPERT_HIDDEN, D_MODEL), EXPERT_HIDDEN),
        'final_g': gain(ks[30], (D_MODEL,)),
    }

def second_block(x, c, positions, w_ada, b_ada, norm1_g, w_in, conv_w, conv_b, dt_bias, a_log, d_skip, ssm_norm_g, w_ssm_out, cmp_pe_k, cmp_w1_k, cmp_w2_k, cmp_pe_v, cmp_w1_v, cmp_w2_v, w_nsa_out, w_o, norm2_g, w_router_group, b_router_group, w_router_expert, b_router_expert, w_exp_gate, w_exp_up, w_exp_down, final_g):
    inv_freq = ROPE_THETA ** (-jnp.arange(0, NSA_HEAD_DIM, 2, dtype=jnp.float32) / NSA_HEAD_DIM)
    ang = positions.astype(jnp.float32)[..., None] * inv_freq
    cos, sin = jnp.cos(ang), jnp.sin(ang)
    h = x
    for l in range(DEPTH_2):
        h = _hybrid_layer(h, c, cos, sin, w_ada[l], b_ada[l], norm1_g[l], w_in[l], conv_w[l], conv_b[l], dt_bias[l], a_log[l], d_skip[l], ssm_norm_g[l], w_ssm_out[l], cmp_pe_k[l], cmp_w1_k[l], cmp_w2_k[l], cmp_pe_v[l], cmp_w1_v[l], cmp_w2_v[l], w_nsa_out[l], w_o[l], norm2_g[l], w_router_group[l], b_router_group[l], w_router_expert[l], b_router_expert[l], w_exp_gate[l], w_exp_up[l], w_exp_down[l])
    return _rmsnorm(h, final_g)


def setup_inputs(seed=0):
    out = dict(first_inputs(seed))
    for name, value in second_inputs(seed + 1).items():
        if name != "x":
            out[name + "_2"] = value
    return out


def reference(
    x, mix_norm_g, w_in, q_norm_g, k_norm_g, sinks, w_branch_sb, w_branch_swa, w_out,
    mlp_norm_g, w_up, w_down, c_2, positions_2, w_ada_2, b_ada_2, norm1_g_2, w_in_2, conv_w_2,
    conv_b_2, dt_bias_2, a_log_2, d_skip_2, ssm_norm_g_2, w_ssm_out_2, cmp_pe_k_2, cmp_w1_k_2,
    cmp_w2_k_2, cmp_pe_v_2, cmp_w1_v_2, cmp_w2_v_2, w_nsa_out_2, w_o_2, norm2_g_2,
    w_router_group_2, b_router_group_2, w_router_expert_2, b_router_expert_2, w_exp_gate_2,
    w_exp_up_2, w_exp_down_2, final_g_2,
):
    x = first_block(
        x, mix_norm_g, w_in, q_norm_g, k_norm_g, sinks, w_branch_sb, w_branch_swa, w_out,
        mlp_norm_g, w_up, w_down,
    )
    return second_block(
        x, c_2, positions_2, w_ada_2, b_ada_2, norm1_g_2, w_in_2, conv_w_2, conv_b_2, dt_bias_2,
        a_log_2, d_skip_2, ssm_norm_g_2, w_ssm_out_2, cmp_pe_k_2, cmp_w1_k_2, cmp_w2_k_2,
        cmp_pe_v_2, cmp_w1_v_2, cmp_w2_v_2, w_nsa_out_2, w_o_2, norm2_g_2, w_router_group_2,
        b_router_group_2, w_router_expert_2, b_router_expert_2, w_exp_gate_2, w_exp_up_2,
        w_exp_down_2, final_g_2,
    )


_drawn_inputs = setup_inputs


def setup_inputs(seed=0):
    import zlib

    import numpy as np

    out = dict(_drawn_inputs(seed))
    spreads = {}
    factors = {'mix_norm_g': 3.017,
     'q_norm_g': 8.0,
     'k_norm_g': 8.0,
     'sinks': 64.0,
     'norm1_g_2': 2.964,
     'conv_b_2': 21.659,
     'd_skip_2': 41.304,
     'ssm_norm_g_2': 11.599,
     'cmp_pe_k_2': 8.0,
     'cmp_pe_v_2': 56.593,
     'b_router_group_2': 36.073,
     'b_router_expert_2': 35.875,
     'norm2_g_2': 4.209}
    for name, (base, spread) in spreads.items():
        noise = np.random.default_rng([zlib.crc32(name.encode()), seed]).standard_normal(out[name].shape)
        drawn = base * np.exp(spread * noise) if base else spread * noise
        out[name] = jnp.asarray(drawn.astype(out[name].dtype))
    for name, factor in factors.items():
        out[name] = (out[name] * factor).astype(out[name].dtype)
    return out
```

```python
from contextlib import ExitStack

import numpy as np

import concourse.bass as bass
from concourse import mybir
from concourse.alu_op_type import AluOpType as ALU

F32 = mybir.dt.float32
F32R = mybir.dt.float32r
I32 = mybir.dt.int32
ACT = mybir.ActivationFunctionType
AX = mybir.AxisListType

P = 128
S, D = 512, 1024
TB, KC = S // P, D // P
HD = 64
DEPTH = 2
SBH = 8
SWH, SWKV = 8, 2
D_FF = 4 * D
EPS = 1e-6
NEG = -1e30
SBW = SBH * HD
SWQ, SWK = SWH * HD, SWKV * HD
COL = 256
C_SBV, C_SWQ, C_SWK, C_SWV, C_GATE = 2 * SBW, 3 * SBW, 3 * SBW + SWQ, 3 * SBW + SWQ + SWK, 3 * SBW + SWQ + 2 * SWK
STRIP = [S - P * b for b in range(TB)]
OFF = [sum(STRIP[:b]) for b in range(TB)]
PACK = sum(STRIP)
POFF = [0, 512, 1024, 1280]

FIRST_ONLY = ("band", "cos", "sin")


def constants():
    p = np.arange(P)[:, None]
    f = np.arange(P)[None, :]
    half = HD // 2
    c = {}
    c["ident"] = (p == f)
    c["ones"] = np.ones((P, P))
    c["suffix"] = (p >= f)
    c["prefix"] = (p <= f)
    c["strict"] = np.where(p < f, 0.0, NEG)
    c["causal_t"] = np.where(p <= f, 0.0, NEG)
    c["causal"] = np.where(f <= p, 0.0, NEG)
    c["headsum"] = (p // HD == f // HD)
    rot = np.zeros((P, P))
    for m in range(P):
        h, i = divmod(m, HD)
        if i < half:
            rot[h * HD + i + half, m] = -1.0
        else:
            rot[h * HD + i - half, m] = 1.0
    c["rot"] = rot
    j = np.arange(2 * P)[None, :]
    rel = j - P - p
    band = np.where((rel <= 0) & (rel > -P), 0.0, NEG)
    first = np.where(j <= p, 0.0, NEG)
    c["band"] = np.concatenate([first, band, band, band], 1)
    inv = (1.0 / np.power(10000.0, (np.arange(0, HD, 2) / HD))).astype(np.float32)
    ang = np.arange(S, dtype=np.float32)[None, :] * inv[(np.arange(P) % half)][:, None]
    c["cos"] = np.cos(ang.astype(np.float64))
    c["sin"] = np.sin(ang.astype(np.float64))
    c["inv"] = inv[np.arange(P) % half][:, None]
    ncmp = (S - 32) // 16 + 1
    t = (np.arange(TB)[None, :, None] * P + np.arange(P)[:, None, None])
    ok = (16 * np.arange(ncmp) + 31)[None, None, :] <= t
    c["cmp_neg"] = np.where(ok, 0.0, NEG).reshape(P, -1)
    c["cmp_one"] = ok.astype(np.float64).reshape(P, -1)
    jb = np.arange(S // 64)[None, None, :]
    loc = t // 64
    c["prio"] = np.where(jb == loc, 1e6, np.where(jb > loc, NEG, np.where(jb == 0, 5e5, 0.0))).reshape(P, -1)
    k8 = np.arange(8)
    c["before"] = np.broadcast_to((k8[None, :] < k8[:, None]).reshape(1, 64), (P, 64))
    c["before4"] = np.broadcast_to((k8[None, :4] < k8[:4, None]).reshape(1, 16), (P, 16))
    c = {n: c[n] for n in sorted(c, key=lambda n: n in FIRST_ONLY)}
    at, n = {}, 0
    for name, a in c.items():
        at[name] = (n, a.shape[1])
        n += a.shape[1]
    return np.ascontiguousarray(np.concatenate([np.asarray(a, np.float32) for a in c.values()], 1)), at


class Stages:

    POOLS, SIZE = 3, 44

    def __init__(self, nc):
        self.nc, self.n = nc, 0
        ids = sorted(nc.free_semaphores)
        self.base = ids[-self.POOLS * self.SIZE]
        assert ids[-1] - self.base + 1 == self.POOLS * self.SIZE

    def open(self, name, ctx):
        k = self.n % self.POOLS
        before = (self.n - 1) % self.POOLS
        self.n += 1
        ids = iter(range(self.base + k * self.SIZE, self.base + (k + 1) * self.SIZE))
        to_clear = range(self.base + before * self.SIZE, self.base + (before + 1) * self.SIZE)
        return (lambda what: ctx.enter_context(self.nc.semaphore(f"{name}_{what}", num=next(ids)))), to_clear


class Link:

    def __init__(self, eng, sem):
        self.eng, self.sem, self.n, self.i, self.per = eng, sem, 0, None, 0

    def __call__(self, ins):
        self.note(ins)
        self.wait()
        return ins

    def note(self, ins):
        ins.then_inc(self.sem, 1)
        self.n += 1

    def value(self):
        return self.n if self.i is None else self.n + self.i * self.per

    def wait(self):
        self.eng.wait_ge(self.sem, self.value())

    def loop(self, i, per):
        self.i, self.per, self.n0 = i, per, self.n

    def end(self, count):
        assert self.n - self.n0 == self.per, (self.n - self.n0, self.per)
        self.n = self.n0 + self.per * count
        self.i = None


class Weights:

    def __init__(self, nc, ctx):
        self.nc = nc
        sb = lambda n, dt: ctx.enter_context(nc.sbuf_tensor(n, [P, 2, KC, COL], dt))
        self.raw, self.hi, self.lo = sb("w_raw", F32), sb("w_hi", F32R), sb("w_lo", F32R)
        sem = lambda n: ctx.enter_context(nc.semaphore(n))
        self.raw_landed = [sem("raw_landed0"), sem("raw_landed1")]
        self.hi_ready, self.lo_ready = sem("hi_ready"), sem("lo_ready")
        self.tile_done = sem("tile_done")
        self.evicted = [sem("evicted0"), sem("evicted1")]

    def issue(self, sp, m, q, quarters, first=False):
        if not first:
            sp.wait_ge(self.lo_ready, 2 * m + q - 1)
        for dst, src in quarters:
            sp.dma_start(dst(self.raw[:, q]), src).then_inc(self.raw_landed[q], 16)

    def split_hi(self, act, m, q, first=False, cols=COL):
        act.wait_ge(self.raw_landed[q], 64 * m + 64)
        if not first:
            act.wait_ge(self.tile_done, 2 * m + q - 1)
        act.activation(self.hi[:, q, :, 0:cols], self.raw[:, q, :, 0:cols], ACT.Copy).then_inc(self.hi_ready, 1)

    def split_lo(self, dve, m, q, cols=COL):
        dve.wait_ge(self.hi_ready, 2 * m + q + 1)
        dve.tensor_tensor(self.lo[:, q, :, 0:cols], self.raw[:, q, :, 0:cols],
                          self.hi[:, q, :, 0:cols].bitcast(F32), ALU.subtract).then_inc(self.lo_ready, 1)

    def ready(self, pe, m, q, first=False):
        pe.wait_ge(self.lo_ready, 2 * m + q + 1)
        if not first:
            pe.wait_ge(self.evicted[q], m)

    def done(self, eng, m, q):
        eng.wait_ge(self.tile_done, 2 * m + q + 1)

    def read(self, eng, m, q):
        eng.wait_ge(self.evicted[q], m + 1)


def products(pe, out, w, x, start, stop):
    pe.matmul(out, w[0], x[0], start=start, stop=False)
    pe.matmul(out, w[0], x[1], start=False, stop=False)
    return pe.matmul(out, w[1], x[0], start=False, stop=stop)


def tile_columns(pe, W, m, q, ps, x, first=False, krange=range(KC), start=True, stop=True):
    W.ready(pe, m, q, first)
    for c in range(COL // P):
        for k in krange:
            mm = products(pe, ps[:, q, c], (W.hi[:, q, k, c * P:(c + 1) * P], W.lo[:, q, k, c * P:(c + 1) * P]),
                          (x[0][:, k - krange[0], :], x[1][:, k - krange[0], :]), k == krange[0], k == krange[-1])
    mm.then_inc(W.tile_done, 1)


def tile_tokens(pe, W, m, q, ps, x, n, first=False):
    W.ready(pe, m, q, first)
    for b in range(TB):
        out = ps[:, q].rearrange("p a b -> p (a b)")[:, b * COL:b * COL + n]
        for k in range(KC):
            mm = products(pe, out, (x[0][:, k, b * P:(b + 1) * P], x[1][:, k, b * P:(b + 1) * P]),
                          (W.hi[:, q, k, 0:n], W.lo[:, q, k, 0:n]), k == 0, k == KC - 1)
    mm.then_inc(W.tile_done, 1)


def quarters_of(src, n=COL, rows=KC):
    v = src.rearrange("(k p) n -> p k n", p=P)
    h = rows // 4
    return [(lambda t, a=a: t[:, a:a + h, 0:n], v[:, a:a + h, :]) for a in range(0, rows, h)]


class Kernel:
    def __init__(self, nc, dram, out, const_at, ctx):
        self.nc, self.d, self.out = nc, dram, out
        self.ctx = ctx
        self.stages = Stages(nc)
        self.W = Weights(nc, ctx)
        sb = self.sb
        self.cat = const_at
        self.n_const = min(const_at[n][0] for n in FIRST_ONLY)
        self.const = sb("const", [P, self.n_const])
        self.until_first = ctx.enter_context(ExitStack())
        self.const_first = self.until_first.enter_context(
            nc.sbuf_tensor("const_first", [P, dram["const"].shape[1] - self.n_const], F32, side="right"))
        self.x = sb("x", [P, KC, S])
        self.h = (sb("h_hi", [P, KC, S], F32R), sb("h_lo", [P, KC, S], F32R))
        self.ps = ctx.enter_context(nc.psum_tensor("ps", [P, 8, 512], F32))
        self.pst = self.ps[:].rearrange("p (q c) n -> p q c n", q=2)
        self.par = sb("par", [P, 96])

    def sb(self, name, shape, dt=F32):
        return self.ctx.enter_context(self.nc.sbuf_tensor(name, shape, dt))

    def c(self, name):
        a, n = self.cat[name]
        if name in FIRST_ONLY:
            return self.const_first[:, a - self.n_const:a - self.n_const + n]
        return self.const[:, a:a + n]

    def flat(self, a, n):
        return self.ps[:].rearrange("p b n -> p (b n)")[:, a * 512:a * 512 + n]

    def load(self):
        nc = self.nc
        with ExitStack() as st:
            sem, clear = self.stages.open("load", st)
            landed, turned, copied = sem("landed"), sem("turned"), sem("copied")
            xt = st.enter_context(nc.sbuf_tensor("x_tokens", [P, TB, D], F32))
            block = st.enter_context(nc.Block())

            @block.sync
            def _(sp):
                sp.dma_start(self.const[:], self.d["const"][:, 0:self.n_const]).then_inc(landed, 16)
                sp.dma_start(self.const_first[:], self.d["const"][:, self.n_const:]).then_inc(landed, 16)
                sp.dma_start(xt[:], self.d["x"].rearrange("o (b p) d -> p (o b) d", p=P)).then_inc(landed, 16)

            @block.tensor
            def _(pe):
                pe.wait_ge(landed, 48)
                for k in range(KC):
                    for b in range(TB):
                        t = pe.transpose(self.ps[:, k, b * P:(b + 1) * P], xt[:, b, k * P:(k + 1) * P], self.c("ident"))
                    t.then_inc(turned, 1)

            @block.vector
            def _(dve):
                for k in range(KC):
                    dve.wait_ge(turned, k + 1)
                    dve.tensor_copy(self.x[:, k, :], self.ps[:, k, :])

            @block.gpsimd
            def _(pool):
                pool.sem_clear(clear)

    def norm(self, name, params, gain, shift=None, prologue=None, split0=None):
        nc, W = self.nc, self.W
        with ExitStack() as st:
            sem, clear = self.stages.open(name, st)
            loaded, squared, summed, root = sem("loaded"), sem("squared"), sem("summed"), sem("root")
            steps, normed, rounded = sem("steps"), sem("normed"), sem("rounded")
            sq = st.enter_context(nc.sbuf_tensor(f"{name}_sq", [P, 2, S], F32))
            rs = st.enter_context(nc.sbuf_tensor(f"{name}_rs", [P, S], F32))
            tmp = st.enter_context(nc.sbuf_tensor(f"{name}_tmp", [P, 2, S], F32))
            used = sem("used")
            block = st.enter_context(nc.Block())
            h_hi, h_lo = self.h

            @block.sync
            def _(sp):
                if params:
                    params(sp, loaded)
                if prologue:
                    prologue(sp)

            @block.scalar
            def _(act):
                for k in range(KC):
                    if k >= 2:
                        act.wait_ge(used, k - 1)
                    act.activation(sq[:, k % 2], self.x[:, k, :], ACT.Square).then_inc(squared, 1)
                act.wait_ge(steps, 1)
                act.activation(rs[:], rs[:], ACT.Sqrt).then_inc(root, 1)
                if split0 is not None:
                    for q in range(2):
                        W.split_hi(act, split0, q, first=True)
                for k in range(KC):
                    act.wait_ge(normed, k + 1)
                    act.activation(h_hi[:, k, :], tmp[:, k % 2], ACT.Copy).then_inc(rounded, 1)

            @block.tensor
            def _(pe):
                for k in range(KC):
                    pe.wait_ge(squared, k + 1)
                    mm = pe.matmul(self.ps[:, 0, :], self.c("ones"), sq[:, k % 2], start=k == 0, stop=k == KC - 1)
                    mm.then_inc(used, 1)

            @block.vector
            def _(dve):
                dve.wait_ge(used, KC)
                dve.tensor_scalar(rs[:], self.ps[:, 0, :], 1.0 / D, EPS, ALU.mult, ALU.add).then_inc(steps, 1)
                if split0 is not None:
                    for q in range(2):
                        W.split_lo(dve, split0, q)
                dve.wait_ge(root, 1)
                dve.reciprocal(rs[:], rs[:]).then_inc(steps, 1)
                if params:
                    dve.wait_ge(loaded, params(None, None))
                dve.wait_ge(steps, 2)
                for k in range(KC):
                    if k >= 2:
                        dve.wait_ge(summed, k - 1)
                    first = dve.scalar_tensor_tensor(tmp[:, k % 2], self.x[:, k, :], gain(k), rs[:], ALU.mult, ALU.mult)
                    if shift is not None:
                        first.then_inc(steps, 1)
                        dve.wait_ge(steps, 3 + k)
                        first = dve.tensor_scalar(tmp[:, k % 2], tmp[:, k % 2], shift(k), None, ALU.add)
                    first.then_inc(normed, 1)
                    dve.wait_ge(rounded, k + 1)
                    dve.tensor_tensor(h_lo[:, k, :], tmp[:, k % 2], h_hi[:, k, :].bitcast(F32), ALU.subtract).then_inc(summed, 1)

            @block.gpsimd
            def _(pool):
                pool.sem_clear(clear)


PAIR_QK, PAIR_SBV, PAIR_SWQ, PAIR_SWKV, PAIR_GATE, PAIR_OUT, PAIR_MLP, PAIRS = 0, 2, 3, 4, 5, 11, 13, 29
QUARTERS = D_FF // D


class FirstBlock(Kernel):

    def row(self, name, l):
        return self.d[name][bass.ds(l, 1)]

    def layer_tile(self, l, m, q):
        w_in = self.row("w_in", l).rearrange("o k n -> (o k) n")
        t = 2 * m + q
        if m < PAIR_SBV:
            return quarters_of(w_in[:, t * COL:(t + 1) * COL])
        if m < PAIR_SWQ:
            t -= 2 * PAIR_SBV
            return quarters_of(w_in[:, C_SBV + t * COL:C_SBV + (t + 1) * COL])
        if m < PAIR_SWKV:
            t -= 2 * PAIR_SWQ
            return quarters_of(w_in[:, C_SWQ + t * COL:C_SWQ + (t + 1) * COL])
        if m < PAIR_GATE and q == 0:
            return self.twice(w_in, C_SWK)
        if m < PAIR_GATE:
            return quarters_of(w_in[:, C_SWV:C_SWV + SWK], SWK)
        if m < PAIR_OUT:
            p, kind = divmod(t - 2 * PAIR_GATE, 3)
            if kind < 2:
                a = C_GATE + kind * D + p * COL
                return quarters_of(w_in[:, a:a + COL])
            half = KC // 2
            sides = [self.row(n, l).rearrange("o k n -> (o k) n")[:, p * COL:(p + 1) * COL].rearrange("(k p) n -> p k n", p=P)
                     for n in ("w_branch_sb", "w_branch_swa")]
            return [(lambda t, a=half * i + 2 * j: t[:, a:a + 2, :], side[:, 2 * j:2 * j + 2, :])
                    for i, side in enumerate(sides) for j in range(2)]
        t -= 2 * PAIR_OUT
        return quarters_of(self.row("w_out", l).rearrange("o k n -> (o k) n")[:, t * COL:(t + 1) * COL])

    def twice(self, w, at):
        out = []
        for j in range(2):
            src = w[:, at + j * HD:at + (j + 1) * HD].rearrange("(k p) n -> p k n", p=P)
            for r in range(2):
                a = (2 * j + r) * HD
                out.append((lambda t, a=a: t[:, :, a:a + HD], src))
        return out

    def up_tile(self, l, j, q):
        w = self.row("w_up", l).rearrange("o k n -> (o k) n")
        return quarters_of(w[:, bass.ds(j * D + q * COL, COL)])

    def down_tile(self, l, j, q):
        w = self.row("w_down", l).rearrange("o k n -> (o k) n")
        return quarters_of(w[bass.ds(j * D, D), q * COL:(q + 1) * COL])

    def layer_params(self, l):
        def load(sp, sem):
            if sp is None:
                return 16 * 9
            col = lambda n: self.row(n, l).rearrange("o (k p) -> p (o k)", p=P)
            sp.dma_start(self.par[:, 0:8], col("mix_norm_g"), allow_slow_non_contiguous=True).then_inc(sem, 16)
            sp.dma_start(self.par[:, 8:16], col("mlp_norm_g"), allow_slow_non_contiguous=True).then_inc(sem, 16)
            for at, n in ((16, "q_norm_g"), (17, "k_norm_g")):
                for r in range(2):
                    sp.dma_start(self.par[r * HD:(r + 1) * HD, at:at + 1], self.row(n, l).rearrange("o k -> k o"),
                                 allow_slow_non_contiguous=True).then_inc(sem, 16)
            for r in range(3):
                a, b = (0, 32, 96)[r], (32, 96, 128)[r]
                sp.dma_start(self.par[a:b, 18:26], self.row("sinks", l).to_broadcast([b - a, SWH])).then_inc(sem, 16)
        return load

    def layer(self, l):
        W = self.W
        base = l * PAIRS
        self.l, self.base = l, base

        def prologue(sp):
            for m in range(2):
                for q in range(2):
                    W.issue(sp, base + m, q, self.layer_tile(l, m, q), first=m == 0)

        self.norm("norm1", self.layer_params(l), lambda k: self.par[:, k:k + 1], prologue=prologue, split0=base)
        with ExitStack() as until_merged:
            self.o_sb = self.parts(until_merged, "o_sb", 4)
            with ExitStack() as until_swa:
                right = lambda n, s: until_swa.enter_context(self.nc.sbuf_tensor(n, s, F32, side="right"))
                self.swq = right("swq", [P, 6, S])
                self.swv = right("swv", [P, TB, SWK])
                with ExitStack() as until_sb:
                    self.qk = until_sb.enter_context(self.nc.sbuf_tensor("qk", [P, 8, S], F32))
                    self.v = until_sb.enter_context(self.nc.sbuf_tensor("v", [P, TB, SBW], F32))
                    self.project()
                    self.stick_breaking()
                self.swa_prepare()
                self.o_sw = self.parts(until_merged, "o_sw", 4)
                self.swa()
            self.m = self.parts(until_merged, "merged", KC)
            self.merge()
            self.out_projection()
        self.norm("norm2", None, lambda k: self.par[:, 8 + k:9 + k])
        self.mlp()

    def parts(self, ctx, name, n):
        sb = lambda nm: ctx.enter_context(self.nc.sbuf_tensor(nm, [P, n, S], F32R))
        return sb(f"{name}_hi"), sb(f"{name}_lo")

    def project(self):
        nc, W, l, base = self.nc, self.W, self.l, self.base
        with ExitStack() as st:
            sem, clear = self.stages.open("project", st)
            block = st.enter_context(nc.Block())
            last = PAIR_GATE

            @block.sync
            def _(sp):
                for m in range(2, last + 2):
                    for q in range(2):
                        W.issue(sp, base + m, q, self.layer_tile(l, m, q))

            @block.tensor
            def _(pe):
                for m in range(last):
                    for q in range(2):
                        if PAIR_SBV <= m < PAIR_SWQ:
                            tile_tokens(pe, W, base + m, q, self.pst, self.h, COL)
                        elif m == PAIR_SWKV and q == 1:
                            tile_tokens(pe, W, base + m, q, self.pst, self.h, SWK)
                        else:
                            tile_columns(pe, W, base + m, q, self.pst, self.h, first=m == 0)

            @block.scalar
            def _(act):
                for m in range(last):
                    for q in range(2):
                        t = 2 * m + q
                        W.done(act, base + m, q)
                        pair = self.pst[:, q, 0:2, :]
                        tokens = self.pst[:, q].rearrange("p a b -> p (a b)")[:, 0:TB * COL].rearrange("p (b n) -> p b n", b=TB)
                        if m < PAIR_SBV // 2:
                            e = act.mul(self.qk[:, 2 * t:2 * t + 2, :], pair, HD ** -0.5)
                        elif m < PAIR_SBV:
                            e = act.activation(self.qk[:, 2 * t:2 * t + 2, :], pair, ACT.Copy)
                        elif m < PAIR_SWQ:
                            e = act.activation(self.v[:, :, q * COL:(q + 1) * COL], tokens, ACT.Copy)
                        elif m < PAIR_SWKV:
                            e = act.activation(self.swq[:, 2 * q:2 * q + 2, :], pair, ACT.Copy)
                        elif q == 0:
                            e = act.activation(self.swq[:, 4:6, :], pair, ACT.Copy)
                        else:
                            e = act.activation(self.swv[:], tokens[:, :, 0:SWK], ACT.Copy)
                        e.then_inc(W.evicted[q], 1)
                        W.split_hi(act, base + m + 1, q, cols=SWK if m + 1 == PAIR_SWKV and q == 1 else COL)

            @block.vector
            def _(dve):
                for m in range(last):
                    for q in range(2):
                        W.split_lo(dve, base + m + 1, q, cols=SWK if m + 1 == PAIR_SWKV and q == 1 else COL)

            @block.gpsimd
            def _(pool):
                pool.sem_clear(clear)

    def stick_breaking(self):
        nc = self.nc
        with ExitStack() as st:
            sem, clear = self.stages.open("sb", st)
            z_ready, z_taken, r_ready, r_taken = sem("z_ready"), sem("z_taken"), sem("r_ready"), sem("r_taken")
            expd, logd, absd, sp_ready, arg_ready, w_ready = (sem(n) for n in ("expd", "logd", "absd", "sp_ready", "arg_ready", "w_ready"))
            o_ready, o_hi, o_lo, w_used, masked = (sem(n) for n in ("o_ready", "o_hi", "o_lo", "w_used", "masked"))
            sb = lambda n, s: st.enter_context(nc.sbuf_tensor(n, s, F32))
            z, sp_, w = sb("sb_z", [P, 2, PACK]), sb("sb_softplus", [P, 2, PACK]), sb("sb_w", [P, 2, PACK])
            mask = sb("sb_mask", [P, PACK])
            z_ps, r_ps = self.flat(0, 1408), self.flat(3, 1408)
            parts = [(0, 896, 0), (896, PACK, 1024)]
            block = st.enter_context(nc.Block())

            def rows(h):
                return slice(HD * (h % 2), HD * (h % 2) + HD)

            @block.tensor
            def _(pe):
                def scores(h):
                    if h >= 1:
                        pe.wait_ge(z_taken, 2 * h)
                    for b in range(TB):
                        mm = pe.matmul(z_ps[:, POFF[b]:POFF[b] + STRIP[b]], self.qk[rows(h), 4 + h // 2, b * P:(b + 1) * P],
                                       self.qk[rows(h), h // 2, b * P:S], start=True, stop=True)
                    mm.then_inc(z_ready, 1)

                def suffix_sums(h):
                    pe.wait_ge(sp_ready, h + 1)
                    if h >= 1:
                        pe.wait_ge(r_taken, 2 * h)
                    for b in range(TB):
                        for j in range(b, TB):
                            a = POFF[b] + P * (j - b)
                            mm = pe.matmul(r_ps[:, a:a + STRIP[j]], self.c("suffix") if j == b else self.c("ones"),
                                           sp_[:, h % 2, OFF[j]:OFF[j] + STRIP[j]], start=j == b, stop=j == TB - 1)
                    mm.then_inc(r_ready, 1)

                def values(h):
                    pe.wait_ge(w_ready, h + 1)
                    if h >= 4:
                        pe.wait_ge(o_lo, h // 2 - 1)
                    for b in range(TB):
                        mm = pe.matmul(self.ps[rows(h), 6 + (h // 2) % 2, b * P:S], self.v[:, b, h * HD:(h + 1) * HD],
                                       w[:, h % 2, OFF[b]:OFF[b] + STRIP[b]], start=b == 0, stop=b == TB - 1)
                    mm.then_inc(o_ready, 1)

                scores(0)
                for h in range(SBH):
                    if h + 1 < SBH:
                        scores(h + 1)
                    if h >= 1:
                        values(h - 1)
                    suffix_sums(h)
                values(SBH - 1)

            @block.vector
            def _(dve):
                dve.wait_ge(masked, 1 + TB)

                def softplus(h):
                    dve.wait_ge(z_ready, h + 1)
                    if h >= 2:
                        dve.wait_ge(w_ready, h - 1)
                        dve.wait_ge(o_ready, h - 1)
                    for a, b, p in parts:
                        dve.tensor_tensor(z[:, h % 2, a:b], z_ps[:, p:p + b - a], mask[:, a:b], ALU.add).then_inc(z_taken, 1)
                    dve.wait_ge(z_taken, 2 * h + 2)
                    dve.scalar_tensor_tensor(w[:, h % 2], z[:, h % 2], -1.0, z[:, h % 2], ALU.mult, ALU.min).then_inc(absd, 1)
                    dve.wait_ge(logd, h + 1)
                    if h >= 2:
                        dve.wait_ge(r_ready, h - 1)
                    dve.scalar_tensor_tensor(sp_[:, h % 2], z[:, h % 2], 0.0, w[:, h % 2], ALU.max, ALU.add).then_inc(sp_ready, 1)

                def exponent(h):
                    dve.wait_ge(r_ready, h + 1)
                    dve.wait_ge(sp_ready, h + 1)
                    for a, b, p in parts:
                        dve.tensor_tensor(w[:, h % 2, a:b], z[:, h % 2, a:b], r_ps[:, p:p + b - a], ALU.subtract).then_inc(r_taken, 1)

                def out_low(c):
                    dve.wait_ge(o_hi, c + 1)
                    dve.tensor_tensor(self.o_sb[1][:, c, :], self.ps[:, 6 + c % 2, :], self.o_sb[0][:, c, :].bitcast(F32),
                                      ALU.subtract).then_inc(o_lo, 1)

                softplus(0)
                for h in range(SBH):
                    if h + 1 < SBH:
                        softplus(h + 1)
                    exponent(h)
                    if h >= 2 and h % 2 == 0:
                        out_low(h // 2 - 1)
                out_low(SBH // 2 - 1)

            @block.scalar
            def _(act):
                def logs(h):
                    act.wait_ge(absd, h + 1)
                    act.activation(w[:, h % 2], w[:, h % 2], ACT.Exp).then_inc(expd, 1)
                    act.wait_ge(expd, h + 1)
                    act.activation(w[:, h % 2], w[:, h % 2], ACT.Ln, bias=1.0).then_inc(logd, 1)

                def weights(h):
                    act.wait_ge(r_taken, 2 * h + 2)
                    act.activation(w[:, h % 2], w[:, h % 2], ACT.Exp).then_inc(w_ready, 1)

                def out_high(c):
                    act.wait_ge(o_ready, 2 * c + 2)
                    act.activation(self.o_sb[0][:, c, :], self.ps[:, 6 + c % 2, :], ACT.Copy).then_inc(o_hi, 1)

                logs(0)
                for h in range(SBH):
                    if h + 1 < SBH:
                        logs(h + 1)
                    weights(h)
                    if h >= 2 and h % 2 == 0:
                        out_high(h // 2 - 1)
                out_high(SBH // 2 - 1)

            @block.gpsimd
            def _(pool):
                pool.sem_clear(clear)
                pool.memset(mask[:], 0.0).then_inc(masked, 1)
                pool.wait_ge(masked, 1)
                for b in range(TB):
                    pool.tensor_copy(mask[:, OFF[b]:OFF[b] + P], self.c("strict")).then_inc(masked, 1)

    def swa_prepare(self):
        nc, n = self.nc, 6
        with ExitStack() as st:
            sem, clear = self.stages.open("swa_prepare", st)
            squared, summed, mean, root, inverse, normed, turned, cosd, sind, done, scaled = (sem(x) for x in (
                "squared", "summed", "mean", "root", "inverse", "normed", "turned", "cosd", "sind", "done", "scaled"))
            sb = lambda nm, s: st.enter_context(nc.sbuf_tensor(nm, s, F32))
            sq, rs, tc, ts = sb("swa_sq", [P, n, S]), sb("swa_rs", [P, n, S]), sb("swa_cos", [P, 2, S]), sb("swa_sin", [P, 2, S])
            gq = sb("swa_gain", [P, 1])
            x = self.swq
            block = st.enter_context(nc.Block())

            @block.scalar
            def _(act):
                act.mul(gq[:], self.par[:, 16:17], HD ** -0.5).then_inc(scaled, 1)
                for c in range(n):
                    act.activation(sq[:, c, :], x[:, c, :], ACT.Square).then_inc(squared, 1)
                for c in range(n):
                    act.wait_ge(mean, c + 1)
                    act.activation(rs[:, c, :], rs[:, c, :], ACT.Sqrt).then_inc(root, 1)

            @block.tensor
            def _(pe):
                for c in range(n):
                    pe.wait_ge(squared, c + 1)
                    pe.matmul(self.ps[:, c, :], self.c("headsum"), sq[:, c, :], start=True, stop=True).then_inc(summed, 1)
                for c in range(n):
                    pe.wait_ge(normed, c + 1)
                    pe.matmul(self.ps[:, c, :], self.c("rot"), x[:, c, :], start=True, stop=True).then_inc(turned, 1)

            @block.vector
            def _(dve):
                for c in range(n):
                    dve.wait_ge(summed, c + 1)
                    dve.tensor_scalar(rs[:, c, :], self.ps[:, c, :], 1.0 / HD, EPS, ALU.mult, ALU.add).then_inc(mean, 1)
                dve.wait_ge(scaled, 1)
                for c in range(n):
                    dve.wait_ge(root, c + 1)
                    dve.reciprocal(rs[:, c, :], rs[:, c, :]).then_inc(inverse, 1)
                    dve.wait_ge(inverse, c + 1)
                    g = gq[:] if c < 4 else self.par[:, 17:18]
                    dve.scalar_tensor_tensor(x[:, c, :], x[:, c, :], g, rs[:, c, :], ALU.mult, ALU.mult).then_inc(normed, 1)
                for c in range(n):
                    dve.wait_ge(turned, c + 1)
                    if c >= 2:
                        dve.wait_ge(done, c - 1)
                    dve.tensor_tensor(tc[:, c % 2], x[:, c, :], self.c("cos"), ALU.mult).then_inc(cosd, 1)
                    dve.tensor_tensor(ts[:, c % 2], self.ps[:, c, :], self.c("sin"), ALU.mult).then_inc(sind, 1)
                    dve.wait_ge(cosd, c + 1)
                    dve.wait_ge(sind, c + 1)
                    dve.tensor_tensor(x[:, c, :], tc[:, c % 2], ts[:, c % 2], ALU.add).then_inc(done, 1)

            @block.gpsimd
            def _(pool):
                pool.sem_clear(clear)

    def swa(self):
        nc = self.nc
        BAND = 2 * P
        turns = [(b, j) for b in range(TB) for j in range(2) if b > 0 or j == 0]
        with ExitStack() as st:
            sem, clear = self.stages.open("swa", st)
            s_ready, s_taken, maxed, negd, expd, sunk, added, inverse, p_ready, turned, t_taken, o_ready, o_hi, o_lo = (sem(x) for x in (
                "s_ready", "s_taken", "maxed", "negd", "expd", "sunk", "added", "inverse", "p_ready", "turned", "t_taken",
                "o_ready", "o_hi", "o_lo"))
            sb = lambda nm, s: st.enter_context(nc.sbuf_tensor(nm, s, F32))
            p, pt = sb("swa_p", [P, 2, TB, BAND]), sb("swa_pt", [P, 2, len(turns) * P])
            mx, neg, den, sink, inv = (sb(f"swa_{x}", [P, 2, TB]) for x in ("mx", "neg", "den", "sink", "inv"))
            block = st.enter_context(nc.Block())
            rows = lambda h: slice(HD * (h % 2), HD * (h % 2) + HD)
            key0 = lambda b: max(b - 1, 0) * P
            s_ps = lambda h: self.flat(2 * (h % 2), TB * BAND)
            t_ps = self.flat(4, len(turns) * P)

            @block.tensor
            def _(pe):
                def scores(h):
                    if h >= 2:
                        pe.wait_ge(s_taken, h - 1)
                    for b in range(TB):
                        mm = pe.matmul(s_ps(h)[:, b * BAND:(b + 1) * BAND], self.swq[rows(h), h // 2, b * P:(b + 1) * P],
                                       self.swq[rows(h), 4 + h // 4, key0(b):key0(b) + BAND], start=True, stop=True)
                    mm.then_inc(s_ready, 1)

                def turn(h):
                    pe.wait_ge(p_ready, h + 1)
                    if h >= 1:
                        pe.wait_ge(t_taken, h)
                    for n, (b, j) in enumerate(turns):
                        mm = pe.transpose(t_ps[:, n * P:(n + 1) * P], p[:, h % 2, b, j * P:(j + 1) * P], self.c("ident"))
                    mm.then_inc(turned, 1)

                def values(h):
                    pe.wait_ge(t_taken, h + 1)
                    if h >= 4:
                        pe.wait_ge(o_lo, h // 2 - 1)
                    for n, (b, j) in enumerate(turns):
                        mm = pe.matmul(self.ps[rows(h), 6 + (h // 2) % 2, b * P:(b + 1) * P],
                                       self.swv[:, key0(b) // P + j, (h // 4) * HD:(h // 4 + 1) * HD],
                                       pt[:, h % 2, n * P:(n + 1) * P], start=j == 0, stop=j == 1 or b == 0)
                    mm.then_inc(o_ready, 1)

                scores(0)
                for h in range(SWH):
                    if h + 1 < SWH:
                        scores(h + 1)
                    if h >= 1:
                        values(h - 1)
                    turn(h)
                values(SWH - 1)

            @block.vector
            def _(dve):
                def softmax_head(h):
                    i = h % 2
                    dve.wait_ge(s_ready, h + 1)
                    if h >= 2:
                        dve.wait_ge(turned, h - 1)
                    flat = p[:, i].rearrange("p b n -> p (b n)")
                    dve.tensor_tensor(flat, s_ps(h), self.c("band"), ALU.add).then_inc(s_taken, 1)
                    dve.wait_ge(s_taken, h + 1)
                    dve.tensor_reduce(mx[:, i], p[:, i], AX.X, ALU.max).then_inc(maxed, 1)
                    dve.wait_ge(maxed, h + 1)
                    dve.tensor_scalar(neg[:, i], mx[:, i], self.par[:, 18 + h:19 + h], -1.0, ALU.max, ALU.mult).then_inc(negd, 1)

                def normalise(h):
                    i = h % 2
                    dve.wait_ge(expd, TB * (h + 1))
                    dve.wait_ge(sunk, h + 1)
                    dve.tensor_tensor(den[:, i], den[:, i], sink[:, i], ALU.add).then_inc(added, 1)
                    dve.wait_ge(added, h + 1)
                    dve.reciprocal(inv[:, i], den[:, i]).then_inc(inverse, 1)
                    dve.wait_ge(inverse, h + 1)
                    dve.tensor_tensor(p[:, i], p[:, i], inv[:, i].unsqueeze(2).to_broadcast([P, TB, BAND]), ALU.mult).then_inc(p_ready, 1)

                def out_low(c):
                    dve.wait_ge(o_hi, c + 1)
                    dve.tensor_tensor(self.o_sw[1][:, c, :], self.ps[:, 6 + c % 2, :], self.o_sw[0][:, c, :].bitcast(F32),
                                      ALU.subtract).then_inc(o_lo, 1)

                softmax_head(0)
                for h in range(SWH):
                    if h + 1 < SWH:
                        softmax_head(h + 1)
                    normalise(h)
                    if h >= 3 and h % 2 == 1:
                        out_low(h // 2 - 1)
                out_low(SWH // 2 - 1)

            @block.scalar
            def _(act):
                def exps(h):
                    i = h % 2
                    act.wait_ge(negd, h + 1)
                    for b in range(TB):
                        act.activation(p[:, i, b], p[:, i, b], ACT.Exp, bias=neg[:, i, b:b + 1],
                                       accum_out=den[:, i, b:b + 1]).then_inc(expd, 1)
                    act.activation(sink[:, i], neg[:, i], ACT.Exp, bias=self.par[:, 18 + h:19 + h]).then_inc(sunk, 1)

                def evict(h):
                    act.wait_ge(turned, h + 1)
                    if h >= 2:
                        act.wait_ge(o_ready, h - 1)
                    act.activation(pt[:, h % 2], t_ps, ACT.Copy).then_inc(t_taken, 1)

                def out_high(c):
                    act.wait_ge(o_ready, 2 * c + 2)
                    act.activation(self.o_sw[0][:, c, :], self.ps[:, 6 + c % 2, :], ACT.Copy).then_inc(o_hi, 1)

                exps(0)
                for h in range(SWH):
                    if h + 1 < SWH:
                        exps(h + 1)
                    evict(h)
                    if h >= 3 and h % 2 == 1:
                        out_high(h // 2 - 1)
                out_high(SWH // 2 - 1)

            @block.gpsimd
            def _(pool):
                pool.sem_clear(clear)

    def merge(self):
        nc, W, l, base = self.nc, self.W, self.l, self.base
        n = COL // P
        with ExitStack() as st:
            sem, clear = self.stages.open("merge", st)
            first, summed, rounded, low = (sem(x) for x in ("first", "summed", "rounded", "low"))
            sb = lambda nm, s: st.enter_context(nc.sbuf_tensor(nm, s, F32))
            gate, y = sb("merge_gate", [P, 2, n, S]), sb("merge_y", [P, 2, n, S])
            tiles = [(m, q, *divmod(2 * (m - PAIR_GATE) + q, 3)) for m in range(PAIR_GATE, PAIR_OUT) for q in range(2)]
            block = st.enter_context(nc.Block())

            @block.sync
            def _(sp):
                for m in range(PAIR_GATE + 2, PAIR_OUT + 2):
                    for q in range(2):
                        W.issue(sp, base + m, q, self.layer_tile(l, m, q))

            @block.tensor
            def _(pe):
                for m, q, p, kind in tiles:
                    if kind < 2:
                        tile_columns(pe, W, base + m, q, self.pst, self.h)
                        continue
                    W.ready(pe, base + m, q)
                    for side, o in ((0, self.o_sb), (1, self.o_sw)):
                        for c in range(n):
                            for k in range(4):
                                cols = slice(c * P, (c + 1) * P)
                                mm = products(pe, self.pst[:, q, 2 * side + c],
                                              (W.hi[:, q, 4 * side + k, cols], W.lo[:, q, 4 * side + k, cols]),
                                              (o[0][:, k, :], o[1][:, k, :]), k == 0, k == 3)
                    mm.then_inc(W.tile_done, 1)

            @block.scalar
            def _(act):
                for m, q, p, kind in tiles:
                    if kind < 2:
                        W.done(act, base + m, q)
                        if p >= 1:
                            act.wait_ge(summed, p)
                        act.activation(gate[:, kind], self.pst[:, q, 0:n, :], ACT.Sigmoid).then_inc(W.evicted[q], 1)
                    W.split_hi(act, base + m + 1, q)
                    if kind == 2:
                        act.wait_ge(summed, p + 1)
                        act.activation(self.m[0][:, n * p:n * p + n, :], y[:, 0], ACT.Copy).then_inc(rounded, 1)

            @block.vector
            def _(dve):
                for m, q, p, kind in tiles:
                    if kind == 2:
                        W.done(dve, base + m, q)
                        for tile in (2 * m + q - 2, 2 * m + q - 1):
                            W.read(dve, base + tile // 2, tile % 2)
                        if p >= 1:
                            dve.wait_ge(low, p)
                        dve.tensor_tensor(y[:, 0], self.pst[:, q, 0:n, :], gate[:, 0], ALU.mult).then_inc(first, 1)
                        dve.tensor_tensor(y[:, 1], self.pst[:, q, n:2 * n, :], gate[:, 1], ALU.mult).then_inc(W.evicted[q], 1)
                        dve.wait_ge(first, p + 1)
                        W.read(dve, base + m, q)
                        dve.tensor_tensor(y[:, 0], y[:, 0], y[:, 1], ALU.add).then_inc(summed, 1)
                    W.split_lo(dve, base + m + 1, q)
                    if kind == 2:
                        dve.wait_ge(rounded, p + 1)
                        dve.tensor_tensor(self.m[1][:, n * p:n * p + n, :], y[:, 0], self.m[0][:, n * p:n * p + n, :].bitcast(F32),
                                          ALU.subtract).then_inc(low, 1)

            @block.gpsimd
            def _(pool):
                pool.sem_clear(clear)

    def out_projection(self):
        l = self.l

        def issue(sp):
            for q in range(4):
                self.W.issue(sp, self.base + PAIR_MLP + q // 2, q % 2, self.up_tile(l, 0, q))

        self.add_projection("out", self.base + PAIR_OUT, self.m, issue)

    def add_projection(self, name, m0, x_in, issue, scale=None):
        nc, W, n = self.nc, self.W, COL // P
        with ExitStack() as st:
            sem, clear = self.stages.open(name, st)
            block = st.enter_context(nc.Block())

            @block.sync
            def _(sp):
                issue(sp)

            @block.tensor
            def _(pe):
                for t in range(4):
                    tile_columns(pe, W, m0 + t // 2, t % 2, self.pst, x_in)

            @block.scalar
            def _(act):
                for t in range(4):
                    W.split_hi(act, m0 + 1 + t // 2, t % 2)

            @block.vector
            def _(dve):
                for t in range(4):
                    W.done(dve, m0 + t // 2, t % 2)
                    for c in range(n):
                        k = n * t + c
                        if scale is None:
                            e = dve.tensor_tensor(self.x[:, k, :], self.x[:, k, :], self.pst[:, t % 2, c], ALU.add)
                        else:
                            e = dve.scalar_tensor_tensor(self.x[:, k, :], self.pst[:, t % 2, c], scale(k), self.x[:, k, :], ALU.mult, ALU.add)
                    e.then_inc(W.evicted[t % 2], 1)
                    W.split_lo(dve, m0 + 1 + t // 2, t % 2)

            @block.gpsimd
            def _(pool):
                pool.sem_clear(clear)

    def mlp(self):
        nc, W, l, base, n = self.nc, self.W, self.l, self.base, COL // P
        with ExitStack() as st:
            sem, clear = self.stages.open("mlp", st)
            relud, squared, rounded, low, added = (sem(x) for x in ("relud", "squared", "rounded", "low", "added"))
            r = st.enter_context(nc.sbuf_tensor("mlp_relu", [P, 2, n, S], F32))
            u = self.parts(st, "mlp_u", KC)
            block = st.enter_context(nc.Block())
            pairs = PAIRS - PAIR_MLP
            m0 = base + PAIR_MLP
            per = 4

            @block.sync
            def _(sp):
                def down(j):
                    for t in range(4):
                        W.issue(sp, m0 + per * j + 2 + t // 2, t % 2, self.down_tile(l, j, t))

                with sp.Fori(0, QUARTERS - 1) as j:
                    down(j)
                    for t in range(4):
                        W.issue(sp, m0 + per * (j + 1) + t // 2, t % 2, self.up_tile(l, j + 1, t))
                down(QUARTERS - 1)

            @block.tensor
            def _(pe):
                with pe.Fori(0, QUARTERS) as j:
                    for t in range(4):
                        tile_columns(pe, W, m0 + per * j + t // 2, t % 2, self.pst, self.h)
                    pe.wait_ge(low, 4 * j + 4)
                    for t in range(4):
                        tile_columns(pe, W, m0 + per * j + 2 + t // 2, t % 2, self.pst, u)

            def scalar_quarter(act, j, last):
                for t in range(4):
                    q = t % 2
                    W.done(act, m0 + per * j + t // 2, q)
                    if t >= 2:
                        act.wait_ge(low, 4 * j + t - 1)
                    act.activation(r[:, q], self.pst[:, q, 0:n, :], ACT.Relu).then_inc(W.evicted[q], 1)
                    W.split_hi(act, m0 + per * j + t // 2 + 1, q)
                    act.wait_ge(squared, 4 * j + t + 1)
                    act.activation(u[0][:, n * t:n * t + n, :], r[:, q], ACT.Copy).then_inc(rounded, 1)
                for t in range(4):
                    if not (last and t >= 2):
                        W.split_hi(act, m0 + per * j + 2 + t // 2 + 1, t % 2)

            @block.scalar
            def _(act):
                with act.Fori(0, QUARTERS - 1) as j:
                    scalar_quarter(act, j, False)
                scalar_quarter(act, QUARTERS - 1, True)

            def vector_quarter(dve, j, last):
                for t in range(4):
                    q = t % 2
                    W.read(dve, m0 + per * j + t // 2, q)
                    dve.tensor_tensor(r[:, q], r[:, q], r[:, q], ALU.mult).then_inc(squared, 1)
                    W.split_lo(dve, m0 + per * j + t // 2 + 1, q)
                    dve.wait_ge(rounded, 4 * j + t + 1)
                    dve.tensor_tensor(u[1][:, n * t:n * t + n, :], r[:, q], u[0][:, n * t:n * t + n, :].bitcast(F32),
                                      ALU.subtract).then_inc(low, 1)
                for t in range(4):
                    W.done(dve, m0 + per * j + 2 + t // 2, t % 2)
                    for c in range(n):
                        k = n * t + c
                        e = dve.tensor_tensor(self.x[:, k, :], self.x[:, k, :], self.pst[:, t % 2, c], ALU.add)
                    e.then_inc(W.evicted[t % 2], 1)
                    if not (last and t >= 2):
                        W.split_lo(dve, m0 + per * j + 2 + t // 2 + 1, t % 2)

            @block.vector
            def _(dve):
                with dve.Fori(0, QUARTERS - 1) as j:
                    vector_quarter(dve, j, False)
                vector_quarter(dve, QUARTERS - 1, True)

            @block.gpsimd
            def _(pool):
                pool.sem_clear(clear)


SSM_IN, SSM_HEADS, SSM_G, SSM_N, CONV = 2 * D, 32, 4, 128, 4
SSM_XBC = SSM_IN + 2 * SSM_G * SSM_N
NH, NG, NKV = 16, 2, 2 * HD
HPG = NH // NG
CMP_STRIDE, CMP_BLOCK, CMP_HID = 16, 32, 256
NC = (S - CMP_BLOCK) // CMP_STRIDE + 1
SEL, TOPK = 64, 4
NSEL = S // SEL
MG, ME, EH = 4, 8, 256
NE = MG * ME
_at = np.cumsum([0, SSM_IN, SSM_XBC, SSM_HEADS, NH * HD] + [NKV] * 6 + [3 * NH, D, D]).tolist()
C_Z, C_XBC, C_DT, C_Q, C_KC, C_VC, C_KS, C_VS, C_KW, C_VW, C_GN, C_GS, C_GA = _at[:13]
B2 = DEPTH * PAIRS
P_XBC, P_SMALL, P_Z, P_SSMO, P_GS, P_Q, P_KK, P_GA, P_NSAO, P_WO, P_MOE = 0, 6, 7, 11, 15, 17, 19, 21, 23, 25, 27
BATCH_E = 4
MOE_PER = BATCH_E + 2
P_END = P_MOE + NE // BATCH_E * MOE_PER
_names = [("n1", 8), ("n2", 8), ("fin", 8), ("bada", 48), ("c", 8), ("convw", 96), ("convb", 24), ("dskip", 16), ("ssmg", 16),
          ("dtb", 32), ("alog", 32), ("brout", 36), ("pek", 16), ("pev", 16), ("ada", 48), ("g1", 8), ("g2", 8)]
PAR2, _n = {}, 0
for _name, _w in _names:
    PAR2[_name] = (_n, _w)
    _n += _w
PAR2_N = _n
TWO_PI = 2 * np.pi
PI_A = 6.28125
PI_B = float(np.float32(int((TWO_PI - PI_A) * 2 ** 20) / 2 ** 20))
PI_C = float(np.float32(TWO_PI - PI_A - PI_B))
ROUND = 1.5 * 2 ** 23


class SecondBlock(FirstBlock):
    def p2(self, name, a=0, n=None):
        o, w = PAR2[name]
        return self.par2[:, o + a:o + (w if n is None else a + n)]

    def tile2(self, m, q):
        w_in = self.d["w_in_2"].rearrange("o k n -> (o k) n")
        flat = lambda n: self.d[n].rearrange("o k n -> (o k) n")

        def both(a, na, b, nb):
            out = []
            for src, n, at in ((a, na, 0), (b, nb, na)):
                v = w_in[:, src:src + n].rearrange("(k p) n -> p k n", p=P)
                out += [(lambda t, h=h, at=at, n=n: t[:, h:h + KC // 2, at:at + n], v[:, h:h + KC // 2, :]) for h in (0, KC // 2)]
            return out

        t = 2 * m + q
        cols = lambda w, first, at=0: quarters_of(w[:, at + (t - 2 * first) * COL:at + (t - 2 * first + 1) * COL])
        if m < P_SMALL:
            return cols(w_in, P_XBC, C_XBC)
        if m < P_Z:
            return both(C_DT, SSM_HEADS, C_GN, 3 * NH) if q == 0 else both(C_VS, NKV, C_VW, NKV)
        if m < P_SSMO:
            return cols(w_in, P_Z, C_Z)
        if m < P_GS:
            half, t = divmod(t - 2 * P_SSMO, 4)
            return quarters_of(flat("w_ssm_out_2")[half * D:(half + 1) * D, t * COL:(t + 1) * COL])
        if m < P_Q:
            return cols(w_in, P_GS, C_GS)
        if m < P_KK:
            return cols(w_in, P_Q, C_Q)
        if m < P_GA:
            return self.twice(w_in, (C_KC, C_VC, C_KS, C_KW)[t - 2 * P_KK])
        if m < P_NSAO:
            return cols(w_in, P_GA, C_GA)
        if m < P_WO:
            return cols(flat("w_nsa_out_2"), P_NSAO)
        if m < P_MOE:
            return cols(flat("w_o_2"), P_WO)
        raise AssertionError

    def expert_tile(self, j, e, q):
        w = self.d["w_exp_up_2" if q else "w_exp_gate_2"].rearrange("o e k n -> (o e) k n")
        return quarters_of(w[bass.ds(j * BATCH_E + e, 1)].rearrange("e k n -> (e k) n"))

    def expert_down_tile(self, j, t):
        w = self.d["w_exp_down_2"].rearrange("o e k n -> (o e k) n")
        return quarters_of(w[bass.ds(j * D, D), t * COL:(t + 1) * COL])

    def issue2(self, sp, a, b):
        for m in range(a + 2, b + 2):
            for q in range(2):
                self.W.issue(sp, B2 + m, q, self.tile2(m, q) if m < P_MOE else self.expert_tile(0, m - P_MOE, q))

    def ada(self):
        nc, d = self.nc, self.d
        tiles, ring = 6 * D // COL, 6
        with ExitStack() as st:
            sem, clear = self.stages.open("ada", st)
            loaded, ctx, steps, product, biased, angle, rounded, folded, trig = (sem(x) for x in (
                "loaded", "ctx", "steps", "product", "biased", "angle", "rounded", "folded", "trig"))
            landed = [sem(f"landed{i}") for i in range(ring)]
            sb = lambda n, s, dt=F32: st.enter_context(nc.sbuf_tensor(n, s, dt))
            raw = sb("ada_w", [P, ring, KC, COL])
            pos, ang, kk = sb("positions", [P, S], I32), sb("angle", [P, 2, S]), sb("turns", [P, 2, S])
            sg = sb("ada_sig", [P, KC])
            cs = sb("ada_c", [P, KC])
            block = st.enter_context(nc.Block())
            loads = [0]

            @block.sync
            def _(sp):
                w = d["w_ada_2"].rearrange("o k n -> (o k) n")
                for t in range(tiles):
                    if t >= ring:
                        sp.wait_ge(product, t - ring + 1)
                    sp.dma_start(raw[:, t % ring], w[:, t * COL:(t + 1) * COL].rearrange("(k p) n -> p k n", p=P)).then_inc(landed[t % ring], 16)

            @block.scalar
            def _(act):
                def load(dst, src):
                    act.dma_start(dst, src, allow_slow_non_contiguous=True).then_inc(loaded, 16)
                    loads[0] += 16

                col = lambda n: d[n].rearrange("o (k p) -> p (o k)", p=P)
                act.dma_start(self.p2("c"), col("c_2"), allow_slow_non_contiguous=True).then_inc(ctx, 16)
                act.dma_start(pos[:], d["positions_2"].to_broadcast([P, S])).then_inc(angle, 16)
                for n, src in (("n1", "norm1_g_2"), ("n2", "norm2_g_2"), ("bada", "b_ada_2"), ("convb", "conv_b_2"), ("ssmg", "ssm_norm_g_2")):
                    load(self.p2(n), col(src))
                load(self.p2("fin"), d["final_g_2"].rearrange("(k p) -> p k", p=P))
                for i in range(CONV):
                    load(self.p2("convw", 24 * i, 24), d["conv_w_2"][0, i].rearrange("(k p) -> p k", p=P))
                for r in range(2):
                    rows = slice(r * HD, (r + 1) * HD)
                    o, w = PAR2["dskip"]
                    load(self.par2[rows, o:o + w], d["d_skip_2"].rearrange("o (k r) -> o k r", r=2)[:, :, r].to_broadcast([HD, w]))
                    for n, src in (("pek", "cmp_pe_k_2"), ("pev", "cmp_pe_v_2")):
                        o, w = PAR2[n]
                        load(self.par2[rows, o:o + w], d[src][0].rearrange("(i r) e -> r e i", r=2)[r])
                for n, src in (("dtb", "dt_bias_2"), ("alog", "a_log_2")):
                    load(self.p2(n), d[src].to_broadcast([P, SSM_HEADS]))
                load(self.p2("brout", 0, MG), d["b_router_group_2"].to_broadcast([P, MG]))
                load(self.p2("brout", MG, NE), d["b_router_expert_2"].to_broadcast([P, NE]))
                act.wait_ge(ctx, 16)
                act.activation(cs[:], self.p2("c"), ACT.Silu).then_inc(steps, 1)
                for i in range(2):
                    act.wait_ge(folded, i + 1)
                    act.activation(self.trig[:, i], ang[:, i], ACT.Sin).then_inc(trig, 1)

            @block.tensor
            def _(pe):
                pe.wait_ge(steps, 1)
                for t in range(tiles):
                    pe.wait_ge(landed[t % ring], 16 * (t // ring + 1))
                    for c in range(2):
                        for k in range(KC):
                            mm = pe.matmul(self.ps[:, 0, 2 * t + c:2 * t + c + 1], raw[:, t % ring, k, c * P:(c + 1) * P], cs[:, k:k + 1],
                                           start=k == 0, stop=k == KC - 1)
                    mm.then_inc(product, 1)

            @block.vector
            def _(dve):
                link = Link(dve, rounded)
                dve.wait_ge(angle, 16)
                link(dve.tensor_copy(ang[:, 0], pos[:]))
                link(dve.tensor_scalar(ang[:, 0], ang[:, 0], self.c("inv"), None, ALU.mult))
                link(dve.tensor_scalar(kk[:, 0], ang[:, 0], 1.0 / TWO_PI, ROUND, ALU.mult, ALU.add))
                link(dve.tensor_scalar(kk[:, 0], kk[:, 0], ROUND, None, ALU.subtract))
                for part in (PI_A, PI_B, PI_C):
                    link(dve.scalar_tensor_tensor(ang[:, 0], kk[:, 0], -part, ang[:, 0], ALU.mult, ALU.add))
                link(dve.tensor_scalar(ang[:, 1], ang[:, 0], float(np.pi / 2), None, ALU.add))
                link(dve.tensor_scalar(kk[:, 1], ang[:, 1], float(np.pi), -TWO_PI, ALU.is_gt, ALU.mult))
                link(dve.tensor_tensor(ang[:, 1], ang[:, 1], kk[:, 1], ALU.add))
                edge = 3.1415925
                for i in range(2):
                    dve.tensor_scalar(ang[:, i], ang[:, i], edge, -edge, ALU.min, ALU.max).then_inc(folded, 1)
                dve.wait_ge(loaded, loads[0])
                dve.wait_ge(product, tiles)
                link(dve.tensor_tensor(self.p2("ada"), self.ps[:, 0, 0:6 * KC], self.p2("bada"), ALU.add))
                for g, n, s in (("g1", "n1", 1), ("g2", "n2", 4)):
                    link(dve.scalar_tensor_tensor(self.p2(g), self.p2("ada", s * KC, KC), 1.0, self.p2(n), ALU.add, ALU.mult))

            @block.gpsimd
            def _(pool):
                pool.sem_clear(clear)

    def ssm_project(self):
        nc, W = self.nc, self.W
        n = COL // P
        with ExitStack() as st:
            sem, clear = self.stages.open("ssm_project", st)
            padded, tap, conved, active = sem("padded"), sem("tap"), sem("conved"), sem("active")
            sb = lambda nm, s: st.enter_context(nc.sbuf_tensor(nm, s, F32))
            xp, acc = sb("conv_in", [P, 2, n, S + CONV - 1]), sb("conv_acc", [P, 2, n, S])
            block = st.enter_context(nc.Block())
            tiles = 2 * (P_SMALL - P_XBC)
            dst = lambda t: self.xs[:, n * t:n * t + n, :] if n * t < 16 else self.bc[:, n * t - 16:n * t - 16 + n, :]

            @block.sync
            def _(sp):
                self.issue2(sp, P_XBC, P_Z)

            @block.tensor
            def _(pe):
                for t in range(tiles):
                    tile_columns(pe, W, B2 + t // 2, t % 2, self.pst, self.h, first=t < 2)
                tile_tokens(pe, W, B2 + P_SMALL, 0, self.pst, self.h, SSM_HEADS + 3 * NH)
                tile_tokens(pe, W, B2 + P_SMALL, 1, self.pst, self.h, 2 * NKV)

            @block.scalar
            def _(act):
                def silu(t):
                    act.wait_ge(conved, t + 1)
                    act.activation(dst(t), acc[:, t % 2], ACT.Silu).then_inc(active, 1)

                act.wait_ge(padded, 1)
                for t in range(tiles):
                    q = t % 2
                    W.done(act, B2 + t // 2, q)
                    if t >= 2:
                        act.wait_ge(conved, t - 1)
                    act.activation(xp[:, q, :, CONV - 1:], self.pst[:, q, 0:n, :], ACT.Copy).then_inc(W.evicted[q], 1)
                    nxt = (t + 2) // 2
                    W.split_hi(act, B2 + nxt, q, cols=SSM_HEADS + 3 * NH if nxt == P_SMALL and q == 0 else COL)
                    if t >= 1:
                        silu(t - 1)
                silu(tiles - 1)
                for q, (to, w) in enumerate(((self.dtgn, SSM_HEADS + 3 * NH), (self.vsvw, 2 * NKV))):
                    W.done(act, B2 + P_SMALL, q)
                    tok = self.pst[:, q].rearrange("p a b -> p (a b)")[:, 0:TB * COL].rearrange("p (b n) -> p b n", b=TB)
                    act.activation(to[:], tok[:, :, 0:w], ACT.Copy).then_inc(W.evicted[q], 1)
                    W.split_hi(act, B2 + P_SMALL + 1, q)

            @block.vector
            def _(dve):
                for t in range(tiles):
                    q = t % 2
                    W.read(dve, B2 + t // 2, q)
                    if t >= 2:
                        dve.wait_ge(active, t - 1)
                    for i in range(CONV - 1, -1, -1):
                        for c in range(n):
                            k = n * t + c
                            wt = self.p2("convw", 24 * i + k, 1)
                            src = xp[:, q, c, i:i + S]
                            if i == CONV - 1:
                                e = dve.tensor_scalar(acc[:, q, c], src, wt, self.p2("convb", k, 1), ALU.mult, ALU.add)
                            else:
                                dve.wait_ge(tap, 6 * t + 2 * (CONV - 2 - i) + c + 1)
                                e = dve.scalar_tensor_tensor(acc[:, q, c], src, wt, acc[:, q, c], ALU.mult, ALU.add)
                            if i:
                                e.then_inc(tap, 1)
                    e.then_inc(conved, 1)
                    nxt = (t + 2) // 2
                    W.split_lo(dve, B2 + nxt, q, cols=SSM_HEADS + 3 * NH if nxt == P_SMALL and q == 0 else COL)
                for q in range(2):
                    W.split_lo(dve, B2 + P_SMALL + 1, q)

            @block.gpsimd
            def _(pool):
                pool.sem_clear(clear)
                pool.memset(xp[:, :, :, 0:CONV - 1], 0.0).then_inc(padded, 1)

    def ssd(self):
        nc = self.nc
        U, HU = 8, 4
        UW = HU * HD
        with ExitStack() as st:
            sem, clear = self.stages.open("ssd", st)
            (prep, prep_a, dt_ready, xt_ready, ac_ready, acs_done, dl_ready, we_ready, wend, xn_copied, xdt_ready, xw_ready, ab_ready,
             seg_done, e_done, l_exp, m_ready, ce_ready, y_ready, s_ready, y_taken, scaled, st_added, cb_ready) = (sem(x) for x in (
                 "prep", "prep_a", "dt_ready", "xt_ready", "ac_ready", "acs_done", "dl_ready", "we_ready", "wend", "xn_copied",
                 "xdt_ready", "xw_ready", "ab_ready", "seg_done", "e_done", "l_exp", "m_ready", "ce_ready", "y_ready", "s_ready",
                 "y_taken", "scaled", "st_added", "cb_ready"))
            sb = lambda nm, s: st.enter_context(nc.sbuf_tensor(nm, s, F32))
            dt, dta, v, ea = sb("dt", [P, TB, SSM_HEADS]), sb("dt_a", [P, TB, SSM_HEADS]), sb("dt_v", [P, TB, SSM_HEADS]), sb("exp_a", [P, SSM_HEADS])
            xn, xdt, bn = sb("x_tok", [P, SSM_IN]), sb("x_dt", [P, SSM_IN]), sb("b_tok", [P, SSM_G * SSM_N])
            acs, dl, el = sb("acum", [P, SSM_HEADS]), sb("decay_end", [P, SSM_HEADS]), sb("decay_all", [P, SSM_HEADS])
            L, E = sb("ssd_l", [P, 2, HU, P]), sb("ssd_e", [P, 2, HU, P])
            state = sb("state", [P, SSM_IN])
            small = self.ps[:, 5, :]
            block = st.enter_context(nc.Block())
            heads = lambda t: t.rearrange("p (h e) -> p h e", e=HD)

            @block.tensor
            def _(pe):
                for ck in range(TB):
                    tok = slice(ck * P, (ck + 1) * P)
                    if ck > 0:
                        pe.wait_ge(y_taken, U * ck)
                        pe.wait_ge(st_added, U * ck)
                    for c in range(16):
                        pe.transpose(self.flat(0, 2048)[:, c * P:(c + 1) * P], self.xs[:, c, tok], self.c("ident"))
                    for g in range(SSM_G):
                        t = pe.transpose(self.ps[:, 4, g * P:(g + 1) * P], self.bc[:, g, tok], self.c("ident"))
                    t.then_inc(xt_ready, 1)
                    pe.wait_ge(dt_ready, 1)
                    pe.matmul(small[:, 0:SSM_HEADS], self.c("prefix"), dta[:, ck, :], start=True, stop=True)
                    pe.matmul(small[:, SSM_HEADS:2 * SSM_HEADS], self.c("ones"), dta[:, ck, :], start=True, stop=True).then_inc(ac_ready, 1)
                    pe.wait_ge(xn_copied, 2 * ck + 1)
                    for g in range(SSM_G):
                        mm = pe.matmul(self.ps[:, 4, g * P:(g + 1) * P], self.bc[:, g, tok], self.bc[:, SSM_G + g, tok], start=True, stop=True)
                    mm.then_inc(cb_ready, 1)

                    def front(u):
                        n, g = U * ck + u, u // 2
                        if n >= 2:
                            pe.wait_ge(seg_done, n - 1)
                        if n - 2 >= U:
                            pe.wait_ge(e_done, n - 1 - U)
                        for j in range(HU):
                            h = u * HU + j
                            mm = pe.matmul(self.ps[:, 6 + n % 2, j * P:(j + 1) * P], dta[:, ck, h:h + 1].to_broadcast([P, P]), self.c("prefix"),
                                           start=True, stop=True)
                        mm.then_inc(ab_ready, 1)

                    def back(u):
                        n, g = U * ck + u, u // 2
                        pe.wait_ge(m_ready, n + 1)
                        pe.wait_ge(xdt_ready, ck + 1)
                        if ck > 0:
                            pe.wait_ge(ce_ready, n + 1 - U)
                        if n >= 2:
                            pe.wait_ge(y_taken, n - 1)
                        for j in range(HU):
                            h = u * HU + j
                            out = self.ps[HD * (j % 2):HD * (j % 2) + HD, n % 2, (j // 2) * P:(j // 2 + 1) * P]
                            mm = pe.matmul(out, xdt[:, h * HD:(h + 1) * HD], L[:, n % 2, j, :], start=True, stop=ck == 0)
                            if ck > 0:
                                mm = pe.matmul(out, state[:, h * HD:(h + 1) * HD], E[:, n % 2, j, :], start=False, stop=True)
                        mm.then_inc(y_ready, 1)
                        if ck + 1 < TB:
                            pe.wait_ge(xw_ready, ck + 1)
                            if n >= 2:
                                pe.wait_ge(st_added, n - 1)
                            pe.matmul(self.ps[:, 2 + n % 2, 0:UW], bn[:, g * P:(g + 1) * P], xn[:, u * UW:(u + 1) * UW],
                                      start=True, stop=True).then_inc(s_ready, 1)

                    front(0)
                    for u in range(U):
                        if u + 1 < U:
                            front(u + 1)
                        back(u)

            @block.scalar
            def _(act):
                act.activation(ea[:], self.p2("alog"), ACT.Exp).then_inc(prep_a, 1)
                act.wait_ge(prep, 2)
                act.activation(dt[:], dt[:], ACT.Exp).then_inc(prep_a, 1)
                act.wait_ge(prep_a, 2)
                act.activation(dt[:], dt[:], ACT.Ln, bias=1.0).then_inc(prep_a, 1)
                for ck in range(TB):
                    act.wait_ge(xt_ready, ck + 1)
                    if ck > 0:
                        act.wait_ge(s_ready, U * ck)
                    act.activation(bn[:], self.ps[:, 4, :], ACT.Copy).then_inc(xn_copied, 1)
                    act.activation(xn[:], self.flat(0, SSM_IN), ACT.Copy).then_inc(xn_copied, 1)
                    act.wait_ge(dl_ready, ck + 1)
                    act.activation(el[:], small[:, SSM_HEADS:2 * SSM_HEADS], ACT.Exp).then_inc(we_ready, 1)
                    act.activation(dl[:], dl[:], ACT.Exp).then_inc(we_ready, 1)

                    def exps(u):
                        n = U * ck + u
                        act.wait_ge(seg_done, n + 1)
                        act.activation(L[:, n % 2], L[:, n % 2], ACT.Exp).then_inc(l_exp, 1)
                        if ck > 0:
                            act.wait_ge(y_ready, n - 1)
                            act.activation(E[:, n % 2], self.ps[:, 6 + n % 2, :].rearrange("p (j t) -> p j t", j=HU), ACT.Exp).then_inc(e_done, 1)

                    for u in range(U):
                        exps(u)

            @block.vector
            def _(dve):
                bias = self.p2("dtb").unsqueeze(1).to_broadcast([P, TB, SSM_HEADS])
                dve.tensor_tensor(v[:], self.dtgn[:, :, 0:SSM_HEADS], bias, ALU.add).then_inc(prep, 1)
                dve.wait_ge(prep, 1)
                dve.scalar_tensor_tensor(dt[:], v[:], -1.0, v[:], ALU.mult, ALU.min).then_inc(prep, 1)
                dve.wait_ge(prep_a, 3)
                dve.scalar_tensor_tensor(dt[:], v[:], 0.0, dt[:], ALU.max, ALU.add).then_inc(prep, 1)
                dve.wait_ge(prep, 3)
                dve.scalar_tensor_tensor(dta[:], dt[:], -1.0, ea[:].unsqueeze(1).to_broadcast([P, TB, SSM_HEADS]), ALU.mult, ALU.mult).then_inc(dt_ready, 1)
                for ck in range(TB):
                    tok = slice(ck * P, (ck + 1) * P)
                    per_head = lambda a: a.unsqueeze(2).to_broadcast([P, SSM_HEADS, HD])
                    dve.wait_ge(ac_ready, ck + 1)
                    if ck > 0:
                        dve.wait_ge(st_added, U * ck)
                    dve.tensor_copy(acs[:], small[:, 0:SSM_HEADS]).then_inc(acs_done, 1)
                    dve.wait_ge(acs_done, ck + 1)
                    if ck > 0:
                        dve.wait_ge(xw_ready, ck)
                    dve.tensor_tensor(dl[:], small[:, SSM_HEADS:2 * SSM_HEADS], acs[:], ALU.subtract).then_inc(dl_ready, 1)
                    dve.wait_ge(xn_copied, 2 * ck + 2)
                    if ck > 0:
                        dve.wait_ge(y_ready, U * ck)
                    dve.tensor_tensor(heads(xdt[:]), heads(xn[:]), per_head(dt[:, ck, :]), ALU.mult).then_inc(xdt_ready, 1)
                    dve.wait_ge(we_ready, 2 * ck + 2)
                    dve.wait_ge(xdt_ready, ck + 1)
                    if ck + 1 < TB:
                        dve.tensor_tensor(heads(xn[:]), heads(xdt[:]), per_head(dl[:]), ALU.mult).then_inc(xw_ready, 1)

                    def segment(u):
                        n = U * ck + u
                        dve.wait_ge(ab_ready, n + 1)
                        if n >= 2:
                            dve.wait_ge(y_ready, n - 1)
                        for j in range(HU):
                            e = dve.scalar_tensor_tensor(L[:, n % 2, j], self.ps[:, 6 + n % 2, j * P:(j + 1) * P], acs[:, u * HU + j:u * HU + j + 1],
                                                         self.c("causal_t"), ALU.subtract, ALU.add)
                        e.then_inc(seg_done, 1)

                    def weigh(u):
                        n, g = U * ck + u, u // 2
                        dve.wait_ge(l_exp, n + 1)
                        dve.wait_ge(cb_ready, ck + 1)
                        cb = self.ps[:, 4, g * P:(g + 1) * P].unsqueeze(1).to_broadcast([P, HU, P])
                        dve.tensor_tensor(L[:, n % 2], L[:, n % 2], cb, ALU.mult).then_inc(m_ready, 1)
                        if ck > 0:
                            dve.wait_ge(e_done, n + 1 - U)
                            cc = self.bc[:, SSM_G + g, tok].unsqueeze(1).to_broadcast([P, HU, P])
                            dve.tensor_tensor(E[:, n % 2], E[:, n % 2], cc, ALU.mult).then_inc(ce_ready, 1)

                    def finish(u):
                        n = U * ck + u
                        dve.wait_ge(y_ready, n + 1)
                        for c in range(2):
                            k = 2 * u + c
                            e = dve.scalar_tensor_tensor(self.xs[:, k, tok], self.xs[:, k, tok], self.p2("dskip", k, 1),
                                                         self.ps[:, n % 2, c * P:(c + 1) * P], ALU.mult, ALU.add)
                        e.then_inc(y_taken, 1)
                        if ck + 1 < TB:
                            mine = state[:, u * UW:(u + 1) * UW]
                            if ck == 0:
                                dve.wait_ge(s_ready, n + 1)
                                dve.tensor_copy(mine, self.ps[:, 2 + n % 2, 0:UW]).then_inc(st_added, 1)
                            else:
                                keep = el[:, u * HU:(u + 1) * HU].unsqueeze(2).to_broadcast([P, HU, HD])
                                dve.tensor_tensor(heads(mine), heads(mine), keep, ALU.mult).then_inc(scaled, 1)
                                dve.wait_ge(s_ready, n + 1)
                                dve.wait_ge(scaled, n + 1 - U)
                                dve.tensor_tensor(mine, mine, self.ps[:, 2 + n % 2, 0:UW], ALU.add).then_inc(st_added, 1)

                    segment(0)
                    for u in range(U):
                        if u + 1 < U:
                            segment(u + 1)
                        weigh(u)
                        if u >= 1:
                            finish(u - 1)
                    finish(U - 1)

            @block.gpsimd
            def _(pool):
                pool.sem_clear(clear)


class SsmTail(SecondBlock):

    def ssm_gate(self):
        nc, W, n = self.nc, self.W, COL // P
        tiles = 2 * (P_SSMO - P_Z)
        with ExitStack() as st:
            sem, clear = self.stages.open("ssm_gate", st)
            used = sem("used")
            z = st.enter_context(nc.sbuf_tensor("silu_z", [P, 2, n, S], F32))
            block = st.enter_context(nc.Block())

            @block.sync
            def _(sp):
                self.issue2(sp, P_Z, P_SSMO)

            @block.tensor
            def _(pe):
                for t in range(tiles):
                    tile_columns(pe, W, B2 + P_Z + t // 2, t % 2, self.pst, self.h)

            @block.scalar
            def _(act):
                for t in range(tiles):
                    m, q = B2 + P_Z + t // 2, t % 2
                    W.done(act, m, q)
                    if t >= 2:
                        act.wait_ge(used, t - 1)
                    act.activation(z[:, q], self.pst[:, q, 0:n, :], ACT.Silu).then_inc(W.evicted[q], 1)
                    W.split_hi(act, m + 1, q)

            @block.vector
            def _(dve):
                for t in range(tiles):
                    m, q = B2 + P_Z + t // 2, t % 2
                    W.read(dve, m, q)
                    dve.tensor_tensor(self.xs[:, n * t:n * t + n, :], self.xs[:, n * t:n * t + n, :], z[:, q], ALU.mult).then_inc(used, 1)
                    W.split_lo(dve, m + 1, q)

            @block.gpsimd
            def _(pool):
                pool.sem_clear(clear)

    def ssm_norm(self):
        nc, GC = self.nc, 4
        with ExitStack() as st:
            sem, clear = self.stages.open("ssm_norm", st)
            squared, used, mean, root, inverse, normed, rounded = (sem(x) for x in ("squared", "used", "mean", "root", "inverse", "normed", "rounded"))
            sb = lambda nm, s: st.enter_context(nc.sbuf_tensor(nm, s, F32))
            sq, rs = sb("ssm_sq", [P, 2, S]), sb("ssm_rs", [P, SSM_G, S])
            block = st.enter_context(nc.Block())

            @block.scalar
            def _(act):
                for k in range(16):
                    if k >= 2:
                        act.wait_ge(used, k - 1)
                    act.activation(sq[:, k % 2], self.xs[:, k, :], ACT.Square).then_inc(squared, 1)
                for g in range(SSM_G):
                    act.wait_ge(mean, g + 1)
                    act.activation(rs[:, g], rs[:, g], ACT.Sqrt).then_inc(root, 1)
                for k in range(KC):
                    act.wait_ge(normed, k + 1)
                    act.activation(self.yn[0][:, k, :], self.xs[:, k, :], ACT.Copy).then_inc(rounded, 1)

            @block.tensor
            def _(pe):
                for k in range(16):
                    pe.wait_ge(squared, k + 1)
                    pe.matmul(self.ps[:, k // GC, :], self.c("ones"), sq[:, k % 2], start=k % GC == 0, stop=k % GC == GC - 1).then_inc(used, 1)

            @block.vector
            def _(dve):
                for g in range(SSM_G):
                    dve.wait_ge(used, GC * g + GC)
                    dve.tensor_scalar(rs[:, g], self.ps[:, g, :], 1.0 / (GC * P), EPS, ALU.mult, ALU.add).then_inc(mean, 1)
                for k in range(16):
                    g = k // GC
                    if k % GC == 0:
                        dve.wait_ge(root, g + 1)
                        dve.reciprocal(rs[:, g], rs[:, g]).then_inc(inverse, 1)
                        dve.wait_ge(inverse, g + 1)
                    dve.scalar_tensor_tensor(self.xs[:, k, :], self.xs[:, k, :], self.p2("ssmg", k, 1), rs[:, g], ALU.mult, ALU.mult).then_inc(normed, 1)
                for k in range(KC):
                    dve.wait_ge(rounded, k + 1)
                    dve.tensor_tensor(self.yn[1][:, k, :], self.xs[:, k, :], self.yn[0][:, k, :].bitcast(F32), ALU.subtract)

            @block.gpsimd
            def _(pool):
                pool.sem_clear(clear)

    def ssm_out(self):
        nc, W, n = self.nc, self.W, COL // P
        with ExitStack() as st:
            sem, clear = self.stages.open("ssm_out", st)
            rounded, low = sem("rounded"), sem("low")
            block = st.enter_context(nc.Block())
            mid = B2 + P_SSMO + 1

            @block.sync
            def _(sp):
                self.issue2(sp, P_SSMO, P_GS)

            @block.tensor
            def _(pe):
                for t in range(8):
                    if t == 4:
                        pe.wait_ge(low, KC)
                    tile_columns(pe, W, B2 + P_SSMO + t // 2, t % 2, self.pst, self.yn)

            @block.scalar
            def _(act):
                for t in range(8):
                    m, q = B2 + P_SSMO + t // 2, t % 2
                    if t == 4:
                        for i in range(2):
                            W.done(act, mid, i)
                        for k in range(KC):
                            act.activation(self.yn[0][:, k, :], self.xs[:, KC + k, :], ACT.Copy).then_inc(rounded, 1)
                    W.split_hi(act, m + 1, q)

            @block.vector
            def _(dve):
                for t in range(8):
                    m, q = B2 + P_SSMO + t // 2, t % 2
                    if t == 4:
                        for k in range(KC):
                            dve.wait_ge(rounded, k + 1)
                            dve.tensor_tensor(self.yn[1][:, k, :], self.xs[:, KC + k, :], self.yn[0][:, k, :].bitcast(F32), ALU.subtract).then_inc(low, 1)
                    W.done(dve, m, q)
                    part = self.merged[:, n * (t % 4):n * (t % 4) + n, :]
                    if t < 4:
                        dve.tensor_copy(part, self.pst[:, q, 0:n, :]).then_inc(W.evicted[q], 1)
                    else:
                        dve.tensor_tensor(part, part, self.pst[:, q, 0:n, :], ALU.add).then_inc(W.evicted[q], 1)
                    W.split_lo(dve, m + 1, q)

            @block.gpsimd
            def _(pool):
                pool.sem_clear(clear)

    def nsa_project(self):
        nc, W, n = self.nc, self.W, COL // P
        with ExitStack() as st:
            sem, clear = self.stages.open("nsa_project", st)
            used = sem("used")
            g = st.enter_context(nc.sbuf_tensor("ssm_sig", [P, 2, n, S], F32))
            block = st.enter_context(nc.Block())
            tiles = 2 * (P_NSAO - P_GS)

            @block.sync
            def _(sp):
                self.issue2(sp, P_GS, P_NSAO)

            @block.tensor
            def _(pe):
                for t in range(tiles):
                    tile_columns(pe, W, B2 + P_GS + t // 2, t % 2, self.pst, self.h)

            @block.scalar
            def _(act):
                for t in range(tiles):
                    m, q = P_GS + t // 2, t % 2
                    pair = self.pst[:, q, 0:n, :]
                    W.done(act, B2 + m, q)
                    if m < P_Q:
                        if t >= 2:
                            act.wait_ge(used, t - 1)
                        e = act.activation(g[:, q], pair, ACT.Sigmoid)
                    elif m < P_KK:
                        e = act.mul(self.rp[:, n * (t - 4):n * (t - 4) + n, :], pair, HD ** -0.5)
                    elif m < P_GA:
                        i = t - 8
                        to = self.vc[:] if i == 1 else self.rp[:, (8, None, 10, 12)[i]:(10, None, 12, 14)[i], :]
                        e = act.activation(to, pair, ACT.Copy)
                    else:
                        i = t - 12
                        e = act.activation(self.gate[:, n * i:n * i + n, :], pair, ACT.Sigmoid)
                    e.then_inc(W.evicted[q], 1)
                    W.split_hi(act, B2 + m + 1, q)

            @block.vector
            def _(dve):
                for t in range(tiles):
                    m, q = P_GS + t // 2, t % 2
                    if m < P_Q:
                        W.read(dve, B2 + m, q)
                        part = self.merged[:, n * t:n * t + n, :]
                        dve.tensor_tensor(part, part, g[:, q], ALU.mult).then_inc(used, 1)
                    W.split_lo(dve, B2 + m + 1, q)

            @block.gpsimd
            def _(pool):
                pool.sem_clear(clear)

    def nsa_rope(self):
        nc, n = self.nc, 14
        with ExitStack() as st:
            sem, clear = self.stages.open("nsa_rope", st)
            turned, cosd, sind, done = sem("turned"), sem("cosd"), sem("sind"), sem("done")
            sb = lambda nm, s: st.enter_context(nc.sbuf_tensor(nm, s, F32))
            tc, ts = sb("rope_cos", [P, 2, S]), sb("rope_sin", [P, 2, S])
            x = self.rp
            block = st.enter_context(nc.Block())

            @block.tensor
            def _(pe):
                for c in range(n):
                    if c >= 8:
                        pe.wait_ge(sind, c - 7)
                    pe.matmul(self.ps[:, c % 8, :], self.c("rot"), x[:, c, :], start=True, stop=True).then_inc(turned, 1)

            @block.vector
            def _(dve):
                for c in range(n):
                    if c >= 2:
                        dve.wait_ge(done, c - 1)
                    dve.tensor_tensor(tc[:, c % 2], x[:, c, :], self.trig[:, 1], ALU.mult).then_inc(cosd, 1)
                    dve.wait_ge(turned, c + 1)
                    dve.tensor_tensor(ts[:, c % 2], self.ps[:, c % 8, :], self.trig[:, 0], ALU.mult).then_inc(sind, 1)
                    dve.wait_ge(cosd, c + 1)
                    dve.wait_ge(sind, c + 1)
                    dve.tensor_tensor(x[:, c, :], tc[:, c % 2], ts[:, c % 2], ALU.add).then_inc(done, 1)

            @block.gpsimd
            def _(pool):
                pool.sem_clear(clear)

    def nsa_compress(self):
        nc, d = self.nc, self.d
        NI, HC, NB = CMP_BLOCK // 2, CMP_HID // P, NG * NC
        with ExitStack() as st:
            sem, clear = self.stages.open("nsa_compress", st)
            w1_landed, w2_landed, cleared, gathered, hid_ready, silud, kv_ready, taken, gated = (sem(x) for x in (
                "w1_landed", "w2_landed", "cleared", "gathered", "hid_ready", "silud", "kv_ready", "taken", "gated"))
            sb = lambda nm, s: st.enter_context(nc.sbuf_tensor(nm, s, F32))
            w1 = sb("cmp_w1", [P, NI, CMP_HID])
            w2 = sb("cmp_w2", [P, 2, HC, P])
            blk = sb("cmp_blk", [P, NI, NB])
            hid_k = sb("cmp_hid_k", [P, HC, NG, NC])
            hid_v = sb("cmp_hid_v", [P, HC, NG, 4, 32])
            block = st.enter_context(nc.Block())

            @block.sync
            def _(sp):
                for i, (a, b) in enumerate((("cmp_w1_k_2", "cmp_w2_k_2"), ("cmp_w1_v_2", "cmp_w2_v_2"))):
                    if i:
                        sp.wait_ge(hid_ready, 1)
                    sp.dma_start(w1[:], d[a][0].rearrange("(k p) n -> p k n", p=P)).then_inc(w1_landed, 16)
                    for r in range(2):
                        sp.dma_start(w2[:, i, :, r * HD:(r + 1) * HD], d[b][0].rearrange("(k p) n -> p k n", p=P)).then_inc(w2_landed, 16)

            @block.vector
            def _(dve):
                for i, (src, pe_) in enumerate(((self.rp[:, 8:10, :], "pek"), (self.vc[:], "pev"))):
                    if i:
                        dve.wait_ge(hid_ready, 1)
                    for r in range(2):
                        rows = slice(r * HD, (r + 1) * HD)
                        o, w = PAR2[pe_]
                        for g in range(NG):
                            for q in range(2):
                                win = src[rows, g, q * 16:q * 16 + 16 * NC].rearrange("p (c i r) -> p i r c", i=8, r=2)[:, :, r, :]
                                e = dve.tensor_tensor(blk[rows, 8 * q:8 * q + 8, g * NC:(g + 1) * NC], win,
                                                      self.par2[rows, o + 8 * q:o + 8 * q + 8].unsqueeze(2).to_broadcast([HD, 8, NC]), ALU.add)
                    e.then_inc(gathered, 1)
                dve.wait_ge(kv_ready, 1)
                dve.tensor_copy(self.kcmp[:], self.ps[:, 4, 0:NB]).then_inc(taken, 1)
                dve.wait_ge(cleared, 1)
                dve.wait_ge(kv_ready, 2)
                for j in range(4):
                    rows = slice(32 * j, 32 * j + 32)
                    dve.tensor_copy(self.vcmp[rows, j], self.ps[rows, 5, 0:NG * HD].rearrange("p (g e) -> p g e", g=NG))

            @block.tensor
            def _(pe):
                for i in range(2):
                    pe.wait_ge(w1_landed, 16 * i + 16)
                    pe.wait_ge(gathered, i + 1)
                    for c in range(HC):
                        for k in range(NI):
                            mm = pe.matmul(self.ps[:, 2 * i + c, 0:NB], w1[:, k, c * P:(c + 1) * P], blk[:, k, :], start=k == 0, stop=k == NI - 1)
                    mm.then_inc(hid_ready, 1)
                pe.wait_ge(silud, 5 * HC)
                pe.wait_ge(w2_landed, 64)
                pe.wait_ge(cleared, 1)
                for c in range(HC):
                    mm = pe.matmul(self.ps[:, 4, 0:NB], w2[:, 0, c, :], hid_k[:, c], start=c == 0, stop=c == HC - 1)
                mm.then_inc(kv_ready, 1)
                for g in range(NG):
                    for c in range(HC):
                        mm = pe.matmul(self.ps[:, 5, g * HD:(g + 1) * HD], hid_v[:, c, g].rearrange("p r c -> p (r c)"), w2[:, 1, c, 0:HD],
                                       start=c == 0, stop=c == HC - 1)
                mm.then_inc(kv_ready, 1)

            @block.scalar
            def _(act):
                act.activation(self.dtgn[:, :, SSM_HEADS:], self.dtgn[:, :, SSM_HEADS:], ACT.Sigmoid).then_inc(gated, 1)
                act.wait_ge(cleared, 1)
                for i in range(2):
                    act.wait_ge(hid_ready, i + 1)
                    for c in range(HC):
                        src = self.ps[:, 2 * i + c, 0:NB].rearrange("p (g c) -> p g c", g=NG)
                        if i == 0:
                            act.activation(hid_k[:, c], src, ACT.Silu).then_inc(silud, 1)
                        else:
                            for r in range(4):
                                act.activation(hid_v[:, c, :, r, 0:NC], src, ACT.Silu).then_inc(silud, 1)

            @block.gpsimd
            def _(pool):
                pool.sem_clear(clear)
                pool.memset(hid_v[:], 0.0)
                pool.memset(self.vcmp[:], 0.0)
                pool.memset(self.strip[:, 0:S - P], 0.0)
                pool.tensor_copy(self.strip[:, S - P:S], self.c("causal")).then_inc(cleared, 1)

    def nsa_compressed(self):
        nc = self.nc
        with ExitStack() as st:
            sem, clear = self.stages.open("nsa_cmp", st)
            s_ready, s_taken, steps, shifted, expd, weighted, turned, t_taken, pooled = (sem(x) for x in (
                "s_ready", "s_taken", "steps", "shifted", "expd", "weighted", "turned", "t_taken", "pooled"))
            sb = lambda nm, s: st.enter_context(nc.sbuf_tensor(nm, s, F32))
            p = sb("cmp_p", [P, 2, HPG, NC])
            pc = sb("cmp_pc", [P, 2, HPG, 32])
            mx = sb("cmp_mx", [P, 2, HPG])
            ic = sb("cmp_ic", [P, NG * TB, 36])
            imp = sb("cmp_imp", [P, NG * TB, NSEL])
            gt, eq = sb("cmp_gt", [P, NG * TB, NSEL, NSEL]), sb("cmp_eq", [P, NG * TB, NSEL, NSEL])
            cnt = sb("cmp_cnt", [P, NG * TB, NSEL])
            block = st.enter_context(nc.Block())
            units = [(g, b) for g in range(NG) for b in range(TB)]

            @block.tensor
            def _(pe):
                def scores(u):
                    g, b = units[u]
                    if u >= 2:
                        pe.wait_ge(s_taken, u - 1)
                    for r in range(HPG):
                        h = HPG * g + r
                        rows = slice(HD * (h % 2), HD * (h % 2) + HD)
                        mm = pe.matmul(self.ps[:, 2 * (u % 2) + r % 2, 32 * (r // 2):32 * (r // 2) + NC], self.rp[rows, h // 2, b * P:(b + 1) * P],
                                       self.kcmp[rows, g * NC:(g + 1) * NC], start=True, stop=True)
                    mm.then_inc(s_ready, 1)

                def turn(u):
                    pe.wait_ge(weighted, u + 1)
                    if u >= 2:
                        pe.wait_ge(t_taken, u - 1)
                    for i in range(2):
                        mm = pe.transpose(self.ps[:, 4 + u % 2, i * P:(i + 1) * P], pc[:, u % 2, 4 * i:4 * i + 4].rearrange("p h c -> p (h c)"), self.c("ident"))
                    mm.then_inc(turned, 1)

                scores(0)
                for u in range(len(units)):
                    if u + 1 < len(units):
                        scores(u + 1)
                    turn(u)

            @block.scalar
            def _(act):
                for u, (g, b) in enumerate(units):
                    act.wait_ge(shifted, u + 1)
                    act.activation(p[:, u % 2], p[:, u % 2], ACT.Exp).then_inc(expd, 1)
                    act.wait_ge(turned, u + 1)
                    act.activation(self.pct[:, 2 * g:2 * g + 2, b * P:(b + 1) * P], self.ps[:, 4 + u % 2, 0:2 * P].rearrange("p (i t) -> p i t", i=2),
                                   ACT.Copy).then_inc(t_taken, 1)

            @block.vector
            def _(dve):
                link = Link(dve, steps)
                dve.wait_ge(pooled, 2)
                for u, (g, b) in enumerate(units):
                    i = u % 2
                    mask = lambda n: self.c(n).rearrange("p (b c) -> p b c", b=TB)[:, b, :].unsqueeze(1)
                    per_head = lambda a: a.unsqueeze(2).to_broadcast([P, HPG, NC])
                    dve.wait_ge(s_ready, u + 1)
                    for par in range(2):
                        src = self.ps[:, 2 * i + par, 0:P].rearrange("p (r c) -> p r c", c=32)[:, :, 0:NC]
                        e = dve.tensor_tensor(p[:, i].rearrange("p (r b) c -> p b r c", b=2)[:, par], src, mask("cmp_neg").to_broadcast([P, 4, NC]), ALU.add)
                    e.then_inc(s_taken, 1)
                    dve.wait_ge(s_taken, u + 1)
                    link(dve.tensor_reduce(mx[:, i], p[:, i], AX.X, ALU.max))
                    dve.tensor_tensor(p[:, i], p[:, i], per_head(mx[:, i]), ALU.subtract).then_inc(shifted, 1)
                    dve.wait_ge(expd, u + 1)
                    link(dve.tensor_tensor(p[:, i], p[:, i], mask("cmp_one").to_broadcast([P, HPG, NC]), ALU.mult))
                    link(dve.tensor_reduce(mx[:, i], p[:, i], AX.X, ALU.add))
                    link(dve.tensor_scalar(mx[:, i], mx[:, i], 1e-30, None, ALU.max))
                    link(dve.reciprocal(mx[:, i], mx[:, i]))
                    link(dve.tensor_tensor(p[:, i], p[:, i], per_head(mx[:, i]), ALU.mult))
                    dve.tensor_reduce(ic[:, u, 1:1 + NC], p[:, i].rearrange("p h c -> p c h"), AX.X, ALU.add)
                    gate = self.dtgn[:, b, SSM_HEADS:].rearrange("p (h t) -> p h t", t=3)[:, HPG * g:HPG * g + HPG, 0]
                    if u >= 2:
                        dve.wait_ge(turned, u - 1)
                    dve.tensor_tensor(pc[:, i, :, 0:NC], p[:, i], per_head(gate), ALU.mult).then_inc(weighted, 1)
                dve.wait_ge(weighted, len(units))
                link(dve.tensor_reduce(imp[:], ic[:, :, 0:32].rearrange("p u (j i) -> p u j i", i=4), AX.X, ALU.add))
                link(dve.tensor_tensor(imp[:], imp[:], ic[:, :, 4:36].rearrange("p u (j i) -> p u j i", i=4)[:, :, :, 0], ALU.add))
                prio = self.c("prio").rearrange("p (b j) -> p b j", b=TB)
                for g in range(NG):
                    e = link(dve.tensor_tensor(imp[:, TB * g:TB * g + TB], imp[:, TB * g:TB * g + TB], prio, ALU.add))
                shape = [P, NG * TB, NSEL, NSEL]
                others, own = imp[:].unsqueeze(2).to_broadcast(shape), imp[:].unsqueeze(3).to_broadcast(shape)
                before = self.c("before").rearrange("p (j k) -> p j k", j=NSEL).unsqueeze(1).to_broadcast(shape)
                link(dve.tensor_tensor(gt[:], others, own, ALU.is_gt))
                link(dve.tensor_tensor(eq[:], others, own, ALU.is_equal))
                link(dve.tensor_tensor(eq[:], eq[:], before, ALU.mult))
                link(dve.tensor_tensor(gt[:], gt[:], eq[:], ALU.add))
                link(dve.tensor_reduce(cnt[:], gt[:], AX.X, ALU.add))
                dve.tensor_scalar(self.selneg[:], cnt[:], float(TOPK), NEG, ALU.is_ge, ALU.mult)

            @block.gpsimd
            def _(pool):
                pool.sem_clear(clear)
                pool.memset(pc[:], 0.0).then_inc(pooled, 1)
                pool.memset(ic[:], 0.0).then_inc(pooled, 1)

    def nsa_attention(self):
        nc = self.nc
        units = [(g, b) for g in range(NG) for b in range(TB)]
        steps = [(u, r) for u in range(len(units)) for r in range(HPG)]
        with ExitStack() as st:
            sem, clear = self.stages.open("nsa", st)
            masked, s_ready, maxed, negd, expd, inverse, gated, p_ready, turned, t_taken, o_ready, o_hi, o_lo = (sem(x) for x in (
                "masked", "s_ready", "maxed", "negd", "expd", "inverse", "gated", "p_ready", "turned", "t_taken", "o_ready", "o_hi", "o_lo"))
            sb = lambda nm, s: st.enter_context(nc.sbuf_tensor(nm, s, F32))
            p, pt = sb("nsa_p", [P, 2, 2, S]), sb("nsa_pt", [P, 2, 2, S])
            mask = self.vc
            mx, neg, den, inv = (sb(f"nsa_{x}", [P, 2, 2]) for x in ("mx", "neg", "den", "inv"))
            o_parts = self.h
            block = st.enter_context(nc.Block())
            t_ps = lambda ty: self.ps[:, 4 + ty, :]

            @block.tensor
            def _(pe):
                def scores(n):
                    u, r = steps[n]
                    g, b = units[u]
                    h, W = HPG * g + r, (b + 1) * P
                    rows = slice(HD * (h % 2), HD * (h % 2) + HD)
                    if n >= 2:
                        pe.wait_ge(maxed, 2 * n - 2)
                    for ty, k0 in ((0, 10), (1, 12)):
                        mm = pe.matmul(self.ps[:, 2 * (n % 2) + ty, 0:W], self.rp[rows, h // 2, b * P:(b + 1) * P], self.rp[rows, k0 + g, 0:W],
                                       start=True, stop=True)
                    mm.then_inc(s_ready, 1)

                def turn(n):
                    u, r = steps[n]
                    g, b = units[u]
                    pe.wait_ge(p_ready, 2 * n + 2)
                    if n >= 1:
                        pe.wait_ge(t_taken, 2 * n)
                    for ty in range(2):
                        for j in range(b + 1):
                            mm = pe.transpose(t_ps(ty)[:, j * P:(j + 1) * P], p[:, n % 2, ty, j * P:(j + 1) * P], self.c("ident"))
                    mm.then_inc(turned, 1)

                def values(n):
                    u, r = steps[n]
                    g, b = units[u]
                    h = HPG * g + r
                    pe.wait_ge(t_taken, 2 * n + 2)
                    if u >= 2:
                        pe.wait_ge(o_lo, u - 1)
                    out = self.ps[HD * (h % 2):HD * (h % 2) + HD, 6 + u % 2, (r // 2) * P:(r // 2 + 1) * P]
                    pe.matmul(out, self.vcmp[:, h % 4, g, :], self.pct[:, h // 4, b * P:(b + 1) * P], start=True, stop=False)
                    for ty in range(2):
                        for j in range(b + 1):
                            mm = pe.matmul(out, self.vsvw[:, j, ty * NKV + g * HD:ty * NKV + (g + 1) * HD], pt[:, n % 2, ty, j * P:(j + 1) * P],
                                           start=False, stop=ty == 1 and j == b)
                    mm.then_inc(o_ready, 1)

                scores(0)
                for n in range(len(steps)):
                    if n + 1 < len(steps):
                        scores(n + 1)
                    if n >= 1:
                        values(n - 1)
                    turn(n)
                values(len(steps) - 1)

            @block.vector
            def _(dve):
                def softmax_max(n):
                    u, r = steps[n]
                    g, b = units[u]
                    W, i = (b + 1) * P, n % 2
                    causal = self.strip[:, S - W:S]
                    if r == 0:
                        view = lambda a: a.rearrange("p (j s) -> p j s", s=SEL)
                        if u >= 2:
                            dve.wait_ge(maxed, 2 * n - 2 * HPG)
                        dve.tensor_tensor(view(mask[:, u % 2, 0:W]), view(causal), self.selneg[:, u, 0:W // SEL].unsqueeze(2).to_broadcast([P, W // SEL, SEL]),
                                          ALU.add).then_inc(masked, 1)
                        dve.wait_ge(masked, u + 1)
                    dve.wait_ge(s_ready, n + 1)
                    if n >= 2:
                        dve.wait_ge(turned, n - 1)
                    for ty in range(2):
                        dve.tensor_tensor_reduce(p[:, i, ty, 0:W], self.ps[:, 2 * i + ty, 0:W], mask[:, u % 2, 0:W] if ty == 0 else causal, 1.0, -3e38,
                                                 ALU.add, ALU.max, mx[:, i, ty:ty + 1]).then_inc(maxed, 1)
                    dve.wait_ge(maxed, 2 * n + 2)
                    dve.tensor_scalar(neg[:, i], mx[:, i], -1.0, None, ALU.mult).then_inc(negd, 1)

                def normalise(n):
                    u, r = steps[n]
                    g, b = units[u]
                    W, i, h = (b + 1) * P, n % 2, HPG * g + r
                    dve.wait_ge(expd, 2 * n + 2)
                    dve.reciprocal(inv[:, i], den[:, i]).then_inc(inverse, 1)
                    dve.wait_ge(inverse, n + 1)
                    a = SSM_HEADS + 3 * h + 1
                    dve.tensor_tensor(inv[:, i], inv[:, i], self.dtgn[:, b, a:a + 2], ALU.mult).then_inc(gated, 1)
                    dve.wait_ge(gated, n + 1)
                    for ty in range(2):
                        dve.tensor_scalar(p[:, i, ty, 0:W], p[:, i, ty, 0:W], inv[:, i, ty:ty + 1], None, ALU.mult).then_inc(p_ready, 1)

                def evict(n):
                    u, r = steps[n]
                    W = (units[u][1] + 1) * P
                    dve.wait_ge(turned, n + 1)
                    if n >= 2:
                        dve.wait_ge(o_ready, n - 1)
                    dve.tensor_copy(pt[:, n % 2, 1, 0:W], t_ps(1)[:, 0:W]).then_inc(t_taken, 1)

                def out_low(u):
                    g, b = units[u]
                    dve.wait_ge(o_hi, u + 1)
                    dst = [part[:, 4 * g:4 * g + 4, b * P:(b + 1) * P] for part in o_parts]
                    dve.tensor_tensor(dst[1], self.ps[:, 6 + u % 2, :].rearrange("p (c t) -> p c t", c=4), dst[0].bitcast(F32), ALU.subtract).then_inc(o_lo, 1)

                softmax_max(0)
                for n in range(len(steps)):
                    if n + 1 < len(steps):
                        softmax_max(n + 1)
                    normalise(n)
                    evict(n)
                    if n >= HPG + 1 and n % HPG == 1:
                        out_low(n // HPG - 1)
                out_low(len(units) - 1)

            @block.scalar
            def _(act):
                def exps(n):
                    u, r = steps[n]
                    W, i = (units[u][1] + 1) * P, n % 2
                    act.wait_ge(negd, n + 1)
                    for ty in range(2):
                        act.activation(p[:, i, ty, 0:W], p[:, i, ty, 0:W], ACT.Exp, bias=neg[:, i, ty:ty + 1], accum_out=den[:, i, ty:ty + 1]).then_inc(expd, 1)

                def evict(n):
                    u, r = steps[n]
                    W = (units[u][1] + 1) * P
                    act.wait_ge(turned, n + 1)
                    if n >= 2:
                        act.wait_ge(o_ready, n - 1)
                    act.activation(pt[:, n % 2, 0, 0:W], t_ps(0)[:, 0:W], ACT.Copy).then_inc(t_taken, 1)

                def out_high(u):
                    g, b = units[u]
                    act.wait_ge(o_ready, HPG * (u + 1))
                    act.activation(o_parts[0][:, 4 * g:4 * g + 4, b * P:(b + 1) * P], self.ps[:, 6 + u % 2, :].rearrange("p (c t) -> p c t", c=4),
                                   ACT.Copy).then_inc(o_hi, 1)

                exps(0)
                for n in range(len(steps)):
                    if n + 1 < len(steps):
                        exps(n + 1)
                    evict(n)
                    if n >= HPG + 1 and n % HPG == 1:
                        out_high(n // HPG - 1)
                out_high(len(units) - 1)

            @block.gpsimd
            def _(pool):
                pool.sem_clear(clear)


class Whole(SsmTail):
    def nsa_out(self):
        nc, W, n = self.nc, self.W, COL // P
        tiles = 2 * (P_WO - P_NSAO)
        with ExitStack() as st:
            sem, clear = self.stages.open("nsa_out", st)
            gated, summed, rounded = sem("gated"), sem("summed"), sem("rounded")
            block = st.enter_context(nc.Block())

            @block.sync
            def _(sp):
                self.issue2(sp, P_NSAO, P_WO)

            @block.tensor
            def _(pe):
                for t in range(tiles):
                    tile_columns(pe, W, B2 + P_NSAO + t // 2, t % 2, self.pst, self.h)

            @block.scalar
            def _(act):
                for t in range(tiles):
                    W.split_hi(act, B2 + P_NSAO + t // 2 + 1, t % 2)
                    act.wait_ge(summed, t + 1)
                    act.activation(self.m[0][:, n * t:n * t + n, :], self.merged[:, n * t:n * t + n, :], ACT.Copy).then_inc(rounded, 1)

            @block.vector
            def _(dve):
                for t in range(tiles):
                    m, q = B2 + P_NSAO + t // 2, t % 2
                    part, gate = self.merged[:, n * t:n * t + n, :], self.gate[:, n * t:n * t + n, :]
                    W.done(dve, m, q)
                    dve.tensor_tensor(gate, gate, self.pst[:, q, 0:n, :], ALU.mult).then_inc(W.evicted[q], 1)
                    W.read(dve, m, q)
                    dve.tensor_tensor(part, part, gate, ALU.add).then_inc(summed, 1)
                    W.split_lo(dve, m + 1, q)
                    dve.wait_ge(rounded, t + 1)
                    dve.tensor_tensor(self.m[1][:, n * t:n * t + n, :], part, self.m[0][:, n * t:n * t + n, :].bitcast(F32), ALU.subtract)

            @block.gpsimd
            def _(pool):
                pool.sem_clear(clear)

    def route(self):
        nc, d = self.nc, self.d
        NR = MG + NE
        with ExitStack() as st:
            sem, clear = self.stages.open("route", st)
            landed, rounded, low, ready, steps, shifted, expd = (sem(x) for x in ("landed", "rounded", "low", "ready", "steps", "shifted", "expd"))
            sb = lambda nm, s, dt=F32: st.enter_context(nc.sbuf_tensor(nm, s, dt))
            raw, hi, lo = sb("route_w", [P, KC, NR]), sb("route_hi", [P, KC, NR], F32R), sb("route_lo", [P, KC, NR], F32R)
            lg = sb("route_logits", [P, TB, NR])
            eg, e8 = sb("route_eg", [P, TB, MG]), sb("route_e8", [P, TB, ME])
            a, b = sb("route_a", [P, TB]), sb("route_b", [P, TB])
            gt, eq = sb("route_gt", [P, TB, ME, ME]), sb("route_eq", [P, TB, ME, ME])
            one, two = sb("route_one", [P, TB, MG]), sb("route_two", [P, TB, ME])
            pick = sb("route_pick", [P, TB, MG, ME])
            block = st.enter_context(nc.Block())

            @block.sync
            def _(sp):
                for n, src, at in ((MG, "w_router_group_2", 0), (NE, "w_router_expert_2", MG)):
                    sp.dma_start(raw[:, :, at:at + n], d[src][0].rearrange("(k p) n -> p k n", p=P)).then_inc(landed, 16)

            @block.tensor
            def _(pe):
                pe.wait_ge(low, 1)
                for t in range(TB):
                    for k in range(KC):
                        mm = products(pe, self.ps[:, t, 0:NR], (self.h[0][:, k, t * P:(t + 1) * P], self.h[1][:, k, t * P:(t + 1) * P]),
                                      (hi[:, k, :], lo[:, k, :]), k == 0, k == KC - 1)
                mm.then_inc(ready, 1)

            @block.scalar
            def _(act):
                act.wait_ge(landed, 32)
                act.activation(hi[:], raw[:], ACT.Copy).then_inc(rounded, 1)
                for i, e in enumerate((eg, e8)):
                    act.wait_ge(shifted, i + 1)
                    act.activation(e[:], e[:], ACT.Exp).then_inc(expd, 1)

            @block.vector
            def _(dve):
                link = Link(dve, steps)
                dve.wait_ge(rounded, 1)
                dve.tensor_tensor(lo[:], raw[:], hi[:].bitcast(F32), ALU.subtract).then_inc(low, 1)
                dve.wait_ge(ready, 1)
                link(dve.tensor_tensor(lg[:], self.ps[:, 0:TB, 0:NR], self.p2("brout").unsqueeze(1).to_broadcast([P, TB, NR]), ALU.add))

                def rank(e, n, before, out, k):
                    shape = [P, TB, n, n]
                    others, own = e.unsqueeze(2).to_broadcast(shape), e.unsqueeze(3).to_broadcast(shape)
                    m = self.c(before).rearrange("p (j k) -> p j k", j=n).unsqueeze(1).to_broadcast(shape)
                    g_, q_ = gt[:, :, 0:n, 0:n], eq[:, :, 0:n, 0:n]
                    link(dve.tensor_tensor(g_, others, own, ALU.is_gt))
                    link(dve.tensor_tensor(q_, others, own, ALU.is_equal))
                    link(dve.tensor_tensor(q_, q_, m, ALU.mult))
                    link(dve.tensor_tensor(g_, g_, q_, ALU.add))
                    link(dve.tensor_reduce(out, g_, AX.X, ALU.add))
                    link(dve.tensor_scalar(out, out, float(k), None, ALU.is_lt))

                wide = lambda v, n: v.unsqueeze(2).to_broadcast([P, TB, n])
                link(dve.tensor_reduce(a[:], lg[:, :, 0:MG], AX.X, ALU.max))
                dve.tensor_tensor(eg[:], lg[:, :, 0:MG], wide(a[:], MG), ALU.subtract).then_inc(shifted, 1)
                dve.wait_ge(expd, 1)
                link(dve.tensor_reduce(a[:], eg[:], AX.X, ALU.add))
                rank(eg[:], MG, "before4", one[:], 1)
                experts = lg[:, :, MG:].rearrange("p t (g e) -> p t g e", g=MG)
                link(dve.tensor_tensor(pick[:], experts, one[:].unsqueeze(3).to_broadcast([P, TB, MG, ME]), ALU.mult))
                link(dve.tensor_reduce(e8[:], pick[:].rearrange("p t g e -> p t e g"), AX.X, ALU.add))
                link(dve.tensor_reduce(b[:], e8[:], AX.X, ALU.max))
                dve.tensor_tensor(e8[:], e8[:], wide(b[:], ME), ALU.subtract).then_inc(shifted, 1)
                dve.wait_ge(expd, 2)
                rank(e8[:], ME, "before", two[:], 2)
                link(dve.tensor_tensor(e8[:], e8[:], two[:], ALU.mult))
                link(dve.tensor_reduce(b[:], e8[:], AX.X, ALU.add))
                link(dve.tensor_tensor(b[:], b[:], a[:], ALU.mult))
                link(dve.reciprocal(b[:], b[:]))
                link(dve.tensor_tensor(e8[:], e8[:], wide(b[:], ME), ALU.mult))
                shape = [P, TB, MG, ME]
                for t in range(TB):
                    dve.tensor_tensor(self.comb[:, t].rearrange("p (g e) -> p g e", g=MG), e8[:, t].unsqueeze(1).to_broadcast([P, MG, ME]),
                                      one[:, t].unsqueeze(2).to_broadcast([P, MG, ME]), ALU.mult)

            @block.gpsimd
            def _(pool):
                pool.sem_clear(clear)

    def moe(self):
        nc, W, n = self.nc, self.W, COL // P
        J = NE // BATCH_E
        m0 = B2 + P_MOE
        with ExitStack() as st:
            sem, clear = self.stages.open("moe", st)
            silud, spread, weights, weighted, rounded, low = (sem(x) for x in ("silud", "spread", "weights", "weighted", "rounded", "low"))
            sb = lambda nm, s: st.enter_context(nc.sbuf_tensor(nm, s, F32))
            g, y, dg = sb("moe_silu", [P, 2, n, S]), sb("moe_y", [P, 2, n, S]), sb("moe_diag", [P, 2, TB, P])
            u = self.parts(st, "moe_u", KC)
            block = st.enter_context(nc.Block())
            bank = lambda e: self.ps[:, 2 + e % 2, :]

            @block.sync
            def _(sp):
                def rest(j):
                    for e in range(2, BATCH_E):
                        for q in range(2):
                            W.issue(sp, m0 + MOE_PER * j + e, q, self.expert_tile(j, e, q))
                    for t in range(4):
                        W.issue(sp, m0 + MOE_PER * j + BATCH_E + t // 2, t % 2, self.expert_down_tile(j, t))

                with sp.Fori(0, J - 1) as j:
                    rest(j)
                    for e in range(2):
                        for q in range(2):
                            W.issue(sp, m0 + MOE_PER * (j + 1) + e, q, self.expert_tile(j + 1, e, q))
                rest(J - 1)

            @block.tensor
            def _(pe):
                with pe.Fori(0, J) as j:
                    for e in range(BATCH_E):
                        pe.wait_ge(spread, BATCH_E * j + e + 1)
                        if e >= 2:
                            pe.wait_ge(weighted, BATCH_E * j + e - 1)
                        pe.matmul(bank(e), self.c("ones"), dg[:, e % 2].rearrange("p b t -> p (b t)"), start=True, stop=True).then_inc(weights, 1)
                        for q in range(2):
                            tile_columns(pe, W, m0 + MOE_PER * j + e, q, self.pst, self.h)
                    pe.wait_ge(low, BATCH_E * (j + 1))
                    for t in range(4):
                        tile_columns(pe, W, m0 + MOE_PER * j + BATCH_E + t // 2, t % 2, self.pst, u)

            def scalar_batch(act, j, last):
                for e in range(BATCH_E):
                    m = m0 + MOE_PER * j + e
                    W.done(act, m, 0)
                    if e >= 2:
                        W.read(act, m - 2, 1)
                    act.activation(g[:, e % 2], self.pst[:, 0, 0:n, :], ACT.Silu).then_inc(W.evicted[0], 1)
                    for q in range(2):
                        W.split_hi(act, m + 1, q)
                    act.wait_ge(weighted, BATCH_E * j + e + 1)
                    act.activation(u[0][:, n * e:n * e + n, :], y[:, e % 2], ACT.Copy).then_inc(rounded, 1)
                for t in range(4):
                    if not (last and t >= 2):
                        W.split_hi(act, m0 + MOE_PER * j + BATCH_E + t // 2 + 1, t % 2)

            @block.scalar
            def _(act):
                with act.Fori(0, J - 1) as j:
                    scalar_batch(act, j, False)
                scalar_batch(act, J - 1, True)

            def vector_batch(dve, j, last):
                def diagonal(e):
                    col = self.comb[:, :, bass.ds(BATCH_E * j + e, 1)].to_broadcast([P, TB, P])
                    dve.tensor_tensor(dg[:, e % 2], self.c("ident").unsqueeze(1).to_broadcast([P, TB, P]), col, ALU.mult).then_inc(spread, 1)

                diagonal(0)
                for e in range(BATCH_E):
                    m = m0 + MOE_PER * j + e
                    if e + 1 < BATCH_E:
                        if e >= 1:
                            dve.wait_ge(weights, BATCH_E * j + e)
                        diagonal(e + 1)
                    W.read(dve, m, 0)
                    W.done(dve, m, 1)
                    dve.tensor_tensor(y[:, e % 2], g[:, e % 2], self.pst[:, 1, 0:n, :], ALU.mult).then_inc(W.evicted[1], 1)
                    W.split_lo(dve, m + 1, 0)
                    W.read(dve, m, 1)
                    dve.wait_ge(weights, BATCH_E * j + e + 1)
                    dve.tensor_tensor(y[:, e % 2], y[:, e % 2], bank(e).unsqueeze(1).to_broadcast([P, n, S]), ALU.mult).then_inc(weighted, 1)
                    W.split_lo(dve, m + 1, 1)
                    dve.wait_ge(rounded, BATCH_E * j + e + 1)
                    dve.tensor_tensor(u[1][:, n * e:n * e + n, :], y[:, e % 2], u[0][:, n * e:n * e + n, :].bitcast(F32), ALU.subtract).then_inc(low, 1)
                for t in range(4):
                    m = m0 + MOE_PER * j + BATCH_E + t // 2
                    W.done(dve, m, t % 2)
                    for c in range(n):
                        k = n * t + c
                        e = dve.scalar_tensor_tensor(self.x[:, k, :], self.pst[:, t % 2, c], self.p2("ada", 5 * KC + k, 1), self.x[:, k, :], ALU.mult, ALU.add)
                    e.then_inc(W.evicted[t % 2], 1)
                    if not (last and t >= 2):
                        W.split_lo(dve, m + 1, t % 2)

            @block.vector
            def _(dve):
                with dve.Fori(0, J - 1) as j:
                    vector_batch(dve, j, False)
                vector_batch(dve, J - 1, True)

            @block.gpsimd
            def _(pool):
                pool.sem_clear(clear)

    def finish(self):
        nc = self.nc
        with ExitStack() as st:
            sem, clear = self.stages.open("finish", st)
            squared, used, mean, root, inverse, normed, turned, taken, copied = (sem(x) for x in (
                "squared", "used", "mean", "root", "inverse", "normed", "turned", "taken", "copied"))
            sb = lambda nm, s: st.enter_context(nc.sbuf_tensor(nm, s, F32))
            sq, rs, y = sb("fin_sq", [P, 2, S]), sb("fin_rs", [P, S]), sb("fin_tokens", [P, TB, D])
            block = st.enter_context(nc.Block())

            @block.scalar
            def _(act):
                for k in range(KC):
                    if k >= 2:
                        act.wait_ge(used, k - 1)
                    act.activation(sq[:, k % 2], self.x[:, k, :], ACT.Square).then_inc(squared, 1)
                act.wait_ge(mean, 1)
                act.activation(rs[:], rs[:], ACT.Sqrt).then_inc(root, 1)
                for k in range(0, KC, 2):
                    act.wait_ge(turned, k + 1)
                    act.activation(y[:, :, k * P:(k + 1) * P], self.ps[:, 1 + k % 4, :].rearrange("p (b f) -> p b f", b=TB), ACT.Copy).then_inc(taken, 1)

            @block.tensor
            def _(pe):
                for k in range(KC):
                    pe.wait_ge(squared, k + 1)
                    pe.matmul(self.ps[:, 0, :], self.c("ones"), sq[:, k % 2], start=k == 0, stop=k == KC - 1).then_inc(used, 1)
                for k in range(KC):
                    pe.wait_ge(normed, k + 1)
                    if k >= 4:
                        pe.wait_ge(taken if k % 2 == 0 else copied, (k - 4) // 2 + 1)
                    for b in range(TB):
                        t = pe.transpose(self.ps[:, 1 + k % 4, b * P:(b + 1) * P], self.x[:, k, b * P:(b + 1) * P], self.c("ident"))
                    t.then_inc(turned, 1)

            @block.vector
            def _(dve):
                dve.wait_ge(used, KC)
                dve.tensor_scalar(rs[:], self.ps[:, 0, :], 1.0 / D, EPS, ALU.mult, ALU.add).then_inc(mean, 1)
                dve.wait_ge(root, 1)
                dve.reciprocal(rs[:], rs[:]).then_inc(inverse, 1)
                dve.wait_ge(inverse, 1)
                for k in range(KC):
                    dve.scalar_tensor_tensor(self.x[:, k, :], self.x[:, k, :], self.p2("fin", k, 1), rs[:], ALU.mult, ALU.mult).then_inc(normed, 1)
                for k in range(1, KC, 2):
                    dve.wait_ge(turned, k + 1)
                    dve.tensor_copy(y[:, :, k * P:(k + 1) * P], self.ps[:, 1 + k % 4, :].rearrange("p (b f) -> p b f", b=TB)).then_inc(copied, 1)

            out_done = sem("out_done")

            @block.sync
            def _(sp):
                sp.wait_ge(taken, KC // 2)
                sp.wait_ge(copied, KC // 2)
                sp.dma_start(self.out.rearrange("o (b p) d -> p (o b) d", p=P), y[:]).then_inc(out_done, 16)
                sp.wait_ge(out_done, 16)

            @block.gpsimd
            def _(pool):
                pool.sem_clear(clear)

    def second(self):
        nc, W, ctx = self.nc, self.W, self.ctx
        sbuf = lambda st, n, s, **kw: st.enter_context(nc.sbuf_tensor(n, s, F32, **kw))
        self.par2 = sbuf(ctx, "par2", [P, PAR2_N])
        with ExitStack() as until_wo:
            self.dtgn = sbuf(until_wo, "dt_gates", [P, TB, SSM_HEADS + 3 * NH])
            self.vsvw = sbuf(until_wo, "v_tokens", [P, TB, 2 * NKV])
            self.trig = sbuf(until_wo, "trig", [P, 2, S], side="right")
            self.ada()

            def prologue(sp):
                for m in range(2):
                    for q in range(2):
                        W.issue(sp, B2 + m, q, self.tile2(m, q), first=m == 0)

            self.norm("norm1_2", None, lambda k: self.p2("g1", k, 1), shift=lambda k: self.p2("ada", k, 1), prologue=prologue, split0=B2)
            with ExitStack() as until_ssm:
                self.xs = sbuf(until_ssm, "xs", [P, 16, S])
                with ExitStack() as until_scan:
                    self.bc = sbuf(until_scan, "bc", [P, 8, S])
                    self.ssm_project()
                    self.ssd()
                self.merged = sbuf(until_wo, "merged2", [P, KC, S], side="right")
                self.ssm_gate()
                self.yn = self.parts(until_ssm, "yn", KC)
                self.ssm_norm()
                self.ssm_out()
            self.gate = sbuf(until_wo, "nsa_gate", [P, KC, S])
            with ExitStack() as until_attention:
                self.rp = sbuf(until_attention, "nsa_q_k", [P, 14, S])
                self.vc = sbuf(until_attention, "vc", [P, NG, S])
                self.nsa_project()
                self.nsa_rope()
                self.kcmp = sbuf(until_attention, "kcmp", [P, NG * NC])
                self.vcmp = sbuf(until_attention, "vcmp", [P, 4, NG, HD])
                self.strip = sbuf(until_attention, "causal_strip", [P, S])
                self.nsa_compress()
                self.pct = sbuf(until_attention, "cmp_probs", [P, 4, S])
                self.selneg = sbuf(until_attention, "selection", [P, NG * TB, NSEL])
                self.nsa_compressed()
                self.nsa_attention()
            self.m = self.parts(until_wo, "merged_two", KC)
            self.nsa_out()
            self.add_projection("w_o", B2 + P_WO, self.m, lambda sp: self.issue2(sp, P_WO, P_MOE), scale=lambda k: self.p2("ada", 2 * KC + k, 1))
        self.norm("norm2_2", None, lambda k: self.p2("g2", k, 1), shift=lambda k: self.p2("ada", 3 * KC + k, 1))
        self.comb = sbuf(ctx, "expert_weights", [P, TB, NE])
        self.route()
        self.moe()
        self.finish()


def program(nc, dram, out, const_at):
    with ExitStack() as ctx:
        k = Whole(nc, dram, out, const_at, ctx)
        k.load()
        with nc.Fori(0, DEPTH) as l:
            k.layer(l)
        k.until_first.close()
        k.second()


def kernel(**inputs):
    import concourse.bacc as bacc
    from concourse.bass_utils import run_bass_kernel_spmd

    nc = bacc.Bacc("TRN2", target_bir_lowering=False, num_devices=1)
    table, at = constants()
    arrays, dram = {}, {}
    for name, a in [*inputs.items(), ("const", table)]:
        a = np.ascontiguousarray(a)
        arrays[f"in_{name}"] = a
        dram[name] = nc.dram_tensor(f"in_{name}", a.shape, mybir.dt.from_np(a.dtype), kind="ExternalInput").ap()
    out = nc.dram_tensor("out_0", (1, S, D), F32, kind="ExternalOutput").ap()
    program(nc, dram, out, at)
    r = run_bass_kernel_spmd(nc, [arrays], core_ids=[0])
    return r.results[0]["out_0"]
```

```python
from contextlib import ExitStack

import numpy as np

import concourse.bass as bass
from concourse import mybir
from concourse.alu_op_type import AluOpType as ALU

F32 = mybir.dt.float32
F32R = mybir.dt.float32r
I32 = mybir.dt.int32
ACT = mybir.ActivationFunctionType
AX = mybir.AxisListType

P = 128
S, D = 512, 1024
TB, KC = S // P, D // P
HD = 64
DEPTH = 2
SBH = 8
SWH, SWKV = 8, 2
D_FF = 4 * D
EPS = 1e-6
NEG = -1e30
SBW = SBH * HD
SWQ, SWK = SWH * HD, SWKV * HD
COL = 256
C_SBV, C_SWQ, C_SWK, C_SWV, C_GATE = 2 * SBW, 3 * SBW, 3 * SBW + SWQ, 3 * SBW + SWQ + SWK, 3 * SBW + SWQ + 2 * SWK
STRIP = [S - P * b for b in range(TB)]
OFF = [sum(STRIP[:b]) for b in range(TB)]
PACK = sum(STRIP)
POFF = [0, 512, 1024, 1280]

FIRST_ONLY = ("band", "cos", "sin")


def constants():
    p = np.arange(P)[:, None]
    f = np.arange(P)[None, :]
    half = HD // 2
    c = {}
    c["ident"] = (p == f)
    c["ones"] = np.ones((P, P))
    c["suffix"] = (p >= f)
    c["prefix"] = (p <= f)
    c["strict"] = np.where(p < f, 0.0, NEG)
    c["causal_t"] = np.where(p <= f, 0.0, NEG)
    c["causal"] = np.where(f <= p, 0.0, NEG)
    c["slot"] = np.broadcast_to(f, (P, P))
    c["headsum"] = (p // HD == f // HD)
    rot = np.zeros((P, P))
    for m in range(P):
        h, i = divmod(m, HD)
        if i < half:
            rot[h * HD + i + half, m] = -1.0
        else:
            rot[h * HD + i - half, m] = 1.0
    c["rot"] = rot
    j = np.arange(2 * P)[None, :]
    rel = j - P - p
    band = np.where((rel <= 0) & (rel > -P), 0.0, NEG)
    first = np.where(j <= p, 0.0, NEG)
    c["band"] = np.concatenate([first, band, band, band], 1)
    inv = (1.0 / np.power(10000.0, (np.arange(0, HD, 2) / HD))).astype(np.float32)
    ang = np.arange(S, dtype=np.float32)[None, :] * inv[(np.arange(P) % half)][:, None]
    c["cos"] = np.cos(ang.astype(np.float64))
    c["sin"] = np.sin(ang.astype(np.float64))
    c["inv"] = inv[np.arange(P) % half][:, None]
    ncmp = (S - 32) // 16 + 1
    t = (np.arange(TB)[None, :, None] * P + np.arange(P)[:, None, None])
    ok = (16 * np.arange(ncmp) + 31)[None, None, :] <= t
    c["cmp_neg"] = np.where(ok, 0.0, NEG).reshape(P, -1)
    c["cmp_one"] = ok.astype(np.float64).reshape(P, -1)
    jb = np.arange(S // 64)[None, None, :]
    loc = t // 64
    c["prio"] = np.where(jb == loc, 1e6, np.where(jb > loc, NEG, np.where(jb == 0, 5e5, 0.0))).reshape(P, -1)
    k8 = np.arange(8)
    c["before"] = np.broadcast_to((k8[None, :] < k8[:, None]).reshape(1, 64), (P, 64))
    c["before4"] = np.broadcast_to((k8[None, :4] < k8[:4, None]).reshape(1, 16), (P, 16))
    c = {n: c[n] for n in sorted(c, key=lambda n: n in FIRST_ONLY)}
    at, n = {}, 0
    for name, a in c.items():
        at[name] = (n, a.shape[1])
        n += a.shape[1]
    return np.ascontiguousarray(np.concatenate([np.asarray(a, np.float32) for a in c.values()], 1)), at


class Stages:

    POOLS, SIZE = 3, 44

    def __init__(self, nc):
        self.nc, self.last = nc, -1
        ids = sorted(nc.free_semaphores)
        self.base = ids[-self.POOLS * self.SIZE]
        assert ids[-1] - self.base + 1 == self.POOLS * self.SIZE

    def open(self, name, ctx, skip=0):
        before, k = self.last, (self.last + 1 + skip) % self.POOLS
        self.last = k
        before %= self.POOLS
        ids = iter(range(self.base + k * self.SIZE, self.base + (k + 1) * self.SIZE))
        to_clear = range(self.base + before * self.SIZE, self.base + (before + 1) * self.SIZE)
        return (lambda what: ctx.enter_context(self.nc.semaphore(f"{name}_{what}", num=next(ids)))), to_clear


class Link:

    def __init__(self, eng, sem):
        self.eng, self.sem, self.n, self.i, self.per = eng, sem, 0, None, 0

    def __call__(self, ins):
        self.note(ins)
        self.wait()
        return ins

    def note(self, ins):
        ins.then_inc(self.sem, 1)
        self.n += 1

    def value(self):
        return self.n if self.i is None else self.n + self.i * self.per

    def wait(self):
        self.eng.wait_ge(self.sem, self.value())

    def loop(self, i, per):
        self.i, self.per, self.n0 = i, per, self.n

    def end(self, count):
        assert self.n - self.n0 == self.per, (self.n - self.n0, self.per)
        self.n = self.n0 + self.per * count
        self.i = None


class Weights:

    def __init__(self, nc, ctx):
        self.nc = nc
        sb = lambda n, dt: ctx.enter_context(nc.sbuf_tensor(n, [P, 2, KC, COL], dt))
        self.raw, self.hi, self.lo = sb("w_raw", F32), sb("w_hi", F32R), sb("w_lo", F32R)
        sem = lambda n: ctx.enter_context(nc.semaphore(n))
        self.raw_landed = [sem("raw_landed0"), sem("raw_landed1")]
        self.hi_ready, self.lo_ready = sem("hi_ready"), sem("lo_ready")
        self.tile_done = sem("tile_done")
        self.evicted = [sem("evicted0"), sem("evicted1")]

    def issue(self, sp, m, q, quarters, first=False):
        if not first:
            sp.wait_ge(self.lo_ready, 2 * m + q - 1)
        for dst, src in quarters:
            sp.dma_start(dst(self.raw[:, q]), src).then_inc(self.raw_landed[q], 16)

    def split_hi(self, act, m, q, first=False, cols=COL):
        act.wait_ge(self.raw_landed[q], 64 * m + 64)
        if not first:
            act.wait_ge(self.tile_done, 2 * m + q - 1)
        act.activation(self.hi[:, q, :, 0:cols], self.raw[:, q, :, 0:cols], ACT.Copy).then_inc(self.hi_ready, 1)

    def split_lo(self, dve, m, q, cols=COL):
        dve.wait_ge(self.hi_ready, 2 * m + q + 1)
        dve.tensor_tensor(self.lo[:, q, :, 0:cols], self.raw[:, q, :, 0:cols],
                          self.hi[:, q, :, 0:cols].bitcast(F32), ALU.subtract).then_inc(self.lo_ready, 1)

    def ready(self, pe, m, q, first=False):
        pe.wait_ge(self.lo_ready, 2 * m + q + 1)
        if not first:
            pe.wait_ge(self.evicted[q], m)

    def done(self, eng, m, q):
        eng.wait_ge(self.tile_done, 2 * m + q + 1)

    def read(self, eng, m, q):
        eng.wait_ge(self.evicted[q], m + 1)


def products(pe, out, w, x, start, stop):
    pe.matmul(out, w[0], x[0], start=start, stop=False)
    pe.matmul(out, w[0], x[1], start=False, stop=False)
    return pe.matmul(out, w[1], x[0], start=False, stop=stop)


def tile_columns(pe, W, m, q, ps, x, first=False, krange=range(KC), start=True, stop=True):
    W.ready(pe, m, q, first)
    for c in range(COL // P):
        for k in krange:
            mm = products(pe, ps[:, q, c], (W.hi[:, q, k, c * P:(c + 1) * P], W.lo[:, q, k, c * P:(c + 1) * P]),
                          (x[0][:, k - krange[0], :], x[1][:, k - krange[0], :]), k == krange[0], k == krange[-1])
    mm.then_inc(W.tile_done, 1)


def tile_tokens(pe, W, m, q, ps, x, n, first=False):
    W.ready(pe, m, q, first)
    for b in range(TB):
        out = ps[:, q].rearrange("p a b -> p (a b)")[:, b * COL:b * COL + n]
        for k in range(KC):
            mm = products(pe, out, (x[0][:, k, b * P:(b + 1) * P], x[1][:, k, b * P:(b + 1) * P]),
                          (W.hi[:, q, k, 0:n], W.lo[:, q, k, 0:n]), k == 0, k == KC - 1)
    mm.then_inc(W.tile_done, 1)


def quarters_of(src, n=COL, rows=KC):
    v = src.rearrange("(k p) n -> p k n", p=P)
    h = rows // 4
    return [(lambda t, a=a: t[:, a:a + h, 0:n], v[:, a:a + h, :]) for a in range(0, rows, h)]


class Kernel:
    def __init__(self, nc, dram, out, const_at, ctx):
        self.nc, self.d, self.out = nc, dram, out
        self.ctx = ctx
        self.stages = Stages(nc)
        self.W = Weights(nc, ctx)
        sb = self.sb
        self.cat = const_at
        self.n_const = min(const_at[n][0] for n in FIRST_ONLY)
        self.const = sb("const", [P, self.n_const])
        self.until_first = ctx.enter_context(ExitStack())
        self.const_first = self.until_first.enter_context(
            nc.sbuf_tensor("const_first", [P, dram["const"].shape[1] - self.n_const], F32, side="right"))
        self.x = sb("x", [P, KC, S])
        self.h = (sb("h_hi", [P, KC, S], F32R), sb("h_lo", [P, KC, S], F32R))
        self.ps = ctx.enter_context(nc.psum_tensor("ps", [P, 8, 512], F32))
        self.pst = self.ps[:].rearrange("p (q c) n -> p q c n", q=2)
        self.par = sb("par", [P, 96])

    def sb(self, name, shape, dt=F32):
        return self.ctx.enter_context(self.nc.sbuf_tensor(name, shape, dt))

    def c(self, name):
        a, n = self.cat[name]
        if name in FIRST_ONLY:
            return self.const_first[:, a - self.n_const:a - self.n_const + n]
        return self.const[:, a:a + n]

    def flat(self, a, n):
        return self.ps[:].rearrange("p b n -> p (b n)")[:, a * 512:a * 512 + n]


class Norm:

    def __init__(self, k, name, sem, st, gain, shift=None, prologue=None, split0=None, rows=None, to=None):
        self.k, self.gain, self.shift, self.prologue, self.split0, self.rows, self.to = k, gain, shift, prologue, split0, rows, to
        self.loaded, self.squared, self.low, self.root = sem("n_loaded"), sem("n_squared"), sem("n_low"), sem("n_root")
        self.steps, self.normed, self.rounded, self.used = sem("n_steps"), sem("n_normed"), sem("n_rounded"), sem("n_used")
        self.shifted, self.turned, self.params = sem("n_shifted"), sem("n_turned"), sem("n_params")
        sb = lambda n, s: st.enter_context(k.nc.sbuf_tensor(f"{name}_{n}", s, F32))
        self.sq, self.rs, self.tmp = sb("sq", [P, 2, S]), sb("rs", [P, S]), sb("tmp", [P, 2, S])
        if rows:
            self.staged = sb("rows", [32, P])
        self.bank = k.ps[:, 7, :]

    def sync(self, sp):
        if self.rows:
            for dst, src in self.rows(self.staged):
                sp.dma_start(dst, src).then_inc(self.loaded, 16)
        if self.prologue:
            self.prologue(sp)

    def scalar(self, act):
        k_, W, (h_hi, _) = self.k, self.k.W, self.k.h
        for k in range(KC):
            if k >= 2:
                act.wait_ge(self.used, k - 1)
            act.activation(self.sq[:, k % 2], k_.x[:, k, :], ACT.Square).then_inc(self.squared, 1)
        if self.split0 is not None:
            for q in range(2):
                W.split_hi(act, self.split0, q, first=True)
        act.wait_ge(self.steps, 1)
        act.activation(self.rs[:], self.rs[:], ACT.Sqrt).then_inc(self.root, 1)
        for k in range(KC):
            act.wait_ge(self.normed, k + 1)
            act.activation(h_hi[:, k, :], self.tmp[:, k % 2], ACT.Copy).then_inc(self.rounded, 1)

    def tensor(self, pe):
        if self.rows:
            pe.wait_ge(self.loaded, 16 * len(self.rows(self.staged)))
            pe.transpose(self.k.ps[:, 6, 0:32], self.staged[:], self.k.c("ident")[0:32, 0:32]).then_inc(self.turned, 1)
        for k in range(KC):
            pe.wait_ge(self.squared, k + 1)
            mm = pe.matmul(self.bank, self.k.c("ones"), self.sq[:, k % 2], start=k == 0, stop=k == KC - 1)
            mm.then_inc(self.used, 1)

    def vector(self, dve):
        k_, W, (h_hi, h_lo), tmp, rs = self.k, self.k.W, self.k.h, self.tmp, self.rs
        if self.rows:
            dve.wait_ge(self.turned, 1)
            dve.tensor_copy(self.to, k_.ps[:, 6, 0:self.to.shape[1]]).then_inc(self.params, 1)
        if self.split0 is not None:
            for q in range(2):
                W.split_lo(dve, self.split0, q)
        dve.wait_ge(self.used, KC)
        dve.tensor_scalar(rs[:], self.bank, 1.0 / D, EPS, ALU.mult, ALU.add).then_inc(self.steps, 1)
        dve.wait_ge(self.root, 1)
        dve.reciprocal(rs[:], rs[:]).then_inc(self.steps, 1)
        dve.wait_ge(self.steps, 2)
        if self.rows:
            dve.wait_ge(self.params, 1)

        def scale(k):
            if k >= 2:
                dve.wait_ge(self.low, k - 1)
            e = dve.scalar_tensor_tensor(tmp[:, k % 2], k_.x[:, k, :], self.gain(k), rs[:], ALU.mult, ALU.mult)
            if self.shift is not None:
                e.then_inc(self.shifted, 1)
                dve.wait_ge(self.shifted, k + 1)
                e = dve.tensor_scalar(tmp[:, k % 2], tmp[:, k % 2], self.shift(k), None, ALU.add)
            e.then_inc(self.normed, 1)

        scale(0)
        for k in range(KC):
            if k + 1 < KC:
                scale(k + 1)
            dve.wait_ge(self.rounded, k + 1)
            dve.tensor_tensor(h_lo[:, k, :], tmp[:, k % 2], h_hi[:, k, :].bitcast(F32), ALU.subtract).then_inc(self.low, 1)

    def chunk(self, pe, k):
        pe.wait_ge(self.low, k + 1)

    def first_pair(self, pe, m, first):
        W, pst, h = self.k.W, self.k.pst, self.k.h
        for q in range(2):
            W.ready(pe, m, q, first)
        for k in range(KC):
            self.chunk(pe, k)
            for q in range(2):
                for c in range(COL // P):
                    cols = slice(c * P, (c + 1) * P)
                    mm = products(pe, pst[:, q, c], (W.hi[:, q, k, cols], W.lo[:, q, k, cols]), (h[0][:, k, :], h[1][:, k, :]), k == 0, k == KC - 1)
                if k == KC - 1:
                    mm.then_inc(W.tile_done, 1)


PAIR_QK, PAIR_SBV, PAIR_SWQ, PAIR_SWKV, PAIR_GATE, PAIR_OUT, PAIR_MLP, PAIRS = 0, 2, 3, 4, 5, 11, 13, 29
QUARTERS = D_FF // D
ADA_PER = 6 * D // COL // DEPTH // QUARTERS


class FirstBlock(Kernel):

    def row(self, name, l):
        return self.d[name][bass.ds(l, 1)]

    def layer_tile(self, l, m, q):
        w_in = self.row("w_in", l).rearrange("o k n -> (o k) n")
        t = 2 * m + q
        if m < PAIR_SBV:
            return quarters_of(w_in[:, t * COL:(t + 1) * COL])
        if m < PAIR_SWQ:
            t -= 2 * PAIR_SBV
            return quarters_of(w_in[:, C_SBV + t * COL:C_SBV + (t + 1) * COL])
        if m < PAIR_SWKV:
            t -= 2 * PAIR_SWQ
            return quarters_of(w_in[:, C_SWQ + t * COL:C_SWQ + (t + 1) * COL])
        if m < PAIR_GATE and q == 0:
            return self.twice(w_in, C_SWK)
        if m < PAIR_GATE:
            return quarters_of(w_in[:, C_SWV:C_SWV + SWK], SWK)
        if m < PAIR_OUT:
            p, kind = divmod(t - 2 * PAIR_GATE, 3)
            if kind < 2:
                a = C_GATE + kind * D + p * COL
                return quarters_of(w_in[:, a:a + COL])
            half = KC // 2
            sides = [self.row(n, l).rearrange("o k n -> (o k) n")[:, p * COL:(p + 1) * COL].rearrange("(k p) n -> p k n", p=P)
                     for n in ("w_branch_sb", "w_branch_swa")]
            return [(lambda t, a=half * i + 2 * j: t[:, a:a + 2, :], side[:, 2 * j:2 * j + 2, :])
                    for i, side in enumerate(sides) for j in range(2)]
        t -= 2 * PAIR_OUT
        return quarters_of(self.row("w_out", l).rearrange("o k n -> (o k) n")[:, t * COL:(t + 1) * COL])

    def twice(self, w, at):
        out = []
        for j in range(2):
            src = w[:, at + j * HD:at + (j + 1) * HD].rearrange("(k p) n -> p k n", p=P)
            for r in range(2):
                a = (2 * j + r) * HD
                out.append((lambda t, a=a: t[:, :, a:a + HD], src))
        return out

    def up_tile(self, l, j, q):
        w = self.row("w_up", l).rearrange("o k n -> (o k) n")
        return quarters_of(w[:, bass.ds(j * D + q * COL, COL)])

    def down_tile(self, l, j, q):
        w = self.row("w_down", l).rearrange("o k n -> (o k) n")
        return quarters_of(w[bass.ds(j * D, D), q * COL:(q + 1) * COL])

    def layer_rows(self, l):
        vec = lambda n: self.row(n, l).rearrange("o (k p) -> (o k) p", p=P)
        return lambda rows: [(rows[0:KC, :], vec("mix_norm_g")), (rows[KC:2 * KC, :], vec("mlp_norm_g"))] + [
            (rows[at:at + 1, r * HD:(r + 1) * HD], self.row(n, l)) for at, n in ((16, "q_norm_g"), (17, "k_norm_g")) for r in range(2)]

    def layer(self, l):
        W = self.W
        base = l * PAIRS
        self.l, self.base = l, base

        def prologue(sp):
            for m in range(2):
                for q in range(2):
                    W.issue(sp, base + m, q, self.layer_tile(l, m, q), first=m == 0)

        with ExitStack() as until_merged:
            self.o_sb = self.parts(until_merged, "o_sb", 4)
            with ExitStack() as until_swa:
                right = lambda n, s: until_swa.enter_context(self.nc.sbuf_tensor(n, s, F32, side="right"))
                self.swq = right("swq", [P, 6, S])
                self.swv = right("swv", [P, TB, SWK])
                with ExitStack() as until_sb:
                    self.qk = until_sb.enter_context(self.nc.sbuf_tensor("qk", [P, 8, S], F32))
                    self.v = until_sb.enter_context(self.nc.sbuf_tensor("v", [P, TB, SBW], F32))
                    self.project(prologue)
                    self.stick_breaking()
                self.swa_prepare()
                self.o_sw = self.parts(until_merged, "o_sw", 4)
                self.swa()
            self.m = self.parts(until_merged, "merged", KC)
            self.merge()
            self.out_projection()
        self.mlp()

    def parts(self, ctx, name, n):
        sb = lambda nm: ctx.enter_context(self.nc.sbuf_tensor(nm, [P, n, S], F32R))
        return sb(f"{name}_hi"), sb(f"{name}_lo")

    def project(self, prologue):
        nc, W, l, base = self.nc, self.W, self.l, self.base
        with ExitStack() as st:
            sem, clear = self.stages.open("project", st)
            sunk = sem("sunk")
            norm = Norm(self, "norm1", sem, st, lambda k: self.par[:, k:k + 1], prologue=prologue, split0=base,
                        rows=self.layer_rows(l), to=self.par[:, 0:18])
            block = st.enter_context(nc.Block())
            last = PAIR_GATE

            @block.sync
            def _(sp):
                norm.sync(sp)
                sp.dma_start(self.par[:, 18:26], self.row("sinks", l).to_broadcast([P, SWH])).then_inc(sunk, 16)
                for m in range(2, last + 2):
                    for q in range(2):
                        W.issue(sp, base + m, q, self.layer_tile(l, m, q))
                sp.wait_ge(sunk, 16)

            @block.tensor
            def _(pe):
                norm.tensor(pe)
                norm.first_pair(pe, base, True)
                for m in range(1, last):
                    for q in range(2):
                        if PAIR_SBV <= m < PAIR_SWQ:
                            tile_tokens(pe, W, base + m, q, self.pst, self.h, COL)
                        elif m == PAIR_SWKV and q == 1:
                            tile_tokens(pe, W, base + m, q, self.pst, self.h, SWK)
                        else:
                            tile_columns(pe, W, base + m, q, self.pst, self.h)

            @block.scalar
            def _(act):
                norm.scalar(act)
                for m in range(last):
                    for q in range(2):
                        t = 2 * m + q
                        W.done(act, base + m, q)
                        pair = self.pst[:, q, 0:2, :]
                        tokens = self.pst[:, q].rearrange("p a b -> p (a b)")[:, 0:TB * COL].rearrange("p (b n) -> p b n", b=TB)
                        if m < PAIR_SBV // 2:
                            e = act.mul(self.qk[:, 2 * t:2 * t + 2, :], pair, HD ** -0.5)
                        elif m < PAIR_SBV:
                            e = act.activation(self.qk[:, 2 * t:2 * t + 2, :], pair, ACT.Copy)
                        elif m < PAIR_SWQ:
                            e = act.activation(self.v[:, :, q * COL:(q + 1) * COL], tokens, ACT.Copy)
                        elif m < PAIR_SWKV:
                            e = act.activation(self.swq[:, 2 * q:2 * q + 2, :], pair, ACT.Copy)
                        elif q == 0:
                            e = act.activation(self.swq[:, 4:6, :], pair, ACT.Copy)
                        else:
                            e = act.activation(self.swv[:], tokens[:, :, 0:SWK], ACT.Copy)
                        e.then_inc(W.evicted[q], 1)
                        W.split_hi(act, base + m + 1, q, cols=SWK if m + 1 == PAIR_SWKV and q == 1 else COL)

            @block.vector
            def _(dve):
                norm.vector(dve)
                for m in range(last):
                    for q in range(2):
                        W.split_lo(dve, base + m + 1, q, cols=SWK if m + 1 == PAIR_SWKV and q == 1 else COL)

            @block.gpsimd
            def _(pool):
                pool.sem_clear(clear)

    def stick_breaking(self):
        nc = self.nc
        with ExitStack() as st:
            sem, clear = self.stages.open("sb", st)
            z_ready, z_taken, r_ready, r_taken = sem("z_ready"), sem("z_taken"), sem("r_ready"), sem("r_taken")
            expd, logd, absd, sp_ready, arg_ready, w_ready = (sem(n) for n in ("expd", "logd", "absd", "sp_ready", "arg_ready", "w_ready"))
            o_ready, o_hi, o_lo, w_used, masked = (sem(n) for n in ("o_ready", "o_hi", "o_lo", "w_used", "masked"))
            sb = lambda n, s: st.enter_context(nc.sbuf_tensor(n, s, F32))
            z, sp_, w = sb("sb_z", [P, 2, PACK]), sb("sb_softplus", [P, 2, PACK]), sb("sb_w", [P, 2, PACK])
            mask = sb("sb_mask", [P, PACK])
            z_ps, r_ps = self.flat(0, 1408), self.flat(3, 1408)
            parts = [(0, 896, 0), (896, PACK, 1024)]
            block = st.enter_context(nc.Block())

            def rows(h):
                return slice(HD * (h % 2), HD * (h % 2) + HD)

            @block.tensor
            def _(pe):
                def scores(h):
                    if h >= 1:
                        pe.wait_ge(z_taken, 2 * h)
                    for b in range(TB):
                        mm = pe.matmul(z_ps[:, POFF[b]:POFF[b] + STRIP[b]], self.qk[rows(h), 4 + h // 2, b * P:(b + 1) * P],
                                       self.qk[rows(h), h // 2, b * P:S], start=True, stop=True)
                    mm.then_inc(z_ready, 1)

                def suffix_sums(h):
                    pe.wait_ge(sp_ready, h + 1)
                    if h >= 1:
                        pe.wait_ge(r_taken, 2 * h)
                    for b in range(TB):
                        for j in range(b, TB):
                            a = POFF[b] + P * (j - b)
                            mm = pe.matmul(r_ps[:, a:a + STRIP[j]], self.c("suffix") if j == b else self.c("ones"),
                                           sp_[:, h % 2, OFF[j]:OFF[j] + STRIP[j]], start=j == b, stop=j == TB - 1)
                    mm.then_inc(r_ready, 1)

                def values(h):
                    pe.wait_ge(w_ready, h + 1)
                    if h >= 4:
                        pe.wait_ge(o_lo, h // 2 - 1)
                    for b in range(TB):
                        mm = pe.matmul(self.ps[rows(h), 6 + (h // 2) % 2, b * P:S], self.v[:, b, h * HD:(h + 1) * HD],
                                       w[:, h % 2, OFF[b]:OFF[b] + STRIP[b]], start=b == 0, stop=b == TB - 1)
                    mm.then_inc(o_ready, 1)

                scores(0)
                for h in range(SBH):
                    if h + 1 < SBH:
                        scores(h + 1)
                    if h >= 1:
                        values(h - 1)
                    suffix_sums(h)
                values(SBH - 1)

            @block.vector
            def _(dve):
                dve.wait_ge(masked, 1 + TB)

                def softplus(h):
                    dve.wait_ge(z_ready, h + 1)
                    if h >= 2:
                        dve.wait_ge(w_ready, h - 1)
                        dve.wait_ge(o_ready, h - 1)
                    for a, b, p in parts:
                        dve.tensor_tensor(z[:, h % 2, a:b], z_ps[:, p:p + b - a], mask[:, a:b], ALU.add).then_inc(z_taken, 1)
                    dve.wait_ge(z_taken, 2 * h + 2)
                    dve.scalar_tensor_tensor(w[:, h % 2], z[:, h % 2], -1.0, z[:, h % 2], ALU.mult, ALU.min).then_inc(absd, 1)
                    dve.wait_ge(logd, h + 1)
                    if h >= 2:
                        dve.wait_ge(r_ready, h - 1)
                    dve.scalar_tensor_tensor(sp_[:, h % 2], z[:, h % 2], 0.0, w[:, h % 2], ALU.max, ALU.add).then_inc(sp_ready, 1)

                def exponent(h):
                    dve.wait_ge(r_ready, h + 1)
                    dve.wait_ge(sp_ready, h + 1)
                    for a, b, p in parts:
                        dve.tensor_tensor(w[:, h % 2, a:b], z[:, h % 2, a:b], r_ps[:, p:p + b - a], ALU.subtract).then_inc(r_taken, 1)

                def out_low(c):
                    dve.wait_ge(o_hi, c + 1)
                    dve.tensor_tensor(self.o_sb[1][:, c, :], self.ps[:, 6 + c % 2, :], self.o_sb[0][:, c, :].bitcast(F32),
                                      ALU.subtract).then_inc(o_lo, 1)

                softplus(0)
                for h in range(SBH):
                    if h + 1 < SBH:
                        softplus(h + 1)
                    exponent(h)
                    if h >= 2 and h % 2 == 0:
                        out_low(h // 2 - 1)
                out_low(SBH // 2 - 1)

            @block.scalar
            def _(act):
                def logs(h):
                    act.wait_ge(absd, h + 1)
                    act.activation(w[:, h % 2], w[:, h % 2], ACT.Exp).then_inc(expd, 1)
                    act.wait_ge(expd, h + 1)
                    act.activation(w[:, h % 2], w[:, h % 2], ACT.Ln, bias=1.0).then_inc(logd, 1)

                def weights(h):
                    act.wait_ge(r_taken, 2 * h + 2)
                    act.activation(w[:, h % 2], w[:, h % 2], ACT.Exp).then_inc(w_ready, 1)

                def out_high(c):
                    act.wait_ge(o_ready, 2 * c + 2)
                    act.activation(self.o_sb[0][:, c, :], self.ps[:, 6 + c % 2, :], ACT.Copy).then_inc(o_hi, 1)

                logs(0)
                for h in range(SBH):
                    if h + 1 < SBH:
                        logs(h + 1)
                    weights(h)
                    if h >= 2 and h % 2 == 0:
                        out_high(h // 2 - 1)
                out_high(SBH // 2 - 1)

            @block.gpsimd
            def _(pool):
                pool.sem_clear(clear)
                pool.memset(mask[:], 0.0).then_inc(masked, 1)
                pool.wait_ge(masked, 1)
                for b in range(TB):
                    pool.tensor_copy(mask[:, OFF[b]:OFF[b] + P], self.c("strict")).then_inc(masked, 1)

    def swa_prepare(self):
        nc, n = self.nc, 6
        with ExitStack() as st:
            sem, clear = self.stages.open("swa_prepare", st)
            squared, summed, mean, root, inverse, normed, turned, cosd, sind, done, scaled = (sem(x) for x in (
                "squared", "summed", "mean", "root", "inverse", "normed", "turned", "cosd", "sind", "done", "scaled"))
            sb = lambda nm, s: st.enter_context(nc.sbuf_tensor(nm, s, F32))
            sq, rs, tc, ts = sb("swa_sq", [P, n, S]), sb("swa_rs", [P, n, S]), sb("swa_cos", [P, 2, S]), sb("swa_sin", [P, 2, S])
            gq = sb("swa_gain", [P, 1])
            x = self.swq
            block = st.enter_context(nc.Block())

            @block.scalar
            def _(act):
                act.mul(gq[:], self.par[:, 16:17], HD ** -0.5).then_inc(scaled, 1)
                for c in range(n):
                    act.activation(sq[:, c, :], x[:, c, :], ACT.Square).then_inc(squared, 1)
                for c in range(n):
                    act.wait_ge(mean, c + 1)
                    act.activation(rs[:, c, :], rs[:, c, :], ACT.Sqrt).then_inc(root, 1)

            @block.tensor
            def _(pe):
                for c in range(n):
                    pe.wait_ge(squared, c + 1)
                    pe.matmul(self.ps[:, c, :], self.c("headsum"), sq[:, c, :], start=True, stop=True).then_inc(summed, 1)
                for c in range(n):
                    pe.wait_ge(normed, c + 1)
                    pe.matmul(self.ps[:, c, :], self.c("rot"), x[:, c, :], start=True, stop=True).then_inc(turned, 1)

            @block.vector
            def _(dve):
                for c in range(n):
                    dve.wait_ge(summed, c + 1)
                    dve.tensor_scalar(rs[:, c, :], self.ps[:, c, :], 1.0 / HD, EPS, ALU.mult, ALU.add).then_inc(mean, 1)
                dve.wait_ge(scaled, 1)
                for c in range(n):
                    dve.wait_ge(root, c + 1)
                    dve.reciprocal(rs[:, c, :], rs[:, c, :]).then_inc(inverse, 1)
                    dve.wait_ge(inverse, c + 1)
                    g = gq[:] if c < 4 else self.par[:, 17:18]
                    dve.scalar_tensor_tensor(x[:, c, :], x[:, c, :], g, rs[:, c, :], ALU.mult, ALU.mult).then_inc(normed, 1)
                for c in range(n):
                    dve.wait_ge(turned, c + 1)
                    if c >= 2:
                        dve.wait_ge(done, c - 1)
                    dve.tensor_tensor(tc[:, c % 2], x[:, c, :], self.c("cos"), ALU.mult).then_inc(cosd, 1)
                    dve.tensor_tensor(ts[:, c % 2], self.ps[:, c, :], self.c("sin"), ALU.mult).then_inc(sind, 1)
                    dve.wait_ge(cosd, c + 1)
                    dve.wait_ge(sind, c + 1)
                    dve.tensor_tensor(x[:, c, :], tc[:, c % 2], ts[:, c % 2], ALU.add).then_inc(done, 1)

            @block.gpsimd
            def _(pool):
                pool.sem_clear(clear)

    def swa(self):
        nc = self.nc
        BAND = 2 * P
        turns = [(b, j) for b in range(TB) for j in range(2) if b > 0 or j == 0]
        with ExitStack() as st:
            sem, clear = self.stages.open("swa", st)
            s_ready, s_taken, maxed, negd, expd, sunk, added, inverse, p_ready, turned, t_taken, o_ready, o_hi, o_lo = (sem(x) for x in (
                "s_ready", "s_taken", "maxed", "negd", "expd", "sunk", "added", "inverse", "p_ready", "turned", "t_taken",
                "o_ready", "o_hi", "o_lo"))
            sb = lambda nm, s: st.enter_context(nc.sbuf_tensor(nm, s, F32))
            p, pt = sb("swa_p", [P, 2, TB, BAND]), sb("swa_pt", [P, 2, len(turns) * P])
            mx, neg, den, sink, inv = (sb(f"swa_{x}", [P, 2, TB]) for x in ("mx", "neg", "den", "sink", "inv"))
            block = st.enter_context(nc.Block())
            rows = lambda h: slice(HD * (h % 2), HD * (h % 2) + HD)
            key0 = lambda b: max(b - 1, 0) * P
            s_ps = lambda h: self.flat(2 * (h % 2), TB * BAND)
            t_ps = self.flat(4, len(turns) * P)

            @block.tensor
            def _(pe):
                def scores(h):
                    if h >= 2:
                        pe.wait_ge(s_taken, h - 1)
                    for b in range(TB):
                        mm = pe.matmul(s_ps(h)[:, b * BAND:(b + 1) * BAND], self.swq[rows(h), h // 2, b * P:(b + 1) * P],
                                       self.swq[rows(h), 4 + h // 4, key0(b):key0(b) + BAND], start=True, stop=True)
                    mm.then_inc(s_ready, 1)

                def turn(h):
                    pe.wait_ge(p_ready, h + 1)
                    if h >= 1:
                        pe.wait_ge(t_taken, h)
                    for n, (b, j) in enumerate(turns):
                        mm = pe.transpose(t_ps[:, n * P:(n + 1) * P], p[:, h % 2, b, j * P:(j + 1) * P], self.c("ident"))
                    mm.then_inc(turned, 1)

                def values(h):
                    pe.wait_ge(t_taken, h + 1)
                    if h >= 4:
                        pe.wait_ge(o_lo, h // 2 - 1)
                    for n, (b, j) in enumerate(turns):
                        mm = pe.matmul(self.ps[rows(h), 6 + (h // 2) % 2, b * P:(b + 1) * P],
                                       self.swv[:, key0(b) // P + j, (h // 4) * HD:(h // 4 + 1) * HD],
                                       pt[:, h % 2, n * P:(n + 1) * P], start=j == 0, stop=j == 1 or b == 0)
                    mm.then_inc(o_ready, 1)

                scores(0)
                for h in range(SWH):
                    if h + 1 < SWH:
                        scores(h + 1)
                    if h >= 1:
                        values(h - 1)
                    turn(h)
                values(SWH - 1)

            @block.vector
            def _(dve):
                def softmax_head(h):
                    i = h % 2
                    dve.wait_ge(s_ready, h + 1)
                    if h >= 2:
                        dve.wait_ge(turned, h - 1)
                    flat = p[:, i].rearrange("p b n -> p (b n)")
                    dve.tensor_tensor(flat, s_ps(h), self.c("band"), ALU.add).then_inc(s_taken, 1)
                    dve.wait_ge(s_taken, h + 1)
                    dve.tensor_reduce(mx[:, i], p[:, i], AX.X, ALU.max).then_inc(maxed, 1)
                    dve.wait_ge(maxed, h + 1)
                    dve.tensor_scalar(neg[:, i], mx[:, i], self.par[:, 18 + h:19 + h], -1.0, ALU.max, ALU.mult).then_inc(negd, 1)

                def normalise(h):
                    i = h % 2
                    dve.wait_ge(expd, TB * (h + 1))
                    dve.wait_ge(sunk, h + 1)
                    dve.tensor_tensor(den[:, i], den[:, i], sink[:, i], ALU.add).then_inc(added, 1)
                    dve.wait_ge(added, h + 1)
                    dve.reciprocal(inv[:, i], den[:, i]).then_inc(inverse, 1)
                    dve.wait_ge(inverse, h + 1)
                    dve.tensor_tensor(p[:, i], p[:, i], inv[:, i].unsqueeze(2).to_broadcast([P, TB, BAND]), ALU.mult).then_inc(p_ready, 1)

                def out_low(c):
                    dve.wait_ge(o_hi, c + 1)
                    dve.tensor_tensor(self.o_sw[1][:, c, :], self.ps[:, 6 + c % 2, :], self.o_sw[0][:, c, :].bitcast(F32),
                                      ALU.subtract).then_inc(o_lo, 1)

                softmax_head(0)
                for h in range(SWH):
                    if h + 1 < SWH:
                        softmax_head(h + 1)
                    normalise(h)
                    if h >= 3 and h % 2 == 1:
                        out_low(h // 2 - 1)
                out_low(SWH // 2 - 1)

            @block.scalar
            def _(act):
                def exps(h):
                    i = h % 2
                    act.wait_ge(negd, h + 1)
                    for b in range(TB):
                        act.activation(p[:, i, b], p[:, i, b], ACT.Exp, bias=neg[:, i, b:b + 1],
                                       accum_out=den[:, i, b:b + 1]).then_inc(expd, 1)
                    act.activation(sink[:, i], neg[:, i], ACT.Exp, bias=self.par[:, 18 + h:19 + h]).then_inc(sunk, 1)

                def evict(h):
                    act.wait_ge(turned, h + 1)
                    if h >= 2:
                        act.wait_ge(o_ready, h - 1)
                    act.activation(pt[:, h % 2], t_ps, ACT.Copy).then_inc(t_taken, 1)

                def out_high(c):
                    act.wait_ge(o_ready, 2 * c + 2)
                    act.activation(self.o_sw[0][:, c, :], self.ps[:, 6 + c % 2, :], ACT.Copy).then_inc(o_hi, 1)

                exps(0)
                for h in range(SWH):
                    if h + 1 < SWH:
                        exps(h + 1)
                    evict(h)
                    if h >= 3 and h % 2 == 1:
                        out_high(h // 2 - 1)
                out_high(SWH // 2 - 1)

            @block.gpsimd
            def _(pool):
                pool.sem_clear(clear)

    def merge(self):
        nc, W, l, base = self.nc, self.W, self.l, self.base
        n = COL // P
        with ExitStack() as st:
            sem, clear = self.stages.open("merge", st)
            first, summed, rounded, low = (sem(x) for x in ("first", "summed", "rounded", "low"))
            sb = lambda nm, s: st.enter_context(nc.sbuf_tensor(nm, s, F32))
            gate, y = sb("merge_gate", [P, 2, n, S]), sb("merge_y", [P, 2, n, S])
            tiles = [(m, q, *divmod(2 * (m - PAIR_GATE) + q, 3)) for m in range(PAIR_GATE, PAIR_OUT) for q in range(2)]
            block = st.enter_context(nc.Block())

            @block.sync
            def _(sp):
                for m in range(PAIR_GATE + 2, PAIR_OUT + 2):
                    for q in range(2):
                        W.issue(sp, base + m, q, self.layer_tile(l, m, q))

            @block.tensor
            def _(pe):
                for m, q, p, kind in tiles:
                    if kind < 2:
                        tile_columns(pe, W, base + m, q, self.pst, self.h)
                        continue
                    W.ready(pe, base + m, q)
                    for side, o in ((0, self.o_sb), (1, self.o_sw)):
                        for c in range(n):
                            for k in range(4):
                                cols = slice(c * P, (c + 1) * P)
                                mm = products(pe, self.pst[:, q, 2 * side + c],
                                              (W.hi[:, q, 4 * side + k, cols], W.lo[:, q, 4 * side + k, cols]),
                                              (o[0][:, k, :], o[1][:, k, :]), k == 0, k == 3)
                    mm.then_inc(W.tile_done, 1)

            @block.scalar
            def _(act):
                for m, q, p, kind in tiles:
                    if kind < 2:
                        W.done(act, base + m, q)
                        if p >= 1:
                            act.wait_ge(summed, p)
                        act.activation(gate[:, kind], self.pst[:, q, 0:n, :], ACT.Sigmoid).then_inc(W.evicted[q], 1)
                    W.split_hi(act, base + m + 1, q)
                    if kind == 2:
                        act.wait_ge(summed, p + 1)
                        act.activation(self.m[0][:, n * p:n * p + n, :], y[:, 0], ACT.Copy).then_inc(rounded, 1)

            @block.vector
            def _(dve):
                for m, q, p, kind in tiles:
                    if kind == 2:
                        W.done(dve, base + m, q)
                        for tile in (2 * m + q - 2, 2 * m + q - 1):
                            W.read(dve, base + tile // 2, tile % 2)
                        if p >= 1:
                            dve.wait_ge(low, p)
                        dve.tensor_tensor(y[:, 0], self.pst[:, q, 0:n, :], gate[:, 0], ALU.mult).then_inc(first, 1)
                        dve.tensor_tensor(y[:, 1], self.pst[:, q, n:2 * n, :], gate[:, 1], ALU.mult).then_inc(W.evicted[q], 1)
                        dve.wait_ge(first, p + 1)
                        W.read(dve, base + m, q)
                        dve.tensor_tensor(y[:, 0], y[:, 0], y[:, 1], ALU.add).then_inc(summed, 1)
                    W.split_lo(dve, base + m + 1, q)
                    if kind == 2:
                        dve.wait_ge(rounded, p + 1)
                        dve.tensor_tensor(self.m[1][:, n * p:n * p + n, :], y[:, 0], self.m[0][:, n * p:n * p + n, :].bitcast(F32),
                                          ALU.subtract).then_inc(low, 1)

            @block.gpsimd
            def _(pool):
                pool.sem_clear(clear)

    def out_projection(self):
        l = self.l

        def issue(sp):
            for q in range(4):
                self.W.issue(sp, self.base + PAIR_MLP + q // 2, q % 2, self.up_tile(l, 0, q))

        self.add_projection("out", self.base + PAIR_OUT, self.m, issue, skip=1)

    def add_projection(self, name, m0, x_in, issue, scale=None, skip=0):
        nc, W, n = self.nc, self.W, COL // P
        with ExitStack() as st:
            sem, clear = self.stages.open(name, st, skip)
            block = st.enter_context(nc.Block())

            @block.sync
            def _(sp):
                issue(sp)

            @block.tensor
            def _(pe):
                for t in range(4):
                    tile_columns(pe, W, m0 + t // 2, t % 2, self.pst, x_in)

            @block.scalar
            def _(act):
                for t in range(4):
                    W.split_hi(act, m0 + 1 + t // 2, t % 2)

            @block.vector
            def _(dve):
                for t in range(4):
                    W.done(dve, m0 + t // 2, t % 2)
                    for c in range(n):
                        k = n * t + c
                        if scale is None:
                            e = dve.tensor_tensor(self.x[:, k, :], self.x[:, k, :], self.pst[:, t % 2, c], ALU.add)
                        else:
                            e = dve.scalar_tensor_tensor(self.x[:, k, :], self.pst[:, t % 2, c], scale(k), self.x[:, k, :], ALU.mult, ALU.add)
                    e.then_inc(W.evicted[t % 2], 1)
                    W.split_lo(dve, m0 + 1 + t // 2, t % 2)

            @block.gpsimd
            def _(pool):
                pool.sem_clear(clear)

    def mlp(self):
        nc, W, l, base, n = self.nc, self.W, self.l, self.base, COL // P
        with ExitStack() as st:
            sem, clear = self.stages.open("mlp", st, 1)
            relud, squared, rounded, low, added = (sem(x) for x in ("relud", "squared", "rounded", "low", "added"))
            norm = Norm(self, "norm2", sem, st, lambda k: self.par[:, KC + k:KC + k + 1])
            r = st.enter_context(nc.sbuf_tensor("mlp_relu", [P, 2, n, S], F32))
            u = self.parts(st, "mlp_u", KC)
            ada_landed = [sem(f"ada_landed{i}") for i in range(ADA_PER)]
            ada_step, ada_part, ada_done = sem("ada_step"), sem("ada_part"), sem("ada_done")
            ada_w = st.enter_context(nc.sbuf_tensor("ada_w", [P, ADA_PER, KC, COL], F32))
            ada_acc = st.enter_context(nc.sbuf_tensor("ada_acc", [P, ADA_PER, COL], F32))
            ada_ps = self.ps[:, 2, :]
            block = st.enter_context(nc.Block())
            pairs = PAIRS - PAIR_MLP
            m0 = base + PAIR_MLP
            per = 4

            @block.sync
            def _(sp):
                w_ada = self.d["w_ada_2"].rearrange("o k n -> (o k) n")

                def ada(j, first):
                    for i in range(ADA_PER):
                        if not first:
                            sp.wait_ge(ada_part, ADA_PER * (j - 1) + i + 1)
                        at = (l * QUARTERS + j) * (ADA_PER * COL) + i * COL
                        for dst, src in quarters_of(w_ada[:, bass.ds(at, COL)]):
                            sp.dma_start(dst(ada_w[:, i]), src).then_inc(ada_landed[i], 16)

                def down(j):
                    for t in range(4):
                        W.issue(sp, m0 + per * j + 2 + t // 2, t % 2, self.down_tile(l, j, t))

                ada(0, True)

                with sp.Fori(0, QUARTERS - 1) as j:
                    down(j)
                    for t in range(4):
                        W.issue(sp, m0 + per * (j + 1) + t // 2, t % 2, self.up_tile(l, j + 1, t))
                    ada(j + 1, False)
                down(QUARTERS - 1)

            @block.tensor
            def _(pe):
                def up(j, ts):
                    for t in ts:
                        tile_columns(pe, W, m0 + per * j + t // 2, t % 2, self.pst, self.h)

                def down(j):
                    m = m0 + per * j + 2
                    W.ready(pe, m, 0)
                    for k in range(KC):
                        if k % n == 0:
                            pe.wait_ge(low, 4 * j + k // n + 1)
                        for c in range(n):
                            cols = slice(c * P, (c + 1) * P)
                            mm = products(pe, self.pst[:, 0, c], (W.hi[:, 0, k, cols], W.lo[:, 0, k, cols]), (u[0][:, k, :], u[1][:, k, :]), k == 0, k == KC - 1)
                    mm.then_inc(W.tile_done, 1)
                    for t in range(1, 4):
                        tile_columns(pe, W, m + t // 2, t % 2, self.pst, u)

                def ada(j):
                    for i in range(ADA_PER):
                        pe.wait_ge(ada_part, ADA_PER * j + i + 1)
                        for c in range(n):
                            mm = pe.matmul(ada_ps[:, bass.ds((j * ADA_PER + i) * n + c, 1)], ada_acc[:, i, c * P:(c + 1) * P], self.c("ones")[:, 0:1],
                                           start=True, stop=True)
                        mm.then_inc(ada_done, 1)

                norm.tensor(pe)
                norm.first_pair(pe, m0, False)
                up(0, (2, 3))
                down(0)
                ada(0)
                with pe.Fori(1, QUARTERS) as j:
                    up(j, range(4))
                    down(j)
                    ada(j)

            def scalar_quarter(act, j, last):
                for t in range(4):
                    q = t % 2
                    W.done(act, m0 + per * j + t // 2, q)
                    if t >= 2:
                        act.wait_ge(low, 4 * j + t - 1)
                    act.activation(r[:, q], self.pst[:, q, 0:n, :], ACT.Relu).then_inc(W.evicted[q], 1)
                    W.split_hi(act, m0 + per * j + t // 2 + 1, q)
                    act.wait_ge(squared, 4 * j + t + 1)
                    act.activation(u[0][:, n * t:n * t + n, :], r[:, q], ACT.Copy).then_inc(rounded, 1)
                for t in range(4):
                    if not (last and t >= 2):
                        W.split_hi(act, m0 + per * j + 2 + t // 2 + 1, t % 2)

            @block.scalar
            def _(act):
                norm.scalar(act)
                with act.Fori(0, QUARTERS - 1) as j:
                    scalar_quarter(act, j, False)
                scalar_quarter(act, QUARTERS - 1, True)

            def vector_quarter(dve, j, last):
                for t in range(4):
                    q = t % 2
                    W.read(dve, m0 + per * j + t // 2, q)
                    dve.tensor_tensor(r[:, q], r[:, q], r[:, q], ALU.mult).then_inc(squared, 1)
                    W.split_lo(dve, m0 + per * j + t // 2 + 1, q)
                    dve.wait_ge(rounded, 4 * j + t + 1)
                    dve.tensor_tensor(u[1][:, n * t:n * t + n, :], r[:, q], u[0][:, n * t:n * t + n, :].bitcast(F32),
                                      ALU.subtract).then_inc(low, 1)
                for t in range(4):
                    W.done(dve, m0 + per * j + 2 + t // 2, t % 2)
                    for c in range(n):
                        k = n * t + c
                        e = dve.tensor_tensor(self.x[:, k, :], self.x[:, k, :], self.pst[:, t % 2, c], ALU.add)
                    e.then_inc(W.evicted[t % 2], 1)
                    if not (last and t >= 2):
                        W.split_lo(dve, m0 + per * j + 2 + t // 2 + 1, t % 2)

            @block.vector
            def _(dve):
                norm.vector(dve)
                with dve.Fori(0, QUARTERS - 1) as j:
                    vector_quarter(dve, j, False)
                vector_quarter(dve, QUARTERS - 1, True)
                dve.wait_ge(ada_done, ADA_PER * QUARTERS)
                share = ADA_PER * QUARTERS * n
                dve.tensor_copy(self.ada_sum[:, bass.ds(l * share, share)], ada_ps[:, 0:share])

            @block.gpsimd
            def _(pool):
                pool.sem_clear(clear)

                def quarter(j, first):
                    for i in range(ADA_PER):
                        pool.wait_ge(ada_landed[i], 64 * j + 64)
                        if i == 0 and not first:
                            pool.wait_ge(ada_done, ADA_PER * j)
                        w, c = ada_w[:, i], self.silu_c[:].unsqueeze(2).to_broadcast([P, KC, COL])
                        pool.tensor_tensor(w, w, c, ALU.mult).then_inc(ada_step, 1)
                        for s, half in enumerate((4, 2)):
                            pool.wait_ge(ada_step, 3 * (ADA_PER * j + i) + s + 1)
                            pool.tensor_tensor(w[:, 0:half], w[:, 0:half], w[:, half:2 * half], ALU.add).then_inc(ada_step, 1)
                        pool.wait_ge(ada_step, 3 * (ADA_PER * j + i) + 3)
                        pool.tensor_tensor(ada_acc[:, i], w[:, 0], w[:, 1], ALU.add).then_inc(ada_part, 1)

                quarter(0, True)
                with pool.Fori(1, QUARTERS) as j:
                    quarter(j, False)


SSM_IN, SSM_HEADS, SSM_G, SSM_N, CONV = 2 * D, 32, 4, 128, 4
SSM_XBC = SSM_IN + 2 * SSM_G * SSM_N
NH, NG, NKV = 16, 2, 2 * HD
HPG = NH // NG
CMP_STRIDE, CMP_BLOCK, CMP_HID = 16, 32, 256
NC = (S - CMP_BLOCK) // CMP_STRIDE + 1
SEL, TOPK = 64, 4
NSEL = S // SEL
MG, ME, EH = 4, 8, 256
NE = MG * ME
_at = np.cumsum([0, SSM_IN, SSM_XBC, SSM_HEADS, NH * HD] + [NKV] * 6 + [3 * NH, D, D]).tolist()
C_Z, C_XBC, C_DT, C_Q, C_KC, C_VC, C_KS, C_VS, C_KW, C_VW, C_GN, C_GS, C_GA = _at[:13]
B2 = DEPTH * PAIRS
P_XBC, P_SMALL, P_Z, P_SSMO, P_GS, P_Q, P_KK, P_GA, P_NSAO, P_WO, P_MOE = 0, 6, 7, 11, 15, 17, 19, 21, 23, 25, 27
BATCH_E = 4
SLOTS, FAR = P, 1000.0
MOE_PER = BATCH_E + 2
P_END = P_MOE + NE // BATCH_E * MOE_PER
_names = [("n1", 8), ("n2", 8), ("fin", 8), ("bada", 48), ("c", 8), ("convb", 24), ("ssmg", 16), ("convw", 96), ("dskip", 16),
          ("dtb", 32), ("alog", 32), ("brout", 36), ("pek", 16), ("pev", 16), ("ada", 48), ("g1", 8), ("g2", 8)]
PAR2, _n = {}, 0
for _name, _w in _names:
    PAR2[_name] = (_n, _w)
    _n += _w
PAR2_N = _n
VECTORS, CONVS = PAR2["convw"]
TWO_PI = 2 * np.pi
PI_A = 6.28125
PI_B = float(np.float32(int((TWO_PI - PI_A) * 2 ** 20) / 2 ** 20))
PI_C = float(np.float32(TWO_PI - PI_A - PI_B))
ROUND = 1.5 * 2 ** 23


class SecondBlock(FirstBlock):
    def p2(self, name, a=0, n=None):
        o, w = PAR2[name]
        return self.par2[:, o + a:o + (w if n is None else a + n)]

    def tile2(self, m, q):
        w_in = self.d["w_in_2"].rearrange("o k n -> (o k) n")
        flat = lambda n: self.d[n].rearrange("o k n -> (o k) n")

        def both(a, na, b, nb):
            out = []
            for src, n, at in ((a, na, 0), (b, nb, na)):
                v = w_in[:, src:src + n].rearrange("(k p) n -> p k n", p=P)
                out += [(lambda t, h=h, at=at, n=n: t[:, h:h + KC // 2, at:at + n], v[:, h:h + KC // 2, :]) for h in (0, KC // 2)]
            return out

        t = 2 * m + q
        cols = lambda w, first, at=0: quarters_of(w[:, at + (t - 2 * first) * COL:at + (t - 2 * first + 1) * COL])
        if m < P_SMALL:
            return cols(w_in, P_XBC, C_XBC)
        if m < P_Z:
            return both(C_DT, SSM_HEADS, C_GN, 3 * NH) if q == 0 else both(C_VS, NKV, C_VW, NKV)
        if m < P_SSMO:
            return cols(w_in, P_Z, C_Z)
        if m < P_GS:
            half, t = divmod(t - 2 * P_SSMO, 4)
            return quarters_of(flat("w_ssm_out_2")[half * D:(half + 1) * D, t * COL:(t + 1) * COL])
        if m < P_Q:
            return cols(w_in, P_GS, C_GS)
        if m < P_KK:
            return cols(w_in, P_Q, C_Q)
        if m < P_GA:
            return self.twice(w_in, (C_KC, C_VC, C_KS, C_KW)[t - 2 * P_KK])
        if m < P_NSAO:
            return cols(w_in, P_GA, C_GA)
        if m < P_WO:
            return cols(flat("w_nsa_out_2"), P_NSAO)
        if m < P_MOE:
            return cols(flat("w_o_2"), P_WO)
        raise AssertionError

    def expert_tile(self, j, e, q):
        w = self.d["w_exp_up_2" if q else "w_exp_gate_2"].rearrange("o e k n -> (o e) k n")
        return quarters_of(w[bass.ds(j * BATCH_E + e, 1)].rearrange("e k n -> (e k) n"))

    def expert_down_tile(self, j, e):
        w = self.d["w_exp_down_2"].rearrange("o e k n -> (o e) k n")[bass.ds(j * BATCH_E + e, 1)].rearrange("e (k p) n -> p (e k) n", p=P)
        flat = lambda t, k, c: t.rearrange("p k n -> p (k n)")[:, k * D + c:k * D + c + 512]
        return [(lambda t, k=k, c=c: flat(t, k, c), w[:, k, c:c + 512]) for k in range(2) for c in (0, 512)]

    def expert_rows_tile(self, j, t):
        w = self.d["w_exp_down_2"].rearrange("o e k n -> (o e k) n")
        return quarters_of(w[bass.ds(j * D, D), t * COL:(t + 1) * COL])

    def issue2(self, sp, a, b):
        for m in range(a + 2, b + 2):
            for q in range(2):
                self.W.issue(sp, B2 + m, q, self.tile2(m, q) if m < P_MOE else self.expert_tile(0, m - P_MOE, q))

    def load(self):
        nc, d = self.nc, self.d
        with ExitStack() as st:
            sem, clear = self.stages.open("load", st)
            landed, vectors, loaded, turned, columns = (sem(x) for x in ("landed", "vectors", "loaded", "turned", "columns"))
            sb = lambda n, s: st.enter_context(nc.sbuf_tensor(n, s, F32))
            xt, rows = sb("x_tokens", [P, TB, D]), sb("vector_rows", [P, 2, P])
            block = st.enter_context(nc.Block())
            loads = [0]

            @block.sync
            def _(sp):
                sp.dma_start(self.const[:], d["const"][:, 0:self.n_const]).then_inc(landed, 16)
                sp.dma_start(xt[:], d["x"].rearrange("o (b p) d -> p (o b) d", p=P)).then_inc(landed, 16)
                sp.dma_start(self.const_first[:], d["const"][:, self.n_const:]).then_inc(loaded, 16)
                loads[0] += 16

            @block.scalar
            def _(act):
                at = 0
                for src in ("norm1_g_2", "norm2_g_2", "final_g_2", "b_ada_2", "c_2", "conv_b_2", "ssm_norm_g_2"):
                    k = d[src].shape[-1] // P
                    v = d[src].rearrange("(k p) -> k p", p=P) if src == "final_g_2" else d[src].rearrange("o (k p) -> (o k) p", p=P)
                    act.dma_start(rows[at:at + k, 0, :], v).then_inc(vectors, 16)
                    at += k
                assert at == VECTORS
                act.dma_start(rows[0:CONVS, 1, :], d["conv_w_2"].rearrange("o i (k p) -> (o i k) p", p=P)).then_inc(vectors, 16)

                def load(dst, src):
                    act.dma_start(dst, src, allow_slow_non_contiguous=True).then_inc(loaded, 16)
                    loads[0] += 16

                for r in range(2):
                    half = slice(r * HD, (r + 1) * HD)
                    o, w = PAR2["dskip"]
                    load(self.par2[half, o:o + w], d["d_skip_2"].rearrange("o (k r) -> o k r", r=2)[:, :, r].to_broadcast([HD, w]))
                    for n, src in (("pek", "cmp_pe_k_2"), ("pev", "cmp_pe_v_2")):
                        o, w = PAR2[n]
                        load(self.par2[half, o:o + w], d[src][0].rearrange("(i r) e -> r e i", r=2)[r])
                for n, src in (("dtb", "dt_bias_2"), ("alog", "a_log_2")):
                    load(self.p2(n), d[src].to_broadcast([P, SSM_HEADS]))
                load(self.p2("brout", 0, MG), d["b_router_group_2"].to_broadcast([P, MG]))
                load(self.p2("brout", MG, NE), d["b_router_expert_2"].to_broadcast([P, NE]))
                act.wait_ge(columns, 2)
                act.activation(self.silu_c[:], self.p2("c"), ACT.Silu)
                act.wait_ge(loaded, loads[0])

            @block.tensor
            def _(pe):
                pe.wait_ge(landed, 32)
                for k in range(KC):
                    for b in range(TB):
                        t = pe.transpose(self.ps[:, k, b * P:(b + 1) * P], xt[:, b, k * P:(k + 1) * P], self.c("ident"))
                    t.then_inc(turned, 1)
                pe.wait_ge(vectors, 16 * 8)
                pe.wait_ge(columns, 1)
                for i, k in enumerate((VECTORS, CONVS)):
                    t = pe.transpose(self.ps[:, i, 0:k], rows[0:k, i, :], self.c("ident")[0:k, 0:k])
                t.then_inc(turned, 1)

            @block.vector
            def _(dve):
                for k in range(KC):
                    dve.wait_ge(turned, k + 1)
                    e = dve.tensor_copy(self.x[:, k, :], self.ps[:, k, :])
                e.then_inc(columns, 1)
                dve.wait_ge(turned, KC + 1)
                dve.tensor_copy(self.p2("convw"), self.ps[:, 1, 0:CONVS])
                dve.tensor_copy(self.par2[:, 0:VECTORS], self.ps[:, 0, 0:VECTORS]).then_inc(columns, 1)

            @block.gpsimd
            def _(pool):
                pool.sem_clear(clear)

    def ssm_project(self, prologue):
        nc, W = self.nc, self.W
        n = COL // P
        with ExitStack() as st:
            sem, clear = self.stages.open("ssm_project", st)
            norm = Norm(self, "norm1_2", sem, st, lambda k: self.p2("g1", k, 1), shift=lambda k: self.p2("ada", k, 1), prologue=prologue, split0=B2)
            padded, tap, conved, active, ada = sem("padded"), sem("tap"), sem("conved"), sem("active"), sem("ada")
            sb = lambda nm, s: st.enter_context(nc.sbuf_tensor(nm, s, F32))
            xp, acc = sb("conv_in", [P, 2, n, S + CONV - 1]), sb("conv_acc", [P, 2, n, S])
            block = st.enter_context(nc.Block())
            tiles = 2 * (P_SMALL - P_XBC)
            dst = lambda t: self.xs[:, n * t:n * t + n, :] if n * t < 16 else self.bc[:, n * t - 16:n * t - 16 + n, :]

            @block.sync
            def _(sp):
                norm.sync(sp)
                self.issue2(sp, P_XBC, P_Z)

            @block.tensor
            def _(pe):
                norm.tensor(pe)
                norm.first_pair(pe, B2, True)
                for t in range(2, tiles):
                    tile_columns(pe, W, B2 + t // 2, t % 2, self.pst, self.h)
                tile_tokens(pe, W, B2 + P_SMALL, 0, self.pst, self.h, SSM_HEADS + 3 * NH)
                tile_tokens(pe, W, B2 + P_SMALL, 1, self.pst, self.h, 2 * NKV)

            @block.scalar
            def _(act):
                def silu(t):
                    act.wait_ge(conved, t + 1)
                    act.activation(dst(t), acc[:, t % 2], ACT.Silu).then_inc(active, 1)

                norm.scalar(act)
                act.wait_ge(padded, 1)
                for t in range(tiles):
                    q = t % 2
                    W.done(act, B2 + t // 2, q)
                    if t >= 2:
                        act.wait_ge(conved, t - 1)
                    act.activation(xp[:, q, :, CONV - 1:], self.pst[:, q, 0:n, :], ACT.Copy).then_inc(W.evicted[q], 1)
                    nxt = (t + 2) // 2
                    W.split_hi(act, B2 + nxt, q, cols=SSM_HEADS + 3 * NH if nxt == P_SMALL and q == 0 else COL)
                    if t >= 1:
                        silu(t - 1)
                silu(tiles - 1)
                for q, (to, w) in enumerate(((self.dtgn, SSM_HEADS + 3 * NH), (self.vsvw, 2 * NKV))):
                    W.done(act, B2 + P_SMALL, q)
                    tok = self.pst[:, q].rearrange("p a b -> p (a b)")[:, 0:TB * COL].rearrange("p (b n) -> p b n", b=TB)
                    act.activation(to[:], tok[:, :, 0:w], ACT.Copy).then_inc(W.evicted[q], 1)
                    W.split_hi(act, B2 + P_SMALL + 1, q)

            @block.vector
            def _(dve):
                link = Link(dve, ada)
                link(dve.tensor_tensor(self.p2("ada"), self.ada_sum[:], self.p2("bada"), ALU.add))
                for g, nm, s in (("g1", "n1", 1), ("g2", "n2", 4)):
                    link(dve.scalar_tensor_tensor(self.p2(g), self.p2("ada", s * KC, KC), 1.0, self.p2(nm), ALU.add, ALU.mult))
                norm.vector(dve)
                for t in range(tiles):
                    q = t % 2
                    W.read(dve, B2 + t // 2, q)
                    if t >= 2:
                        dve.wait_ge(active, t - 1)
                    for i in range(CONV - 1, -1, -1):
                        for c in range(n):
                            k = n * t + c
                            wt = self.p2("convw", 24 * i + k, 1)
                            src = xp[:, q, c, i:i + S]
                            if i == CONV - 1:
                                e = dve.tensor_scalar(acc[:, q, c], src, wt, self.p2("convb", k, 1), ALU.mult, ALU.add)
                            else:
                                dve.wait_ge(tap, 6 * t + 2 * (CONV - 2 - i) + c + 1)
                                e = dve.scalar_tensor_tensor(acc[:, q, c], src, wt, acc[:, q, c], ALU.mult, ALU.add)
                            if i:
                                e.then_inc(tap, 1)
                    e.then_inc(conved, 1)
                    nxt = (t + 2) // 2
                    W.split_lo(dve, B2 + nxt, q, cols=SSM_HEADS + 3 * NH if nxt == P_SMALL and q == 0 else COL)
                for q in range(2):
                    W.split_lo(dve, B2 + P_SMALL + 1, q)

            @block.gpsimd
            def _(pool):
                pool.sem_clear(clear)
                pool.memset(xp[:, :, :, 0:CONV - 1], 0.0).then_inc(padded, 1)

    def ssd(self):
        nc = self.nc
        U, HU = 8, 4
        UW = HU * HD
        with ExitStack() as st:
            sem, clear = self.stages.open("ssd", st)
            (prep, prep_a, dt_ready, xt_ready, ac_ready, acs_done, dl_ready, we_ready, wend, xn_copied, xdt_ready, xw_ready, ab_ready,
             seg_done, e_done, l_exp, m_ready, ce_ready, y_ready, s_ready, y_taken, scaled, st_added, cb_ready) = (sem(x) for x in (
                 "prep", "prep_a", "dt_ready", "xt_ready", "ac_ready", "acs_done", "dl_ready", "we_ready", "wend", "xn_copied",
                 "xdt_ready", "xw_ready", "ab_ready", "seg_done", "e_done", "l_exp", "m_ready", "ce_ready", "y_ready", "s_ready",
                 "y_taken", "scaled", "st_added", "cb_ready"))
            sb = lambda nm, s: st.enter_context(nc.sbuf_tensor(nm, s, F32))
            dt, dta, v, ea = sb("dt", [P, TB, SSM_HEADS]), sb("dt_a", [P, TB, SSM_HEADS]), sb("dt_v", [P, TB, SSM_HEADS]), sb("exp_a", [P, SSM_HEADS])
            xn, xdt, bn = sb("x_tok", [P, SSM_IN]), sb("x_dt", [P, SSM_IN]), sb("b_tok", [P, SSM_G * SSM_N])
            acs, dl, el = sb("acum", [P, SSM_HEADS]), sb("decay_end", [P, SSM_HEADS]), sb("decay_all", [P, SSM_HEADS])
            L, E = sb("ssd_l", [P, 2, HU, P]), sb("ssd_e", [P, 2, HU, P])
            state = sb("state", [P, SSM_IN])
            small = self.ps[:, 5, :]
            block = st.enter_context(nc.Block())
            heads = lambda t: t.rearrange("p (h e) -> p h e", e=HD)

            @block.tensor
            def _(pe):
                for ck in range(TB):
                    tok = slice(ck * P, (ck + 1) * P)
                    if ck > 0:
                        pe.wait_ge(y_taken, U * ck)
                        pe.wait_ge(st_added, U * ck)
                    for c in range(16):
                        pe.transpose(self.flat(0, 2048)[:, c * P:(c + 1) * P], self.xs[:, c, tok], self.c("ident"))
                    for g in range(SSM_G):
                        t = pe.transpose(self.ps[:, 4, g * P:(g + 1) * P], self.bc[:, g, tok], self.c("ident"))
                    t.then_inc(xt_ready, 1)
                    pe.wait_ge(dt_ready, 1)
                    pe.matmul(small[:, 0:SSM_HEADS], self.c("prefix"), dta[:, ck, :], start=True, stop=True)
                    pe.matmul(small[:, SSM_HEADS:2 * SSM_HEADS], self.c("ones"), dta[:, ck, :], start=True, stop=True).then_inc(ac_ready, 1)
                    pe.wait_ge(xn_copied, 2 * ck + 1)
                    for g in range(SSM_G):
                        mm = pe.matmul(self.ps[:, 4, g * P:(g + 1) * P], self.bc[:, g, tok], self.bc[:, SSM_G + g, tok], start=True, stop=True)
                    mm.then_inc(cb_ready, 1)

                    def front(u):
                        n, g = U * ck + u, u // 2
                        if n >= 2:
                            pe.wait_ge(seg_done, n - 1)
                        if n - 2 >= U:
                            pe.wait_ge(e_done, n - 1 - U)
                        for j in range(HU):
                            h = u * HU + j
                            mm = pe.matmul(self.ps[:, 6 + n % 2, j * P:(j + 1) * P], dta[:, ck, h:h + 1].to_broadcast([P, P]), self.c("prefix"),
                                           start=True, stop=True)
                        mm.then_inc(ab_ready, 1)

                    def back(u):
                        n, g = U * ck + u, u // 2
                        pe.wait_ge(m_ready, n + 1)
                        pe.wait_ge(xdt_ready, ck + 1)
                        if ck > 0:
                            pe.wait_ge(ce_ready, n + 1 - U)
                        if n >= 2:
                            pe.wait_ge(y_taken, n - 1)
                        for j in range(HU):
                            h = u * HU + j
                            out = self.ps[HD * (j % 2):HD * (j % 2) + HD, n % 2, (j // 2) * P:(j // 2 + 1) * P]
                            mm = pe.matmul(out, xdt[:, h * HD:(h + 1) * HD], L[:, n % 2, j, :], start=True, stop=ck == 0)
                            if ck > 0:
                                mm = pe.matmul(out, state[:, h * HD:(h + 1) * HD], E[:, n % 2, j, :], start=False, stop=True)
                        mm.then_inc(y_ready, 1)
                        if ck + 1 < TB:
                            pe.wait_ge(xw_ready, ck + 1)
                            if n >= 2:
                                pe.wait_ge(st_added, n - 1)
                            pe.matmul(self.ps[:, 2 + n % 2, 0:UW], bn[:, g * P:(g + 1) * P], xn[:, u * UW:(u + 1) * UW],
                                      start=True, stop=True).then_inc(s_ready, 1)

                    front(0)
                    for u in range(U):
                        if u + 1 < U:
                            front(u + 1)
                        back(u)

            @block.scalar
            def _(act):
                act.activation(ea[:], self.p2("alog"), ACT.Exp).then_inc(prep_a, 1)
                act.wait_ge(prep, 2)
                act.activation(dt[:], dt[:], ACT.Exp).then_inc(prep_a, 1)
                act.wait_ge(prep_a, 2)
                act.activation(dt[:], dt[:], ACT.Ln, bias=1.0).then_inc(prep_a, 1)
                for ck in range(TB):
                    act.wait_ge(xt_ready, ck + 1)
                    if ck > 0:
                        act.wait_ge(s_ready, U * ck)
                    act.activation(bn[:], self.ps[:, 4, :], ACT.Copy).then_inc(xn_copied, 1)
                    act.activation(xn[:], self.flat(0, SSM_IN), ACT.Copy).then_inc(xn_copied, 1)
                    act.wait_ge(dl_ready, ck + 1)
                    act.activation(el[:], small[:, SSM_HEADS:2 * SSM_HEADS], ACT.Exp).then_inc(we_ready, 1)
                    act.activation(dl[:], dl[:], ACT.Exp).then_inc(we_ready, 1)

                    def exps(u):
                        n = U * ck + u
                        act.wait_ge(seg_done, n + 1)
                        act.activation(L[:, n % 2], L[:, n % 2], ACT.Exp).then_inc(l_exp, 1)
                        if ck > 0:
                            act.wait_ge(y_ready, n - 1)
                            act.activation(E[:, n % 2], self.ps[:, 6 + n % 2, :].rearrange("p (j t) -> p j t", j=HU), ACT.Exp).then_inc(e_done, 1)

                    for u in range(U):
                        exps(u)

            @block.vector
            def _(dve):
                bias = self.p2("dtb").unsqueeze(1).to_broadcast([P, TB, SSM_HEADS])
                dve.tensor_tensor(v[:], self.dtgn[:, :, 0:SSM_HEADS], bias, ALU.add).then_inc(prep, 1)
                dve.wait_ge(prep, 1)
                dve.scalar_tensor_tensor(dt[:], v[:], -1.0, v[:], ALU.mult, ALU.min).then_inc(prep, 1)
                dve.wait_ge(prep_a, 3)
                dve.scalar_tensor_tensor(dt[:], v[:], 0.0, dt[:], ALU.max, ALU.add).then_inc(prep, 1)
                dve.wait_ge(prep, 3)
                dve.scalar_tensor_tensor(dta[:], dt[:], -1.0, ea[:].unsqueeze(1).to_broadcast([P, TB, SSM_HEADS]), ALU.mult, ALU.mult).then_inc(dt_ready, 1)
                for ck in range(TB):
                    tok = slice(ck * P, (ck + 1) * P)
                    per_head = lambda a: a.unsqueeze(2).to_broadcast([P, SSM_HEADS, HD])
                    dve.wait_ge(ac_ready, ck + 1)
                    if ck > 0:
                        dve.wait_ge(st_added, U * ck)
                    dve.tensor_copy(acs[:], small[:, 0:SSM_HEADS]).then_inc(acs_done, 1)
                    dve.wait_ge(acs_done, ck + 1)
                    if ck > 0:
                        dve.wait_ge(xw_ready, ck)
                    dve.tensor_tensor(dl[:], small[:, SSM_HEADS:2 * SSM_HEADS], acs[:], ALU.subtract).then_inc(dl_ready, 1)
                    dve.wait_ge(xn_copied, 2 * ck + 2)
                    if ck > 0:
                        dve.wait_ge(y_ready, U * ck)
                    dve.tensor_tensor(heads(xdt[:]), heads(xn[:]), per_head(dt[:, ck, :]), ALU.mult).then_inc(xdt_ready, 1)
                    dve.wait_ge(we_ready, 2 * ck + 2)
                    dve.wait_ge(xdt_ready, ck + 1)
                    if ck + 1 < TB:
                        dve.tensor_tensor(heads(xn[:]), heads(xdt[:]), per_head(dl[:]), ALU.mult).then_inc(xw_ready, 1)

                    def segment(u):
                        n = U * ck + u
                        dve.wait_ge(ab_ready, n + 1)
                        if n >= 2:
                            dve.wait_ge(y_ready, n - 1)
                        for j in range(HU):
                            e = dve.scalar_tensor_tensor(L[:, n % 2, j], self.ps[:, 6 + n % 2, j * P:(j + 1) * P], acs[:, u * HU + j:u * HU + j + 1],
                                                         self.c("causal_t"), ALU.subtract, ALU.add)
                        e.then_inc(seg_done, 1)

                    def weigh(u):
                        n, g = U * ck + u, u // 2
                        dve.wait_ge(l_exp, n + 1)
                        dve.wait_ge(cb_ready, ck + 1)
                        cb = self.ps[:, 4, g * P:(g + 1) * P].unsqueeze(1).to_broadcast([P, HU, P])
                        dve.tensor_tensor(L[:, n % 2], L[:, n % 2], cb, ALU.mult).then_inc(m_ready, 1)
                        if ck > 0:
                            dve.wait_ge(e_done, n + 1 - U)
                            cc = self.bc[:, SSM_G + g, tok].unsqueeze(1).to_broadcast([P, HU, P])
                            dve.tensor_tensor(E[:, n % 2], E[:, n % 2], cc, ALU.mult).then_inc(ce_ready, 1)

                    def finish(u):
                        n = U * ck + u
                        dve.wait_ge(y_ready, n + 1)
                        for c in range(2):
                            k = 2 * u + c
                            e = dve.scalar_tensor_tensor(self.xs[:, k, tok], self.xs[:, k, tok], self.p2("dskip", k, 1),
                                                         self.ps[:, n % 2, c * P:(c + 1) * P], ALU.mult, ALU.add)
                        e.then_inc(y_taken, 1)
                        if ck + 1 < TB:
                            mine = state[:, u * UW:(u + 1) * UW]
                            if ck == 0:
                                dve.wait_ge(s_ready, n + 1)
                                dve.tensor_copy(mine, self.ps[:, 2 + n % 2, 0:UW]).then_inc(st_added, 1)
                            else:
                                keep = el[:, u * HU:(u + 1) * HU].unsqueeze(2).to_broadcast([P, HU, HD])
                                dve.tensor_tensor(heads(mine), heads(mine), keep, ALU.mult).then_inc(scaled, 1)
                                dve.wait_ge(s_ready, n + 1)
                                dve.wait_ge(scaled, n + 1 - U)
                                dve.tensor_tensor(mine, mine, self.ps[:, 2 + n % 2, 0:UW], ALU.add).then_inc(st_added, 1)

                    segment(0)
                    for u in range(U):
                        if u + 1 < U:
                            segment(u + 1)
                        weigh(u)
                        if u >= 1:
                            finish(u - 1)
                    finish(U - 1)

            @block.gpsimd
            def _(pool):
                pool.sem_clear(clear)


class SsmTail(SecondBlock):

    def ssm_gate(self):
        nc, W, n = self.nc, self.W, COL // P
        tiles = 2 * (P_SSMO - P_Z)
        with ExitStack() as st:
            sem, clear = self.stages.open("ssm_gate", st)
            used, angle, steps, folded = sem("used"), sem("angle"), sem("steps"), sem("folded")
            z = st.enter_context(nc.sbuf_tensor("silu_z", [P, 2, n, S], F32))
            pos = st.enter_context(nc.sbuf_tensor("positions", [P, S], I32))
            ang, turns = (st.enter_context(nc.sbuf_tensor(nm, [P, 2, S], F32)) for nm in ("angle", "turns"))
            block = st.enter_context(nc.Block())

            @block.sync
            def _(sp):
                sp.dma_start(pos[:], self.d["positions_2"].to_broadcast([P, S])).then_inc(angle, 16)
                self.issue2(sp, P_Z, P_SSMO)

            @block.tensor
            def _(pe):
                for t in range(tiles):
                    tile_columns(pe, W, B2 + P_Z + t // 2, t % 2, self.pst, self.h)

            @block.scalar
            def _(act):
                for t in range(tiles):
                    m, q = B2 + P_Z + t // 2, t % 2
                    W.done(act, m, q)
                    if t >= 2:
                        act.wait_ge(used, t - 1)
                    act.activation(z[:, q], self.pst[:, q, 0:n, :], ACT.Silu).then_inc(W.evicted[q], 1)
                    W.split_hi(act, m + 1, q)
                act.wait_ge(folded, 2)
                for i in range(2):
                    act.activation(self.trig[:, i], ang[:, i], ACT.Sin)

            def angles(dve):
                link = Link(dve, steps)
                dve.wait_ge(angle, 16)
                link(dve.tensor_copy(ang[:, 0], pos[:]))
                link(dve.tensor_scalar(ang[:, 0], ang[:, 0], self.c("inv"), None, ALU.mult))
                link(dve.tensor_scalar(turns[:, 0], ang[:, 0], 1.0 / TWO_PI, ROUND, ALU.mult, ALU.add))
                link(dve.tensor_scalar(turns[:, 0], turns[:, 0], ROUND, None, ALU.subtract))
                for part in (PI_A, PI_B, PI_C):
                    link(dve.scalar_tensor_tensor(ang[:, 0], turns[:, 0], -part, ang[:, 0], ALU.mult, ALU.add))
                link(dve.tensor_scalar(ang[:, 1], ang[:, 0], float(np.pi / 2), None, ALU.add))
                link(dve.tensor_scalar(turns[:, 1], ang[:, 1], float(np.pi), -TWO_PI, ALU.is_gt, ALU.mult))
                link(dve.tensor_tensor(ang[:, 1], ang[:, 1], turns[:, 1], ALU.add))
                edge = 3.1415925
                for i in range(2):
                    dve.tensor_scalar(ang[:, i], ang[:, i], edge, -edge, ALU.min, ALU.max).then_inc(folded, 1)

            @block.vector
            def _(dve):
                for t in range(tiles):
                    m, q = B2 + P_Z + t // 2, t % 2
                    W.read(dve, m, q)
                    dve.tensor_tensor(self.xs[:, n * t:n * t + n, :], self.xs[:, n * t:n * t + n, :], z[:, q], ALU.mult).then_inc(used, 1)
                    W.split_lo(dve, m + 1, q)
                    if t == 1:
                        angles(dve)

            @block.gpsimd
            def _(pool):
                pool.sem_clear(clear)

    def ssm_norm(self):
        nc, GC = self.nc, 4
        with ExitStack() as st:
            sem, clear = self.stages.open("ssm_norm", st)
            squared, used, mean, root, inverse, normed, rounded = (sem(x) for x in ("squared", "used", "mean", "root", "inverse", "normed", "rounded"))
            sb = lambda nm, s: st.enter_context(nc.sbuf_tensor(nm, s, F32))
            sq, rs = sb("ssm_sq", [P, 2, S]), sb("ssm_rs", [P, SSM_G, S])
            block = st.enter_context(nc.Block())

            @block.scalar
            def _(act):
                for k in range(16):
                    if k >= 2:
                        act.wait_ge(used, k - 1)
                    act.activation(sq[:, k % 2], self.xs[:, k, :], ACT.Square).then_inc(squared, 1)
                for g in range(SSM_G):
                    act.wait_ge(mean, g + 1)
                    act.activation(rs[:, g], rs[:, g], ACT.Sqrt).then_inc(root, 1)
                for k in range(KC):
                    act.wait_ge(normed, k + 1)
                    act.activation(self.yn[0][:, k, :], self.xs[:, k, :], ACT.Copy).then_inc(rounded, 1)

            @block.tensor
            def _(pe):
                for k in range(16):
                    pe.wait_ge(squared, k + 1)
                    pe.matmul(self.ps[:, k // GC, :], self.c("ones"), sq[:, k % 2], start=k % GC == 0, stop=k % GC == GC - 1).then_inc(used, 1)

            @block.vector
            def _(dve):
                for g in range(SSM_G):
                    dve.wait_ge(used, GC * g + GC)
                    dve.tensor_scalar(rs[:, g], self.ps[:, g, :], 1.0 / (GC * P), EPS, ALU.mult, ALU.add).then_inc(mean, 1)
                for k in range(16):
                    g = k // GC
                    if k % GC == 0:
                        dve.wait_ge(root, g + 1)
                        dve.reciprocal(rs[:, g], rs[:, g]).then_inc(inverse, 1)
                        dve.wait_ge(inverse, g + 1)
                    dve.scalar_tensor_tensor(self.xs[:, k, :], self.xs[:, k, :], self.p2("ssmg", k, 1), rs[:, g], ALU.mult, ALU.mult).then_inc(normed, 1)
                for k in range(KC):
                    dve.wait_ge(rounded, k + 1)
                    dve.tensor_tensor(self.yn[1][:, k, :], self.xs[:, k, :], self.yn[0][:, k, :].bitcast(F32), ALU.subtract)

            @block.gpsimd
            def _(pool):
                pool.sem_clear(clear)

    def ssm_out(self):
        nc, W, n = self.nc, self.W, COL // P
        with ExitStack() as st:
            sem, clear = self.stages.open("ssm_out", st)
            rounded, low = sem("rounded"), sem("low")
            block = st.enter_context(nc.Block())
            mid = B2 + P_SSMO + 1

            @block.sync
            def _(sp):
                self.issue2(sp, P_SSMO, P_GS)

            @block.tensor
            def _(pe):
                for t in range(8):
                    if t == 4:
                        pe.wait_ge(low, KC)
                    tile_columns(pe, W, B2 + P_SSMO + t // 2, t % 2, self.pst, self.yn)

            @block.scalar
            def _(act):
                for t in range(8):
                    m, q = B2 + P_SSMO + t // 2, t % 2
                    if t == 4:
                        for i in range(2):
                            W.done(act, mid, i)
                        for k in range(KC):
                            act.activation(self.yn[0][:, k, :], self.xs[:, KC + k, :], ACT.Copy).then_inc(rounded, 1)
                    W.split_hi(act, m + 1, q)

            @block.vector
            def _(dve):
                for t in range(8):
                    m, q = B2 + P_SSMO + t // 2, t % 2
                    if t == 4:
                        for k in range(KC):
                            dve.wait_ge(rounded, k + 1)
                            dve.tensor_tensor(self.yn[1][:, k, :], self.xs[:, KC + k, :], self.yn[0][:, k, :].bitcast(F32), ALU.subtract).then_inc(low, 1)
                    W.done(dve, m, q)
                    part = self.merged[:, n * (t % 4):n * (t % 4) + n, :]
                    if t < 4:
                        dve.tensor_copy(part, self.pst[:, q, 0:n, :]).then_inc(W.evicted[q], 1)
                    else:
                        dve.tensor_tensor(part, part, self.pst[:, q, 0:n, :], ALU.add).then_inc(W.evicted[q], 1)
                    W.split_lo(dve, m + 1, q)

            @block.gpsimd
            def _(pool):
                pool.sem_clear(clear)

    def nsa_project(self):
        nc, W, n = self.nc, self.W, COL // P
        with ExitStack() as st:
            sem, clear = self.stages.open("nsa_project", st)
            used = sem("used")
            g = st.enter_context(nc.sbuf_tensor("ssm_sig", [P, 2, n, S], F32))
            block = st.enter_context(nc.Block())
            tiles = 2 * (P_NSAO - P_GS)

            @block.sync
            def _(sp):
                self.issue2(sp, P_GS, P_NSAO)

            @block.tensor
            def _(pe):
                for t in range(tiles):
                    tile_columns(pe, W, B2 + P_GS + t // 2, t % 2, self.pst, self.h)

            @block.scalar
            def _(act):
                for t in range(tiles):
                    m, q = P_GS + t // 2, t % 2
                    pair = self.pst[:, q, 0:n, :]
                    W.done(act, B2 + m, q)
                    if m < P_Q:
                        if t >= 2:
                            act.wait_ge(used, t - 1)
                        e = act.activation(g[:, q], pair, ACT.Sigmoid)
                    elif m < P_KK:
                        e = act.mul(self.rp[:, n * (t - 4):n * (t - 4) + n, :], pair, HD ** -0.5)
                    elif m < P_GA:
                        i = t - 8
                        to = self.vc[:] if i == 1 else self.rp[:, (8, None, 10, 12)[i]:(10, None, 12, 14)[i], :]
                        e = act.activation(to, pair, ACT.Copy)
                    else:
                        i = t - 12
                        e = act.activation(self.gate[:, n * i:n * i + n, :], pair, ACT.Sigmoid)
                    e.then_inc(W.evicted[q], 1)
                    W.split_hi(act, B2 + m + 1, q)

            @block.vector
            def _(dve):
                for t in range(tiles):
                    m, q = P_GS + t // 2, t % 2
                    if m < P_Q:
                        W.read(dve, B2 + m, q)
                        part = self.merged[:, n * t:n * t + n, :]
                        dve.tensor_tensor(part, part, g[:, q], ALU.mult).then_inc(used, 1)
                    W.split_lo(dve, B2 + m + 1, q)

            @block.gpsimd
            def _(pool):
                pool.sem_clear(clear)

    def nsa_rope(self):
        nc, n = self.nc, 14
        with ExitStack() as st:
            sem, clear = self.stages.open("nsa_rope", st)
            turned, cosd, sind, done = sem("turned"), sem("cosd"), sem("sind"), sem("done")
            sb = lambda nm, s: st.enter_context(nc.sbuf_tensor(nm, s, F32))
            tc, ts = sb("rope_cos", [P, 2, S]), sb("rope_sin", [P, 2, S])
            x = self.rp
            block = st.enter_context(nc.Block())

            @block.tensor
            def _(pe):
                for c in range(n):
                    if c >= 8:
                        pe.wait_ge(sind, c - 7)
                    pe.matmul(self.ps[:, c % 8, :], self.c("rot"), x[:, c, :], start=True, stop=True).then_inc(turned, 1)

            @block.vector
            def _(dve):
                for c in range(n):
                    if c >= 2:
                        dve.wait_ge(done, c - 1)
                    dve.tensor_tensor(tc[:, c % 2], x[:, c, :], self.trig[:, 1], ALU.mult).then_inc(cosd, 1)
                    dve.wait_ge(turned, c + 1)
                    dve.tensor_tensor(ts[:, c % 2], self.ps[:, c % 8, :], self.trig[:, 0], ALU.mult).then_inc(sind, 1)
                    dve.wait_ge(cosd, c + 1)
                    dve.wait_ge(sind, c + 1)
                    dve.tensor_tensor(x[:, c, :], tc[:, c % 2], ts[:, c % 2], ALU.add).then_inc(done, 1)

            @block.gpsimd
            def _(pool):
                pool.sem_clear(clear)

    def nsa_compress(self):
        nc, d = self.nc, self.d
        NI, HC, NB = CMP_BLOCK // 2, CMP_HID // P, NG * NC
        with ExitStack() as st:
            sem, clear = self.stages.open("nsa_compress", st)
            w1_landed, w2_landed, cleared, gathered, hid_ready, silud, kv_ready, taken, gated = (sem(x) for x in (
                "w1_landed", "w2_landed", "cleared", "gathered", "hid_ready", "silud", "kv_ready", "taken", "gated"))
            sb = lambda nm, s: st.enter_context(nc.sbuf_tensor(nm, s, F32))
            w1 = sb("cmp_w1", [P, NI, CMP_HID])
            w2 = sb("cmp_w2", [P, 2, HC, P])
            blk = sb("cmp_blk", [P, NI, NB])
            hid_k = sb("cmp_hid_k", [P, HC, NG, NC])
            hid_v = sb("cmp_hid_v", [P, HC, NG, 4, 32])
            block = st.enter_context(nc.Block())

            @block.sync
            def _(sp):
                for i, (a, b) in enumerate((("cmp_w1_k_2", "cmp_w2_k_2"), ("cmp_w1_v_2", "cmp_w2_v_2"))):
                    if i:
                        sp.wait_ge(hid_ready, 1)
                    sp.dma_start(w1[:], d[a][0].rearrange("(k p) n -> p k n", p=P)).then_inc(w1_landed, 16)
                    for r in range(2):
                        sp.dma_start(w2[:, i, :, r * HD:(r + 1) * HD], d[b][0].rearrange("(k p) n -> p k n", p=P)).then_inc(w2_landed, 16)

            @block.vector
            def _(dve):
                for i, (src, pe_) in enumerate(((self.rp[:, 8:10, :], "pek"), (self.vc[:], "pev"))):
                    if i:
                        dve.wait_ge(hid_ready, 1)
                    for r in range(2):
                        rows = slice(r * HD, (r + 1) * HD)
                        o, w = PAR2[pe_]
                        for g in range(NG):
                            for q in range(2):
                                win = src[rows, g, q * 16:q * 16 + 16 * NC].rearrange("p (c i r) -> p i r c", i=8, r=2)[:, :, r, :]
                                e = dve.tensor_tensor(blk[rows, 8 * q:8 * q + 8, g * NC:(g + 1) * NC], win,
                                                      self.par2[rows, o + 8 * q:o + 8 * q + 8].unsqueeze(2).to_broadcast([HD, 8, NC]), ALU.add)
                    e.then_inc(gathered, 1)
                dve.wait_ge(kv_ready, 1)
                dve.tensor_copy(self.kcmp[:], self.ps[:, 4, 0:NB]).then_inc(taken, 1)
                dve.wait_ge(cleared, 1)
                dve.wait_ge(kv_ready, 2)
                for j in range(4):
                    rows = slice(32 * j, 32 * j + 32)
                    dve.tensor_copy(self.vcmp[rows, j], self.ps[rows, 5, 0:NG * HD].rearrange("p (g e) -> p g e", g=NG))

            @block.tensor
            def _(pe):
                for i in range(2):
                    pe.wait_ge(w1_landed, 16 * i + 16)
                    pe.wait_ge(gathered, i + 1)
                    for c in range(HC):
                        for k in range(NI):
                            mm = pe.matmul(self.ps[:, 2 * i + c, 0:NB], w1[:, k, c * P:(c + 1) * P], blk[:, k, :], start=k == 0, stop=k == NI - 1)
                    mm.then_inc(hid_ready, 1)
                pe.wait_ge(silud, 5 * HC)
                pe.wait_ge(w2_landed, 64)
                pe.wait_ge(cleared, 1)
                for c in range(HC):
                    mm = pe.matmul(self.ps[:, 4, 0:NB], w2[:, 0, c, :], hid_k[:, c], start=c == 0, stop=c == HC - 1)
                mm.then_inc(kv_ready, 1)
                for g in range(NG):
                    for c in range(HC):
                        mm = pe.matmul(self.ps[:, 5, g * HD:(g + 1) * HD], hid_v[:, c, g].rearrange("p r c -> p (r c)"), w2[:, 1, c, 0:HD],
                                       start=c == 0, stop=c == HC - 1)
                mm.then_inc(kv_ready, 1)

            @block.scalar
            def _(act):
                act.activation(self.dtgn[:, :, SSM_HEADS:], self.dtgn[:, :, SSM_HEADS:], ACT.Sigmoid).then_inc(gated, 1)
                act.wait_ge(cleared, 1)
                for i in range(2):
                    act.wait_ge(hid_ready, i + 1)
                    for c in range(HC):
                        src = self.ps[:, 2 * i + c, 0:NB].rearrange("p (g c) -> p g c", g=NG)
                        if i == 0:
                            act.activation(hid_k[:, c], src, ACT.Silu).then_inc(silud, 1)
                        else:
                            for r in range(4):
                                act.activation(hid_v[:, c, :, r, 0:NC], src, ACT.Silu).then_inc(silud, 1)

            @block.gpsimd
            def _(pool):
                pool.sem_clear(clear)
                pool.memset(hid_v[:], 0.0)
                pool.memset(self.vcmp[:], 0.0)
                pool.memset(self.strip[:, 0:S - P], 0.0)
                pool.tensor_copy(self.strip[:, S - P:S], self.c("causal")).then_inc(cleared, 1)

    def nsa_compressed(self):
        nc = self.nc
        with ExitStack() as st:
            sem, clear = self.stages.open("nsa_cmp", st)
            s_ready, s_taken, steps, shifted, expd, weighted, turned, t_taken, pooled = (sem(x) for x in (
                "s_ready", "s_taken", "steps", "shifted", "expd", "weighted", "turned", "t_taken", "pooled"))
            sb = lambda nm, s: st.enter_context(nc.sbuf_tensor(nm, s, F32))
            p = sb("cmp_p", [P, 2, HPG, NC])
            pc = sb("cmp_pc", [P, 2, HPG, 32])
            mx = sb("cmp_mx", [P, 2, HPG])
            ic = sb("cmp_ic", [P, NG * TB, 36])
            imp = sb("cmp_imp", [P, NG * TB, NSEL])
            gt, eq = sb("cmp_gt", [P, NG * TB, NSEL, NSEL]), sb("cmp_eq", [P, NG * TB, NSEL, NSEL])
            cnt = sb("cmp_cnt", [P, NG * TB, NSEL])
            block = st.enter_context(nc.Block())
            units = [(g, b) for g in range(NG) for b in range(TB)]

            @block.tensor
            def _(pe):
                def scores(u):
                    g, b = units[u]
                    if u >= 2:
                        pe.wait_ge(s_taken, u - 1)
                    for r in range(HPG):
                        h = HPG * g + r
                        rows = slice(HD * (h % 2), HD * (h % 2) + HD)
                        mm = pe.matmul(self.ps[:, 2 * (u % 2) + r % 2, 32 * (r // 2):32 * (r // 2) + NC], self.rp[rows, h // 2, b * P:(b + 1) * P],
                                       self.kcmp[rows, g * NC:(g + 1) * NC], start=True, stop=True)
                    mm.then_inc(s_ready, 1)

                def turn(u):
                    pe.wait_ge(weighted, u + 1)
                    if u >= 2:
                        pe.wait_ge(t_taken, u - 1)
                    for i in range(2):
                        mm = pe.transpose(self.ps[:, 4 + u % 2, i * P:(i + 1) * P], pc[:, u % 2, 4 * i:4 * i + 4].rearrange("p h c -> p (h c)"), self.c("ident"))
                    mm.then_inc(turned, 1)

                scores(0)
                for u in range(len(units)):
                    if u + 1 < len(units):
                        scores(u + 1)
                    turn(u)

            @block.scalar
            def _(act):
                for u, (g, b) in enumerate(units):
                    act.wait_ge(shifted, u + 1)
                    act.activation(p[:, u % 2], p[:, u % 2], ACT.Exp).then_inc(expd, 1)
                    act.wait_ge(turned, u + 1)
                    act.activation(self.pct[:, 2 * g:2 * g + 2, b * P:(b + 1) * P], self.ps[:, 4 + u % 2, 0:2 * P].rearrange("p (i t) -> p i t", i=2),
                                   ACT.Copy).then_inc(t_taken, 1)

            @block.vector
            def _(dve):
                link = Link(dve, steps)
                dve.wait_ge(pooled, 2)
                for u, (g, b) in enumerate(units):
                    i = u % 2
                    mask = lambda n: self.c(n).rearrange("p (b c) -> p b c", b=TB)[:, b, :].unsqueeze(1)
                    per_head = lambda a: a.unsqueeze(2).to_broadcast([P, HPG, NC])
                    dve.wait_ge(s_ready, u + 1)
                    for par in range(2):
                        src = self.ps[:, 2 * i + par, 0:P].rearrange("p (r c) -> p r c", c=32)[:, :, 0:NC]
                        e = dve.tensor_tensor(p[:, i].rearrange("p (r b) c -> p b r c", b=2)[:, par], src, mask("cmp_neg").to_broadcast([P, 4, NC]), ALU.add)
                    e.then_inc(s_taken, 1)
                    dve.wait_ge(s_taken, u + 1)
                    link(dve.tensor_reduce(mx[:, i], p[:, i], AX.X, ALU.max))
                    dve.tensor_tensor(p[:, i], p[:, i], per_head(mx[:, i]), ALU.subtract).then_inc(shifted, 1)
                    dve.wait_ge(expd, u + 1)
                    link(dve.tensor_tensor(p[:, i], p[:, i], mask("cmp_one").to_broadcast([P, HPG, NC]), ALU.mult))
                    link(dve.tensor_reduce(mx[:, i], p[:, i], AX.X, ALU.add))
                    link(dve.tensor_scalar(mx[:, i], mx[:, i], 1e-30, None, ALU.max))
                    link(dve.reciprocal(mx[:, i], mx[:, i]))
                    link(dve.tensor_tensor(p[:, i], p[:, i], per_head(mx[:, i]), ALU.mult))
                    dve.tensor_reduce(ic[:, u, 1:1 + NC], p[:, i].rearrange("p h c -> p c h"), AX.X, ALU.add)
                    gate = self.dtgn[:, b, SSM_HEADS:].rearrange("p (h t) -> p h t", t=3)[:, HPG * g:HPG * g + HPG, 0]
                    if u >= 2:
                        dve.wait_ge(turned, u - 1)
                    dve.tensor_tensor(pc[:, i, :, 0:NC], p[:, i], per_head(gate), ALU.mult).then_inc(weighted, 1)
                dve.wait_ge(weighted, len(units))
                link(dve.tensor_reduce(imp[:], ic[:, :, 0:32].rearrange("p u (j i) -> p u j i", i=4), AX.X, ALU.add))
                link(dve.tensor_tensor(imp[:], imp[:], ic[:, :, 4:36].rearrange("p u (j i) -> p u j i", i=4)[:, :, :, 0], ALU.add))
                prio = self.c("prio").rearrange("p (b j) -> p b j", b=TB)
                for g in range(NG):
                    e = link(dve.tensor_tensor(imp[:, TB * g:TB * g + TB], imp[:, TB * g:TB * g + TB], prio, ALU.add))
                shape = [P, NG * TB, NSEL, NSEL]
                others, own = imp[:].unsqueeze(2).to_broadcast(shape), imp[:].unsqueeze(3).to_broadcast(shape)
                before = self.c("before").rearrange("p (j k) -> p j k", j=NSEL).unsqueeze(1).to_broadcast(shape)
                link(dve.tensor_tensor(gt[:], others, own, ALU.is_gt))
                link(dve.tensor_tensor(eq[:], others, own, ALU.is_equal))
                link(dve.tensor_tensor(eq[:], eq[:], before, ALU.mult))
                link(dve.tensor_tensor(gt[:], gt[:], eq[:], ALU.add))
                link(dve.tensor_reduce(cnt[:], gt[:], AX.X, ALU.add))
                dve.tensor_scalar(self.selneg[:], cnt[:], float(TOPK), NEG, ALU.is_ge, ALU.mult)

            @block.gpsimd
            def _(pool):
                pool.sem_clear(clear)
                pool.memset(pc[:], 0.0).then_inc(pooled, 1)
                pool.memset(ic[:], 0.0).then_inc(pooled, 1)

    def nsa_attention(self):
        nc = self.nc
        units = [(g, b) for g in range(NG) for b in range(TB)]
        steps = [(u, r) for u in range(len(units)) for r in range(HPG)]
        with ExitStack() as st:
            sem, clear = self.stages.open("nsa", st)
            masked, s_ready, maxed, negd, expd, inverse, gated, p_ready, turned, t_taken, o_ready, o_hi, o_lo = (sem(x) for x in (
                "masked", "s_ready", "maxed", "negd", "expd", "inverse", "gated", "p_ready", "turned", "t_taken", "o_ready", "o_hi", "o_lo"))
            sb = lambda nm, s: st.enter_context(nc.sbuf_tensor(nm, s, F32))
            p, pt = sb("nsa_p", [P, 2, 2, S]), sb("nsa_pt", [P, 2, 2, S])
            mask = self.vc
            mx, neg, den, inv = (sb(f"nsa_{x}", [P, 2, 2]) for x in ("mx", "neg", "den", "inv"))
            o_parts = self.h
            block = st.enter_context(nc.Block())
            t_ps = lambda ty: self.ps[:, 4 + ty, :]

            @block.tensor
            def _(pe):
                def scores(n):
                    u, r = steps[n]
                    g, b = units[u]
                    h, W = HPG * g + r, (b + 1) * P
                    rows = slice(HD * (h % 2), HD * (h % 2) + HD)
                    if n >= 2:
                        pe.wait_ge(maxed, 2 * n - 2)
                    for ty, k0 in ((0, 10), (1, 12)):
                        mm = pe.matmul(self.ps[:, 2 * (n % 2) + ty, 0:W], self.rp[rows, h // 2, b * P:(b + 1) * P], self.rp[rows, k0 + g, 0:W],
                                       start=True, stop=True)
                    mm.then_inc(s_ready, 1)

                def turn(n):
                    u, r = steps[n]
                    g, b = units[u]
                    pe.wait_ge(p_ready, 2 * n + 2)
                    if n >= 1:
                        pe.wait_ge(t_taken, 2 * n)
                    for ty in range(2):
                        for j in range(b + 1):
                            mm = pe.transpose(t_ps(ty)[:, j * P:(j + 1) * P], p[:, n % 2, ty, j * P:(j + 1) * P], self.c("ident"))
                    mm.then_inc(turned, 1)

                def values(n):
                    u, r = steps[n]
                    g, b = units[u]
                    h = HPG * g + r
                    pe.wait_ge(t_taken, 2 * n + 2)
                    if u >= 2:
                        pe.wait_ge(o_lo, u - 1)
                    out = self.ps[HD * (h % 2):HD * (h % 2) + HD, 6 + u % 2, (r // 2) * P:(r // 2 + 1) * P]
                    pe.matmul(out, self.vcmp[:, h % 4, g, :], self.pct[:, h // 4, b * P:(b + 1) * P], start=True, stop=False)
                    for ty in range(2):
                        for j in range(b + 1):
                            mm = pe.matmul(out, self.vsvw[:, j, ty * NKV + g * HD:ty * NKV + (g + 1) * HD], pt[:, n % 2, ty, j * P:(j + 1) * P],
                                           start=False, stop=ty == 1 and j == b)
                    mm.then_inc(o_ready, 1)

                scores(0)
                for n in range(len(steps)):
                    if n + 1 < len(steps):
                        scores(n + 1)
                    if n >= 1:
                        values(n - 1)
                    turn(n)
                values(len(steps) - 1)

            @block.vector
            def _(dve):
                def softmax_max(n):
                    u, r = steps[n]
                    g, b = units[u]
                    W, i = (b + 1) * P, n % 2
                    causal = self.strip[:, S - W:S]
                    if r == 0:
                        view = lambda a: a.rearrange("p (j s) -> p j s", s=SEL)
                        if u >= 2:
                            dve.wait_ge(maxed, 2 * n - 2 * HPG)
                        dve.tensor_tensor(view(mask[:, u % 2, 0:W]), view(causal), self.selneg[:, u, 0:W // SEL].unsqueeze(2).to_broadcast([P, W // SEL, SEL]),
                                          ALU.add).then_inc(masked, 1)
                        dve.wait_ge(masked, u + 1)
                    dve.wait_ge(s_ready, n + 1)
                    if n >= 2:
                        dve.wait_ge(turned, n - 1)
                    for ty in range(2):
                        dve.tensor_tensor_reduce(p[:, i, ty, 0:W], self.ps[:, 2 * i + ty, 0:W], mask[:, u % 2, 0:W] if ty == 0 else causal, 1.0, -3e38,
                                                 ALU.add, ALU.max, mx[:, i, ty:ty + 1]).then_inc(maxed, 1)
                    dve.wait_ge(maxed, 2 * n + 2)
                    dve.tensor_scalar(neg[:, i], mx[:, i], -1.0, None, ALU.mult).then_inc(negd, 1)

                def normalise(n):
                    u, r = steps[n]
                    g, b = units[u]
                    W, i, h = (b + 1) * P, n % 2, HPG * g + r
                    dve.wait_ge(expd, 2 * n + 2)
                    dve.reciprocal(inv[:, i], den[:, i]).then_inc(inverse, 1)
                    dve.wait_ge(inverse, n + 1)
                    a = SSM_HEADS + 3 * h + 1
                    dve.tensor_tensor(inv[:, i], inv[:, i], self.dtgn[:, b, a:a + 2], ALU.mult).then_inc(gated, 1)
                    dve.wait_ge(gated, n + 1)
                    for ty in range(2):
                        dve.tensor_scalar(p[:, i, ty, 0:W], p[:, i, ty, 0:W], inv[:, i, ty:ty + 1], None, ALU.mult).then_inc(p_ready, 1)

                def evict(n):
                    u, r = steps[n]
                    W = (units[u][1] + 1) * P
                    dve.wait_ge(turned, n + 1)
                    if n >= 2:
                        dve.wait_ge(o_ready, n - 1)
                    dve.tensor_copy(pt[:, n % 2, 1, 0:W], t_ps(1)[:, 0:W]).then_inc(t_taken, 1)

                def out_low(u):
                    g, b = units[u]
                    dve.wait_ge(o_hi, u + 1)
                    dst = [part[:, 4 * g:4 * g + 4, b * P:(b + 1) * P] for part in o_parts]
                    dve.tensor_tensor(dst[1], self.ps[:, 6 + u % 2, :].rearrange("p (c t) -> p c t", c=4), dst[0].bitcast(F32), ALU.subtract).then_inc(o_lo, 1)

                softmax_max(0)
                for n in range(len(steps)):
                    if n + 1 < len(steps):
                        softmax_max(n + 1)
                    normalise(n)
                    evict(n)
                    if n >= HPG + 1 and n % HPG == 1:
                        out_low(n // HPG - 1)
                out_low(len(units) - 1)

            @block.scalar
            def _(act):
                def exps(n):
                    u, r = steps[n]
                    W, i = (units[u][1] + 1) * P, n % 2
                    act.wait_ge(negd, n + 1)
                    for ty in range(2):
                        act.activation(p[:, i, ty, 0:W], p[:, i, ty, 0:W], ACT.Exp, bias=neg[:, i, ty:ty + 1], accum_out=den[:, i, ty:ty + 1]).then_inc(expd, 1)

                def evict(n):
                    u, r = steps[n]
                    W = (units[u][1] + 1) * P
                    act.wait_ge(turned, n + 1)
                    if n >= 2:
                        act.wait_ge(o_ready, n - 1)
                    act.activation(pt[:, n % 2, 0, 0:W], t_ps(0)[:, 0:W], ACT.Copy).then_inc(t_taken, 1)

                def out_high(u):
                    g, b = units[u]
                    act.wait_ge(o_ready, HPG * (u + 1))
                    act.activation(o_parts[0][:, 4 * g:4 * g + 4, b * P:(b + 1) * P], self.ps[:, 6 + u % 2, :].rearrange("p (c t) -> p c t", c=4),
                                   ACT.Copy).then_inc(o_hi, 1)

                exps(0)
                for n in range(len(steps)):
                    if n + 1 < len(steps):
                        exps(n + 1)
                    evict(n)
                    if n >= HPG + 1 and n % HPG == 1:
                        out_high(n // HPG - 1)
                out_high(len(units) - 1)

            @block.gpsimd
            def _(pool):
                pool.sem_clear(clear)


class Whole(SsmTail):
    def nsa_out(self):
        nc, W, n = self.nc, self.W, COL // P
        tiles = 2 * (P_WO - P_NSAO)
        with ExitStack() as st:
            sem, clear = self.stages.open("nsa_out", st)
            gated, summed, rounded = sem("gated"), sem("summed"), sem("rounded")
            block = st.enter_context(nc.Block())

            @block.sync
            def _(sp):
                self.issue2(sp, P_NSAO, P_WO)

            @block.tensor
            def _(pe):
                for t in range(tiles):
                    tile_columns(pe, W, B2 + P_NSAO + t // 2, t % 2, self.pst, self.h)

            @block.scalar
            def _(act):
                for t in range(tiles):
                    W.split_hi(act, B2 + P_NSAO + t // 2 + 1, t % 2)
                    act.wait_ge(summed, t + 1)
                    act.activation(self.m[0][:, n * t:n * t + n, :], self.merged[:, n * t:n * t + n, :], ACT.Copy).then_inc(rounded, 1)

            @block.vector
            def _(dve):
                for t in range(tiles):
                    m, q = B2 + P_NSAO + t // 2, t % 2
                    part, gate = self.merged[:, n * t:n * t + n, :], self.gate[:, n * t:n * t + n, :]
                    W.done(dve, m, q)
                    dve.tensor_tensor(gate, gate, self.pst[:, q, 0:n, :], ALU.mult).then_inc(W.evicted[q], 1)
                    W.read(dve, m, q)
                    dve.tensor_tensor(part, part, gate, ALU.add).then_inc(summed, 1)
                    W.split_lo(dve, m + 1, q)
                    dve.wait_ge(rounded, t + 1)
                    dve.tensor_tensor(self.m[1][:, n * t:n * t + n, :], part, self.m[0][:, n * t:n * t + n, :].bitcast(F32), ALU.subtract)

            @block.gpsimd
            def _(pool):
                pool.sem_clear(clear)

    def route(self):
        nc, d = self.nc, self.d
        NR = MG + NE
        with ExitStack() as st:
            sem, clear = self.stages.open("route", st)
            landed, rounded, low, ready, steps, shifted, expd, chosen, counted, over_ready, over_sum, turned, kept_hi, kept_lo = (sem(x) for x in (
                "landed", "rounded", "low", "ready", "steps", "shifted", "expd", "chosen", "counted", "over_ready", "over_sum", "turned",
                "kept_hi", "kept_lo"))
            norm = Norm(self, "norm2_2", sem, st, lambda k: self.p2("g2", k, 1), shift=lambda k: self.p2("ada", 3 * KC + k, 1))
            sb = lambda nm, s, dt=F32: st.enter_context(nc.sbuf_tensor(nm, s, dt))
            raw, hi, lo = sb("route_w", [P, KC, NR]), sb("route_hi", [P, KC, NR], F32R), sb("route_lo", [P, KC, NR], F32R)
            lg = sb("route_logits", [P, TB, NR])
            eg, e8 = sb("route_eg", [P, TB, MG]), sb("route_e8", [P, TB, ME])
            a, b = sb("route_a", [P, TB]), sb("route_b", [P, TB])
            gt, eq = sb("route_gt", [P, TB, ME, ME]), sb("route_eq", [P, TB, ME, ME])
            one, two = sb("route_one", [P, TB, MG]), sb("route_two", [P, TB, ME])
            pick = sb("route_pick", [P, TB, MG, ME])
            mine, over = sb("route_mine", [P, TB, NE]), sb("route_over", [P, 1])
            block = st.enter_context(nc.Block())

            @block.sync
            def _(sp):
                for n, src, at in ((MG, "w_router_group_2", 0), (NE, "w_router_expert_2", MG)):
                    sp.dma_start(raw[:, :, at:at + n], d[src][0].rearrange("(k p) n -> p k n", p=P)).then_inc(landed, 16)

            @block.tensor
            def _(pe):
                norm.tensor(pe)
                for k in range(KC):
                    norm.chunk(pe, k)
                pe.wait_ge(low, 1)
                for t in range(TB):
                    for k in range(KC):
                        mm = products(pe, self.ps[:, t, 0:NR], (self.h[0][:, k, t * P:(t + 1) * P], self.h[1][:, k, t * P:(t + 1) * P]),
                                      (hi[:, k, :], lo[:, k, :]), k == 0, k == KC - 1)
                mm.then_inc(ready, 1)
                for k in range(KC):
                    if k >= 1:
                        pe.wait_ge(kept_hi, k)
                        pe.wait_ge(kept_lo, k)
                    for i in range(2):
                        for t in range(TB):
                            mm = pe.transpose(self.ps[:, 4 + i, t * P:(t + 1) * P], self.h[i][:, k, t * P:(t + 1) * P].bitcast(F32), self.c("ident"))
                    mm.then_inc(turned, 1)
                pe.wait_ge(chosen, 1)
                for t in range(TB):
                    for b in range(t + 1):
                        mm = pe.matmul(self.ps[:, 6, t * NE:(t + 1) * NE], self.c("prefix") if b == t else self.c("ones"), mine[:, b, :],
                                       start=b == 0, stop=b == t)
                mm.then_inc(counted, 1)
                pe.wait_ge(over_ready, 1)
                pe.matmul(self.ps[:, 7, 0:1], self.c("ones"), over[:], start=True, stop=True).then_inc(over_sum, 1)

            @block.scalar
            def _(act):
                norm.scalar(act)
                act.wait_ge(landed, 32)
                act.activation(hi[:], raw[:], ACT.Copy).then_inc(rounded, 1)
                for k in range(KC):
                    act.wait_ge(turned, k + 1)
                    act.activation(self.h_tok[0][:, :, k * P:(k + 1) * P], self.ps[:, 4, :].rearrange("p (t f) -> p t f", t=TB), ACT.Copy).then_inc(kept_hi, 1)
                for i, e in enumerate((eg, e8)):
                    act.wait_ge(shifted, i + 1)
                    act.activation(e[:], e[:], ACT.Exp).then_inc(expd, 1)

            @block.vector
            def _(dve):
                link = Link(dve, steps)
                norm.vector(dve)
                dve.wait_ge(rounded, 1)
                dve.tensor_tensor(lo[:], raw[:], hi[:].bitcast(F32), ALU.subtract).then_inc(low, 1)
                for k in range(KC):
                    dve.wait_ge(turned, k + 1)
                    dve.tensor_copy(self.h_tok[1][:, :, k * P:(k + 1) * P], self.ps[:, 5, :].rearrange("p (t f) -> p t f", t=TB)).then_inc(kept_lo, 1)
                dve.wait_ge(ready, 1)
                link(dve.tensor_tensor(lg[:], self.ps[:, 0:TB, 0:NR], self.p2("brout").unsqueeze(1).to_broadcast([P, TB, NR]), ALU.add))

                def rank(e, n, before, out, k):
                    shape = [P, TB, n, n]
                    others, own = e.unsqueeze(2).to_broadcast(shape), e.unsqueeze(3).to_broadcast(shape)
                    m = self.c(before).rearrange("p (j k) -> p j k", j=n).unsqueeze(1).to_broadcast(shape)
                    g_, q_ = gt[:, :, 0:n, 0:n], eq[:, :, 0:n, 0:n]
                    link(dve.tensor_tensor(g_, others, own, ALU.is_gt))
                    link(dve.tensor_tensor(q_, others, own, ALU.is_equal))
                    link(dve.tensor_tensor(q_, q_, m, ALU.mult))
                    link(dve.tensor_tensor(g_, g_, q_, ALU.add))
                    link(dve.tensor_reduce(out, g_, AX.X, ALU.add))
                    link(dve.tensor_scalar(out, out, float(k), None, ALU.is_lt))

                wide = lambda v, n: v.unsqueeze(2).to_broadcast([P, TB, n])
                link(dve.tensor_reduce(a[:], lg[:, :, 0:MG], AX.X, ALU.max))
                dve.tensor_tensor(eg[:], lg[:, :, 0:MG], wide(a[:], MG), ALU.subtract).then_inc(shifted, 1)
                dve.wait_ge(expd, 1)
                link(dve.tensor_reduce(a[:], eg[:], AX.X, ALU.add))
                rank(eg[:], MG, "before4", one[:], 1)
                experts = lg[:, :, MG:].rearrange("p t (g e) -> p t g e", g=MG)
                link(dve.tensor_tensor(pick[:], experts, one[:].unsqueeze(3).to_broadcast([P, TB, MG, ME]), ALU.mult))
                link(dve.tensor_reduce(e8[:], pick[:].rearrange("p t g e -> p t e g"), AX.X, ALU.add))
                link(dve.tensor_reduce(b[:], e8[:], AX.X, ALU.max))
                dve.tensor_tensor(e8[:], e8[:], wide(b[:], ME), ALU.subtract).then_inc(shifted, 1)
                dve.wait_ge(expd, 2)
                rank(e8[:], ME, "before", two[:], 2)
                link(dve.tensor_tensor(e8[:], e8[:], two[:], ALU.mult))
                link(dve.tensor_reduce(b[:], e8[:], AX.X, ALU.add))
                link(dve.tensor_tensor(b[:], b[:], a[:], ALU.mult))
                link(dve.reciprocal(b[:], b[:]))
                link(dve.tensor_tensor(e8[:], e8[:], wide(b[:], ME), ALU.mult))
                shape = [P, TB, MG, ME]
                for values, to in ((two, mine), (e8, self.comb)):
                    for t in range(TB):
                        e = dve.tensor_tensor(to[:, t].rearrange("p (g e) -> p g e", g=MG), values[:, t].unsqueeze(1).to_broadcast([P, MG, ME]),
                                              one[:, t].unsqueeze(2).to_broadcast([P, MG, ME]), ALU.mult)
                    e.then_inc(chosen, 1)
                dve.wait_ge(counted, 1)
                link(dve.scalar_tensor_tensor(self.rank[:], self.ps[:, 6, 0:TB * NE].rearrange("p (t e) -> p t e", t=TB), -1.0 - FAR, mine[:], ALU.add, ALU.mult))
                link(dve.tensor_scalar(self.rank[:], self.rank[:], FAR, None, ALU.add))
                link(dve.tensor_scalar(self.over[:], self.rank[:], float(SLOTS), None, ALU.is_ge))
                link(dve.tensor_tensor(mine[:], mine[:], self.over[:], ALU.mult))
                dve.tensor_reduce(over[:], mine[:], AX.XY, ALU.add).then_inc(over_ready, 1)
                dve.wait_ge(chosen, 2)
                dve.tensor_tensor(self.over[:], self.over[:], self.comb[:], ALU.mult)
                dve.wait_ge(over_sum, 1)
                dve.tensor_scalar(self.passes[:], self.ps[:, 7, 0:1], 1.0, None, ALU.min)

            @block.gpsimd
            def _(pool):
                pool.sem_clear(clear)

    def moe(self):
        nc, W = self.nc, self.W
        J, B = NE // BATCH_E, BATCH_E
        m0 = B2 + P_MOE
        with ExitStack() as st:
            sem, clear = self.stages.open("moe", st)
            (sel_ready, slot_w, wsl_ready, gathered, x_hi, x_lo, u_turned, u_hi, u_lo, g_turned, g_ready, scattered, x_added, y_hi) = (sem(x) for x in (
                "sel_ready", "slot_w", "wsl_ready", "gathered", "x_hi", "x_lo", "u_turned", "u_hi", "u_lo", "g_turned", "g_ready",
                "scattered", "x_added", "y_hi"))
            sb = lambda nm, s, dt=F32: st.enter_context(nc.sbuf_tensor(nm, s, dt))
            sel = sb("select", [P, TB, B, SLOTS], F32R)
            back = sb("select_t", [P, B, S], F32R)
            wsl = sb("slot_weight", [P, B])
            g, uw = sb("moe_silu", [P, 2, EH]), sb("moe_weighted", [P, 2, EH])
            uT = sb("moe_u_hi", [P, B, 2, SLOTS], F32R), sb("moe_u_lo", [P, B, 2, SLOTS], F32R)
            y = sb("moe_y_hi", [P, B, D], F32R), sb("moe_y_lo", [P, B, D], F32R)
            xg = self.h
            block = st.enter_context(nc.Block())
            u_bank = lambda e: self.ps[:, 1 + 4 * (e % 2), 0:EH]
            spare = (2, 3, 6, 7)
            pair = lambda j, e: m0 + MOE_PER * j + e
            down = lambda j, e: (m0 + MOE_PER * j + B + e // 2, e % 2)

            @block.sync
            def _(sp):
                def rest(j):
                    for e in range(2, B):
                        for q in range(2):
                            W.issue(sp, pair(j, e), q, self.expert_tile(j, e, q))
                    for e in range(B):
                        W.issue(sp, *down(j, e), self.expert_down_tile(j, e))

                with sp.Fori(0, J - 1) as j:
                    rest(j)
                    for e in range(2):
                        for q in range(2):
                            W.issue(sp, pair(j + 1, e), q, self.expert_tile(j + 1, e, q))
                rest(J - 1)

            @block.tensor
            def _(pe):
                def weigh(j):
                    pe.wait_ge(sel_ready, j + 1)
                    for e in range(B):
                        for b in range(TB):
                            mm = pe.matmul(self.ps[:, 6, e:e + 1], sel[:, b, e].bitcast(F32), self.comb[:, b, bass.ds(B * j + e, 1)],
                                           start=b == 0, stop=b == TB - 1)
                    mm.then_inc(slot_w, 1)

                def gather(j, k, first):
                    if k == 1:
                        pe.wait_ge(wsl_ready, j + 1)
                    if not first or k >= 2:
                        n = KC * j + k - 1
                        pe.wait_ge(x_hi, n)
                        pe.wait_ge(x_lo, n)
                    for i in range(2):
                        for b in range(TB):
                            mm = pe.matmul(self.ps[:, spare[2 * (k % 2) + i], :], self.h_tok[i][:, b, k * P:(k + 1) * P],
                                           sel[:, b].rearrange("p e s -> p (e s)"), start=b == 0, stop=b == TB - 1)
                    mm.then_inc(gathered, 1)

                def scatter(j, k):
                    if k == 0:
                        pe.wait_ge(g_ready, B * (j + 1))
                        for q in range(2):
                            W.read(pe, down(j, B - 2 + q)[0], q)
                    if k >= 4:
                        pe.wait_ge(x_added, KC * j + k - 3)
                    for e in range(B):
                        for i in range(2):
                            mm = pe.matmul(self.ps[:, spare[k % 4], :], y[i][:, e, k * P:(k + 1) * P], back[:, e, :],
                                           start=e == 0 and i == 0, stop=e == B - 1 and i == 1)
                    mm.then_inc(scattered, 1)

                def turn(j, e):
                    W.read(pe, pair(j, e), 1)
                    if e >= 2:
                        pe.wait_ge(u_lo, B * j + e - 1)
                    for c in range(2):
                        mm = pe.transpose(u_bank(e)[:, c * P:(c + 1) * P], uw[:, e % 2, c * P:(c + 1) * P], self.c("ident"))
                    mm.then_inc(u_turned, 1)

                def batch(j, first, last):
                    pe.wait_ge(x_hi, KC * (j + 1))
                    pe.wait_ge(x_lo, KC * (j + 1))
                    for e in range(B):
                        for q in range(2):
                            W.ready(pe, pair(j, e), q)
                            for k in range(KC):
                                mm = products(pe, self.ps[:, 4 * q, 0:EH], (xg[0][:, k, e * SLOTS:(e + 1) * SLOTS], xg[1][:, k, e * SLOTS:(e + 1) * SLOTS]),
                                              (W.hi[:, q, k, :], W.lo[:, q, k, :]), k == 0, k == KC - 1)
                            mm.then_inc(W.tile_done, 1)
                            if not first:
                                scatter(j - 1, 2 * e + q)
                        if e >= 1:
                            turn(j, e - 1)
                    if not first:
                        pe.wait_ge(x_added, KC * j)
                    for e in range(B):
                        for b in range(TB):
                            mm = pe.transpose(self.ps[:, spare[e], b * P:(b + 1) * P], sel[:, b, e].bitcast(F32), self.c("ident"))
                        mm.then_inc(g_turned, 1)
                    turn(j, B - 1)
                    if not last:
                        pe.wait_ge(g_ready, B * (j + 1))
                        weigh(j + 1)
                    for e in range(B):
                        if not last:
                            for k in (2 * e, 2 * e + 1):
                                gather(j + 1, k, False)
                        m, q = down(j, e)
                        if e == 0:
                            pe.wait_ge(u_lo, B * (j + 1))
                        W.ready(pe, m, q)
                        for c in range(2):
                            for k in range(2):
                                cols = slice(c * 512, (c + 1) * 512)
                                flat = lambda w: w[:, q].rearrange("p k n -> p (k n)")[:, k * D:(k + 1) * D][:, cols]
                                mm = products(pe, self.pst[:, q, c], (uT[0][:, e, k, :], uT[1][:, e, k, :]), (flat(W.hi), flat(W.lo)), k == 0, k == 1)
                        mm.then_inc(W.tile_done, 1)

                weigh(0)
                for k in range(KC):
                    gather(0, k, True)
                batch(0, True, False)
                with pe.Fori(1, J - 1) as j:
                    batch(j, False, False)
                batch(J - 1, False, True)
                for k in range(KC):
                    scatter(J - 1, k)

            @block.scalar
            def _(act):
                def gather(j, k):
                    act.wait_ge(gathered, KC * j + k + 1)
                    act.activation(xg[0][:, k, :], self.ps[:, spare[2 * (k % 2)], :], ACT.Copy).then_inc(x_hi, 1)

                def turn(j, e):
                    act.wait_ge(u_turned, B * j + e + 1)
                    act.activation(uT[0][:, e], u_bank(e).rearrange("p (c s) -> p c s", c=2), ACT.Copy).then_inc(u_hi, 1)

                def batch(j, first, last):
                    for e in range(B):
                        m = pair(j, e)
                        W.done(act, m, 0)
                        if e >= 2:
                            W.read(act, m - 2, 1)
                        act.activation(g[:, e % 2], self.ps[:, 0, 0:EH], ACT.Silu).then_inc(W.evicted[0], 1)
                        for q in range(2):
                            W.split_hi(act, m + 1, q)
                        if e >= 1:
                            turn(j, e - 1)
                    for e in range(B):
                        act.wait_ge(g_turned, B * j + e + 1)
                        act.activation(back[:, e, :], self.ps[:, spare[e], :], ACT.Copy).then_inc(g_ready, 1)
                    turn(j, B - 1)
                    for e in range(B):
                        if not last:
                            for k in (2 * e, 2 * e + 1):
                                gather(j + 1, k)
                        m, q = down(j, e)
                        W.done(act, m, q)
                        if e == 0 and not first:
                            act.wait_ge(scattered, KC * j)
                        act.activation(y[0][:, e], self.pst[:, q, 0:2].rearrange("p c n -> p (c n)"), ACT.Copy).then_inc(y_hi, 1)
                        if not (last and e >= 2):
                            W.split_hi(act, m + 1, q)

                for k in range(KC):
                    gather(0, k)
                batch(0, True, False)
                with act.Fori(1, J - 1) as j:
                    batch(j, False, False)
                batch(J - 1, False, True)

            @block.vector
            def _(dve):
                def select(j, first):
                    if not first:
                        dve.wait_ge(g_turned, B * j)
                    for e in range(B):
                        rank = self.rank[:, :, bass.ds(B * j + e, 1)].to_broadcast([P, TB, SLOTS])
                        s = dve.tensor_tensor(sel[:, :, e, :], self.c("slot").unsqueeze(1).to_broadcast([P, TB, SLOTS]), rank, ALU.is_equal)
                    s.then_inc(sel_ready, 1)

                def weights(j):
                    dve.wait_ge(slot_w, j + 1)
                    dve.tensor_copy(wsl[:], self.ps[:, 6, 0:B]).then_inc(wsl_ready, 1)

                def gather(j, k):
                    dve.wait_ge(gathered, KC * j + k + 1)
                    dve.tensor_copy(xg[1][:, k, :], self.ps[:, spare[2 * (k % 2) + 1], :]).then_inc(x_lo, 1)

                def add(j, k):
                    dve.wait_ge(scattered, KC * j + k + 1)
                    dve.scalar_tensor_tensor(self.x[:, k, :], self.ps[:, spare[k % 4], :], self.p2("ada", 5 * KC + k, 1), self.x[:, k, :],
                                             ALU.mult, ALU.add).then_inc(x_added, 1)

                def turn(j, e):
                    dve.wait_ge(u_hi, B * j + e + 1)
                    dve.tensor_tensor(uT[1][:, e], u_bank(e).rearrange("p (c s) -> p c s", c=2), uT[0][:, e].bitcast(F32), ALU.subtract).then_inc(u_lo, 1)

                def batch(j, first, last):
                    dve.wait_ge(wsl_ready, j + 1)
                    for e in range(B):
                        m = pair(j, e)
                        W.split_lo(dve, m + 1, 0)
                        W.read(dve, m, 0)
                        W.done(dve, m, 1)
                        if e >= 2:
                            dve.wait_ge(u_turned, B * j + e - 1)
                        dve.scalar_tensor_tensor(uw[:, e % 2], self.ps[:, 4, 0:EH], wsl[:, e:e + 1], g[:, e % 2], ALU.mult, ALU.mult).then_inc(W.evicted[1], 1)
                        W.split_lo(dve, m + 1, 1)
                        if not first:
                            for k in (2 * e, 2 * e + 1):
                                add(j - 1, k)
                        if e >= 1:
                            turn(j, e - 1)
                    if not last:
                        select(j + 1, False)
                    turn(j, B - 1)
                    if not last:
                        weights(j + 1)
                    for e in range(B):
                        if not last:
                            for k in (2 * e, 2 * e + 1):
                                gather(j + 1, k)
                        m, q = down(j, e)
                        dve.wait_ge(y_hi, B * j + e + 1)
                        dve.tensor_tensor(y[1][:, e], self.pst[:, q, 0:2].rearrange("p c n -> p (c n)"), y[0][:, e].bitcast(F32), ALU.subtract).then_inc(W.evicted[q], 1)
                        if not (last and e >= 2):
                            W.split_lo(dve, m + 1, q)

                select(0, True)
                weights(0)
                for k in range(KC):
                    gather(0, k)
                batch(0, True, False)
                with dve.Fori(1, J - 1) as j:
                    batch(j, False, False)
                batch(J - 1, False, True)
                for k in range(KC):
                    add(J - 1, k)

            @block.gpsimd
            def _(pool):
                pool.sem_clear(clear)

    def restore_h(self):
        with ExitStack() as st:
            sem, clear = self.stages.open("restore_h", st)
            turned, back_hi, back_lo = sem("turned"), sem("back_hi"), sem("back_lo")
            block = st.enter_context(self.nc.Block())

            @block.sync
            def _(sp):
                for q in range(2):
                    self.W.issue(sp, B2 + P_END, q, self.expert_tile(0, 0, q), first=True)

            @block.tensor
            def _(pe):
                for k in range(KC):
                    if k >= 1:
                        pe.wait_ge(back_hi, k)
                        pe.wait_ge(back_lo, k)
                    for i in range(2):
                        for t in range(TB):
                            mm = pe.transpose(self.ps[:, i, t * P:(t + 1) * P], self.h_tok[i][:, t, k * P:(k + 1) * P].bitcast(F32), self.c("ident"))
                    mm.then_inc(turned, 1)

            @block.scalar
            def _(act):
                for k in range(KC):
                    act.wait_ge(turned, k + 1)
                    act.activation(self.h[0][:, k, :], self.ps[:, 0, :], ACT.Copy).then_inc(back_hi, 1)

            @block.vector
            def _(dve):
                for k in range(KC):
                    dve.wait_ge(turned, k + 1)
                    dve.tensor_copy(self.h[1][:, k, :], self.ps[:, 1, :]).then_inc(back_lo, 1)

            @block.gpsimd
            def _(pool):
                pool.sem_clear(clear)

    def moe_rest(self):
        nc, W, n = self.nc, self.W, COL // P
        J = NE // BATCH_E
        m0 = B2 + P_END
        with ExitStack() as st:
            sem, clear = self.stages.open("moe_rest", st)
            silud, spread, weights, weighted, rounded, low = (sem(x) for x in ("silud", "spread", "weights", "weighted", "rounded", "low"))
            sb = lambda nm, s: st.enter_context(nc.sbuf_tensor(nm, s, F32))
            g, y, dg = sb("rest_silu", [P, 2, n, S]), sb("rest_y", [P, 2, n, S]), sb("rest_diag", [P, 2, TB, P])
            u = self.parts(st, "rest_u", KC)
            block = st.enter_context(nc.Block())
            bank = lambda e: self.ps[:, 2 + e % 2, :]

            @block.sync
            def _(sp):
                for q in range(2):
                    W.issue(sp, m0 + 1, q, self.expert_tile(0, 1, q))

                def rest(j):
                    for e in range(2, BATCH_E):
                        for q in range(2):
                            W.issue(sp, m0 + MOE_PER * j + e, q, self.expert_tile(j, e, q))
                    for t in range(4):
                        W.issue(sp, m0 + MOE_PER * j + BATCH_E + t // 2, t % 2, self.expert_rows_tile(j, t))

                with sp.Fori(0, J - 1) as j:
                    rest(j)
                    for e in range(2):
                        for q in range(2):
                            W.issue(sp, m0 + MOE_PER * (j + 1) + e, q, self.expert_tile(j + 1, e, q))
                rest(J - 1)

            @block.tensor
            def _(pe):
                with pe.Fori(0, J) as j:
                    for e in range(BATCH_E):
                        pe.wait_ge(spread, BATCH_E * j + e + 1)
                        if e >= 2:
                            pe.wait_ge(weighted, BATCH_E * j + e - 1)
                        pe.matmul(bank(e), self.c("ones"), dg[:, e % 2].rearrange("p b t -> p (b t)"), start=True, stop=True).then_inc(weights, 1)
                        for q in range(2):
                            tile_columns(pe, W, m0 + MOE_PER * j + e, q, self.pst, self.h)
                    pe.wait_ge(low, BATCH_E * (j + 1))
                    for t in range(4):
                        tile_columns(pe, W, m0 + MOE_PER * j + BATCH_E + t // 2, t % 2, self.pst, u)

            def scalar_batch(act, j, last):
                for e in range(BATCH_E):
                    m = m0 + MOE_PER * j + e
                    W.done(act, m, 0)
                    if e >= 2:
                        W.read(act, m - 2, 1)
                    act.activation(g[:, e % 2], self.pst[:, 0, 0:n, :], ACT.Silu).then_inc(W.evicted[0], 1)
                    for q in range(2):
                        W.split_hi(act, m + 1, q)
                    act.wait_ge(weighted, BATCH_E * j + e + 1)
                    act.activation(u[0][:, n * e:n * e + n, :], y[:, e % 2], ACT.Copy).then_inc(rounded, 1)
                for t in range(4):
                    if not (last and t >= 2):
                        W.split_hi(act, m0 + MOE_PER * j + BATCH_E + t // 2 + 1, t % 2)

            @block.scalar
            def _(act):
                for q in range(2):
                    W.split_hi(act, m0, q, first=True)
                with act.Fori(0, J - 1) as j:
                    scalar_batch(act, j, False)
                scalar_batch(act, J - 1, True)

            def vector_batch(dve, j, last):
                def diagonal(e):
                    col = self.over[:, :, bass.ds(BATCH_E * j + e, 1)].to_broadcast([P, TB, P])
                    dve.tensor_tensor(dg[:, e % 2], self.c("ident").unsqueeze(1).to_broadcast([P, TB, P]), col, ALU.mult).then_inc(spread, 1)

                diagonal(0)
                for e in range(BATCH_E):
                    m = m0 + MOE_PER * j + e
                    if e + 1 < BATCH_E:
                        if e >= 1:
                            dve.wait_ge(weights, BATCH_E * j + e)
                        diagonal(e + 1)
                    W.read(dve, m, 0)
                    W.done(dve, m, 1)
                    dve.tensor_tensor(y[:, e % 2], g[:, e % 2], self.pst[:, 1, 0:n, :], ALU.mult).then_inc(W.evicted[1], 1)
                    W.split_lo(dve, m + 1, 0)
                    W.read(dve, m, 1)
                    dve.wait_ge(weights, BATCH_E * j + e + 1)
                    dve.tensor_tensor(y[:, e % 2], y[:, e % 2], bank(e).unsqueeze(1).to_broadcast([P, n, S]), ALU.mult).then_inc(weighted, 1)
                    W.split_lo(dve, m + 1, 1)
                    dve.wait_ge(rounded, BATCH_E * j + e + 1)
                    dve.tensor_tensor(u[1][:, n * e:n * e + n, :], y[:, e % 2], u[0][:, n * e:n * e + n, :].bitcast(F32), ALU.subtract).then_inc(low, 1)
                for t in range(4):
                    m = m0 + MOE_PER * j + BATCH_E + t // 2
                    W.done(dve, m, t % 2)
                    for c in range(n):
                        k = n * t + c
                        e = dve.scalar_tensor_tensor(self.x[:, k, :], self.pst[:, t % 2, c], self.p2("ada", 5 * KC + k, 1), self.x[:, k, :], ALU.mult, ALU.add)
                    e.then_inc(W.evicted[t % 2], 1)
                    if not (last and t >= 2):
                        W.split_lo(dve, m + 1, t % 2)

            @block.vector
            def _(dve):
                for q in range(2):
                    W.split_lo(dve, m0, q)
                with dve.Fori(0, J - 1) as j:
                    vector_batch(dve, j, False)
                vector_batch(dve, J - 1, True)

            @block.gpsimd
            def _(pool):
                pool.sem_clear(clear)

    def finish(self):
        nc = self.nc
        with ExitStack() as st:
            sem, clear = self.stages.open("finish", st)
            squared, used, mean, root, inverse, normed, turned, taken, copied = (sem(x) for x in (
                "squared", "used", "mean", "root", "inverse", "normed", "turned", "taken", "copied"))
            sb = lambda nm, s: st.enter_context(nc.sbuf_tensor(nm, s, F32))
            sq, rs, y = sb("fin_sq", [P, 2, S]), sb("fin_rs", [P, S]), sb("fin_tokens", [P, TB, D])
            block = st.enter_context(nc.Block())

            @block.scalar
            def _(act):
                for k in range(KC):
                    if k >= 2:
                        act.wait_ge(used, k - 1)
                    act.activation(sq[:, k % 2], self.x[:, k, :], ACT.Square).then_inc(squared, 1)
                act.wait_ge(mean, 1)
                act.activation(rs[:], rs[:], ACT.Sqrt).then_inc(root, 1)
                for k in range(0, KC, 2):
                    act.wait_ge(turned, k + 1)
                    act.activation(y[:, :, k * P:(k + 1) * P], self.ps[:, 1 + k % 4, :].rearrange("p (b f) -> p b f", b=TB), ACT.Copy).then_inc(taken, 1)

            @block.tensor
            def _(pe):
                for k in range(KC):
                    pe.wait_ge(squared, k + 1)
                    pe.matmul(self.ps[:, 0, :], self.c("ones"), sq[:, k % 2], start=k == 0, stop=k == KC - 1).then_inc(used, 1)
                for k in range(KC):
                    pe.wait_ge(normed, k + 1)
                    if k >= 4:
                        pe.wait_ge(taken if k % 2 == 0 else copied, (k - 4) // 2 + 1)
                    for b in range(TB):
                        t = pe.transpose(self.ps[:, 1 + k % 4, b * P:(b + 1) * P], self.x[:, k, b * P:(b + 1) * P], self.c("ident"))
                    t.then_inc(turned, 1)

            @block.vector
            def _(dve):
                dve.wait_ge(used, KC)
                dve.tensor_scalar(rs[:], self.ps[:, 0, :], 1.0 / D, EPS, ALU.mult, ALU.add).then_inc(mean, 1)
                dve.wait_ge(root, 1)
                dve.reciprocal(rs[:], rs[:]).then_inc(inverse, 1)
                dve.wait_ge(inverse, 1)
                for k in range(KC):
                    dve.scalar_tensor_tensor(self.x[:, k, :], self.x[:, k, :], self.p2("fin", k, 1), rs[:], ALU.mult, ALU.mult).then_inc(normed, 1)
                for k in range(1, KC, 2):
                    dve.wait_ge(turned, k + 1)
                    dve.tensor_copy(y[:, :, k * P:(k + 1) * P], self.ps[:, 1 + k % 4, :].rearrange("p (b f) -> p b f", b=TB)).then_inc(copied, 1)

            out_done = sem("out_done")

            @block.sync
            def _(sp):
                sp.wait_ge(taken, KC // 2)
                sp.wait_ge(copied, KC // 2)
                sp.dma_start(self.out.rearrange("o (b p) d -> p (o b) d", p=P), y[:]).then_inc(out_done, 16)
                sp.wait_ge(out_done, 16)

            @block.gpsimd
            def _(pool):
                pool.sem_clear(clear)

    def __init__(self, *args):
        super().__init__(*args)
        self.par2 = self.sb("par2", [P, PAR2_N])
        self.silu_c = self.sb("silu_c", [P, KC])
        self.ada_sum = self.sb("ada_sum", [P, 6 * KC])

    def second(self):
        nc, W, ctx = self.nc, self.W, self.ctx
        sbuf = lambda st, n, s, **kw: st.enter_context(nc.sbuf_tensor(n, s, F32, **kw))
        with ExitStack() as until_wo:
            self.dtgn = sbuf(until_wo, "dt_gates", [P, TB, SSM_HEADS + 3 * NH])
            self.vsvw = sbuf(until_wo, "v_tokens", [P, TB, 2 * NKV])
            self.trig = sbuf(until_wo, "trig", [P, 2, S], side="right")
            def prologue(sp):
                for m in range(2):
                    for q in range(2):
                        W.issue(sp, B2 + m, q, self.tile2(m, q), first=m == 0)

            with ExitStack() as until_ssm:
                self.xs = sbuf(until_ssm, "xs", [P, 16, S])
                with ExitStack() as until_scan:
                    self.bc = sbuf(until_scan, "bc", [P, 8, S])
                    self.ssm_project(prologue)
                    self.ssd()
                self.merged = sbuf(until_wo, "merged2", [P, KC, S], side="right")
                self.ssm_gate()
                self.yn = self.parts(until_ssm, "yn", KC)
                self.ssm_norm()
                self.ssm_out()
            self.gate = sbuf(until_wo, "nsa_gate", [P, KC, S])
            with ExitStack() as until_attention:
                self.rp = sbuf(until_attention, "nsa_q_k", [P, 14, S])
                self.vc = sbuf(until_attention, "vc", [P, NG, S])
                self.nsa_project()
                self.nsa_rope()
                self.kcmp = sbuf(until_attention, "kcmp", [P, NG * NC])
                self.vcmp = sbuf(until_attention, "vcmp", [P, 4, NG, HD])
                self.strip = sbuf(until_attention, "causal_strip", [P, S])
                self.nsa_compress()
                self.pct = sbuf(until_attention, "cmp_probs", [P, 4, S])
                self.selneg = sbuf(until_attention, "selection", [P, NG * TB, NSEL])
                self.nsa_compressed()
                self.nsa_attention()
            self.m = self.parts(until_wo, "merged_two", KC)
            self.nsa_out()
            self.add_projection("w_o", B2 + P_WO, self.m, lambda sp: self.issue2(sp, P_WO, P_MOE), scale=lambda k: self.p2("ada", 2 * KC + k, 1))
        self.passes = ctx.enter_context(nc.sbuf_tensor("passes", [P, 1], I32))
        with ExitStack() as until_moe:
            self.comb, self.rank, self.over = (sbuf(until_moe, n, [P, TB, NE]) for n in ("expert_weights", "slot_rank", "weights_over"))
            self.h_tok = tuple(until_moe.enter_context(nc.sbuf_tensor(f"h_tokens_{i}", [P, TB, D], F32R)) for i in ("hi", "lo"))
            self.route()
            self.moe()
            pool = self.stages.last
            with nc.If(nc.values_load(self.passes[0:1, 0:1], min_val=0, max_val=1) > 0):
                self.restore_h()
                self.moe_rest()
            self.stages.last = pool
        self.finish()


def program(nc, dram, out, const_at):
    with ExitStack() as ctx:
        k = Whole(nc, dram, out, const_at, ctx)
        k.load()
        with nc.Fori(0, DEPTH) as l:
            k.layer(l)
        k.until_first.close()
        k.second()


def kernel(**inputs):
    import concourse.bacc as bacc
    from concourse.bass_utils import run_bass_kernel_spmd

    nc = bacc.Bacc("TRN2", target_bir_lowering=False, num_devices=1)
    table, at = constants()
    arrays, dram = {}, {}
    for name, a in [*inputs.items(), ("const", table)]:
        a = np.ascontiguousarray(a)
        arrays[f"in_{name}"] = a
        dram[name] = nc.dram_tensor(f"in_{name}", a.shape, mybir.dt.from_np(a.dtype), kind="ExternalInput").ap()
    out = nc.dram_tensor("out_0", (1, S, D), F32, kind="ExternalOutput").ap()
    program(nc, dram, out, at)
    r = run_bass_kernel_spmd(nc, [arrays], core_ids=[0])
    return r.results[0]["out_0"]
```
